# Optimizing a Trainium2 kernel written in Bass

```python
import math
import jax, jax.numpy as jnp
from jax import lax
import numpy as np

D_MODEL = 1024
BATCH = 1
SEQ = 128
DEPTH = 2
DEC_BATCH = 1
DEC_SEQ = 512
PAST_LEN = 256

GRID_W = 64
D_MIX = D_MODEL
N_DIFF_HEADS = 4
DIFF_HEAD_DIM = 64
DIFF_V_DIM = 2 * DIFF_HEAD_DIM
D_DIFF_QK = N_DIFF_HEADS * 2 * DIFF_HEAD_DIM
D_DIFF = N_DIFF_HEADS * DIFF_V_DIM
N_MLA_HEADS = 4
MLA_NOPE_DIM = 64
MLA_ROPE_DIM = 32
MLA_V_DIM = 128
Q_LORA = 256
KV_LORA = 128
D_MLA = N_MLA_HEADS * MLA_V_DIM
D_IN_PROJ = 2 * D_DIFF_QK + D_DIFF + Q_LORA + KV_LORA + MLA_ROPE_DIM
D_FF = 2816
N_EXPERTS = 8
TOP_K = 2
D_FF_EXPERT = 1408
N_DENSE = (DEPTH + 1) // 2
N_MOE = DEPTH // 2
ROPE_THETA = 10000.0
RMS_EPS = 1e-6
Q_BLOCK = 128

kernel_name = "hymba_diffmla_diffusion_step"

def _rmsnorm(x, g):
    x32 = x.astype(jnp.float32)
    y = x32 * lax.rsqrt(jnp.mean(x32 * x32, axis=-1, keepdims=True) + RMS_EPS)
    return (y * g.astype(jnp.float32)).astype(x.dtype)

def _rope_1d(x, pos):
    half = x.shape[-1] // 2
    freqs = ROPE_THETA ** (-jnp.arange(half, dtype=jnp.float32) / half)
    ang = pos.astype(jnp.float32)[:, None] * freqs[None, :]
    cos = jnp.cos(ang)[None, :, None, :]
    sin = jnp.sin(ang)[None, :, None, :]
    x1, x2 = x[..., :half], x[..., half:]
    return jnp.concatenate([x1 * cos - x2 * sin, x1 * sin + x2 * cos], axis=-1).astype(x.dtype)

def _axial_rope(x, rows, cols):
    r = x.shape[-1] // 2
    return jnp.concatenate([_rope_1d(x[..., :r], rows), _rope_1d(x[..., r:], cols)], axis=-1)

def _sweep_query_blocks(fn, qs):
    B, Tq = qs[0].shape[:2]
    blk = min(Q_BLOCK, Tq)
    nb = Tq // blk
    qb = tuple(jnp.moveaxis(q.reshape(B, nb, blk, *q.shape[2:]), 1, 0) for q in qs)
    out = lax.map(lambda a: fn(*a), qb)
    return jnp.moveaxis(out, 0, 1).reshape(B, Tq, *out.shape[3:])

def _swiglu(x, wg, wu, wd):
    return (jax.nn.silu(x @ wg) * (x @ wu)) @ wd

def _moe(h, m, P):
    B, T, D = h.shape
    xf = h.reshape(B * T, D)
    logits = jnp.einsum('nd,de->ne', xf, P['router'][m], preferred_element_type=jnp.float32)
    probs = jax.nn.softmax(logits, axis=-1)
    top_p, top_i = lax.top_k(probs, TOP_K)
    top_p = top_p / jnp.sum(top_p, axis=-1, keepdims=True)
    gates = jnp.sum(jax.nn.one_hot(top_i, N_EXPERTS, dtype=jnp.float32) * top_p[..., None], axis=1)
    y = jnp.zeros_like(xf)
    for e in range(N_EXPERTS):
        y = y + gates[:, e:e + 1].astype(xf.dtype) * _swiglu(
            xf, P['moe_w_gate'][m, e], P['moe_w_up'][m, e], P['moe_w_down'][m, e])
    return y.reshape(B, T, D)

def _mixer(h, l, P, pos, ctx):
    B, T, _ = h.shape
    z = h @ P['w_in'][l]
    o1 = D_DIFF_QK
    o2 = o1 + D_DIFF_QK
    o3 = o2 + D_DIFF
    o4 = o3 + Q_LORA
    o5 = o4 + KV_LORA
    qd, kd, vd, cq, ckv, kr = jnp.split(z, [o1, o2, o3, o4, o5], axis=-1)
    qd = qd.reshape(B, T, 2 * N_DIFF_HEADS, DIFF_HEAD_DIM)
    kd = kd.reshape(B, T, 2 * N_DIFF_HEADS, DIFF_HEAD_DIM)
    vd = vd.reshape(B, T, N_DIFF_HEADS, DIFF_V_DIM)
    q_mla = (_rmsnorm(cq, P['mla_q_norm_g'][l]) @ P['w_uq'][l]).reshape(
        B, T, N_MLA_HEADS, MLA_NOPE_DIM + MLA_ROPE_DIM)
    qn, qr = q_mla[..., :MLA_NOPE_DIM], q_mla[..., MLA_NOPE_DIM:]
    ckv = _rmsnorm(ckv, P['mla_kv_norm_g'][l])
    kr = kr[:, :, None, :]
    if pos is not None:
        rows, cols = pos
        qd = _axial_rope(qd, rows, cols)
        kd = _axial_rope(kd, rows, cols)
        qr = _axial_rope(qr, rows, cols)
        kr = _axial_rope(kr, rows, cols)
    kd = kd.reshape(B, T, N_DIFF_HEADS, 2 * DIFF_HEAD_DIM)
    kr = kr[:, :, 0, :]
    own = (kd, vd, ckv, kr)
    if ctx is None:
        k_all, v_all, ckv_all, kr_all = own
    else:
        k_all, v_all, ckv_all, kr_all = (jnp.concatenate([ctx[0], kd], axis=1),
                                         jnp.concatenate([ctx[1], vd], axis=1),
                                         jnp.concatenate([ctx[2], ckv], axis=1),
                                         jnp.concatenate([ctx[3], kr], axis=1))
    Tk = k_all.shape[1]

    k5 = k_all.reshape(B, Tk, N_DIFF_HEADS, 2, DIFF_HEAD_DIM)
    k1, k2 = k5[..., 0, :], k5[..., 1, :]
    q5 = qd.reshape(B, T, N_DIFF_HEADS, 2, DIFF_HEAD_DIM)
    q1, q2 = q5[..., 0, :], q5[..., 1, :]
    lam_init = 0.8 - 0.6 * math.exp(-0.3 * l)
    f32 = jnp.float32
    lam = (jnp.exp(jnp.sum(P['diff_lq1'][l].astype(f32) * P['diff_lk1'][l].astype(f32)))
           - jnp.exp(jnp.sum(P['diff_lq2'][l].astype(f32) * P['diff_lk2'][l].astype(f32)))
           + lam_init)
    d_scale = DIFF_HEAD_DIM ** -0.5

    def diff_block(q1b, q2b):
        s1 = jnp.einsum('bqhd,bkhd->bhqk', q1b, k1, preferred_element_type=f32) * d_scale
        s2 = jnp.einsum('bqhd,bkhd->bhqk', q2b, k2, preferred_element_type=f32) * d_scale
        p = jax.nn.softmax(s1, axis=-1) - lam * jax.nn.softmax(s2, axis=-1)
        return jnp.einsum('bhqk,bkhe->bqhe', p.astype(v_all.dtype), v_all)

    diff_out = _sweep_query_blocks(diff_block, (q1, q2))
    diff_out = _rmsnorm(diff_out, P['diff_subln_g'][l]) * (1.0 - lam_init)

    k_nope = (ckv_all @ P['w_uk'][l]).reshape(B, Tk, N_MLA_HEADS, MLA_NOPE_DIM)
    v_mla = (ckv_all @ P['w_uv'][l]).reshape(B, Tk, N_MLA_HEADS, MLA_V_DIM)
    m_scale = (MLA_NOPE_DIM + MLA_ROPE_DIM) ** -0.5

    def mla_block(qnb, qrb):
        s = (jnp.einsum('bqhd,bkhd->bhqk', qnb, k_nope, preferred_element_type=f32)
             + jnp.einsum('bqhr,bkr->bhqk', qrb, kr_all, preferred_element_type=f32)) * m_scale
        p = jax.nn.softmax(s, axis=-1)
        return jnp.einsum('bhqk,bkhe->bqhe', p.astype(v_mla.dtype), v_mla)

    mla_out = _sweep_query_blocks(mla_block, (qn, qr))

    mixed = jnp.concatenate([diff_out.reshape(B, T, D_DIFF), mla_out.reshape(B, T, D_MLA)], axis=-1)
    return mixed @ P['w_o'][l], own

def _ada(cond, l, P):
    return (jax.nn.silu(cond) @ P['w_ada'][l] + P['b_ada'][l])[:, None, :]

def _layer(x, mod, l, P, pos, ctx):
    sm, scm, gm, sf, scf, gf = jnp.split(mod, 6, axis=-1)
    h = _rmsnorm(x, P['norm_mix_g'][l]) * (1 + scm) + sm
    a, own = _mixer(h, l, P, pos, ctx)
    x = x + gm * a
    h = _rmsnorm(x, P['norm_ffn_g'][l]) * (1 + scf) + sf
    if l % 2 == 0:
        i = l // 2
        f = _swiglu(h, P['w_gate'][i], P['w_up'][i], P['w_down'][i])
    else:
        f = _moe(h, l // 2, P)
    x = x + gf * f
    return x, own

def setup_inputs(seed: int = 0) -> dict:
    key = jax.random.key(seed)
    ks = jax.random.split(key, 40)
    f32 = jnp.float32

    def nrm(k, shape, scale=1.0):
        return jax.random.normal(k, shape, f32) * scale

    def gain(k, shape):
        return 1.0 + 0.05 * jax.random.normal(k, shape, f32)

    D = D_MODEL
    return {
        'x_prompt': nrm(ks[0], (BATCH, SEQ, D)),
        'x_sample': nrm(ks[1], (DEC_BATCH, DEC_SEQ, D)),
        'cache_diff_k': nrm(ks[2], (DEC_BATCH, DEPTH, PAST_LEN, N_DIFF_HEADS, 2 * DIFF_HEAD_DIM)),
        'cache_diff_v': nrm(ks[3], (DEC_BATCH, DEPTH, PAST_LEN, N_DIFF_HEADS, DIFF_V_DIM)),
        'cache_mla_ckv': nrm(ks[4], (DEC_BATCH, DEPTH, PAST_LEN, KV_LORA)),
        'cache_mla_krope': nrm(ks[5], (DEC_BATCH, DEPTH, PAST_LEN, MLA_ROPE_DIM)),
        'c': nrm(ks[6], (DEC_BATCH, D)),
        'c_ctx': nrm(ks[7], (D,)),
        'w_ada': nrm(ks[8], (DEPTH, D, 6 * D), 0.5 * D ** -0.5),
        'b_ada': nrm(ks[9], (DEPTH, 6 * D), 0.01),
        'norm_mix_g': gain(ks[10], (DEPTH, D)),
        'norm_ffn_g': gain(ks[11], (DEPTH, D)),
        'w_in': nrm(ks[12], (DEPTH, D, D_IN_PROJ), D ** -0.5),
        'mla_q_norm_g': gain(ks[13], (DEPTH, Q_LORA)),
        'mla_kv_norm_g': gain(ks[14], (DEPTH, KV_LORA)),
        'w_uq': nrm(ks[15], (DEPTH, Q_LORA, N_MLA_HEADS * (MLA_NOPE_DIM + MLA_ROPE_DIM)), Q_LORA ** -0.5),
        'w_uk': nrm(ks[16], (DEPTH, KV_LORA, N_MLA_HEADS * MLA_NOPE_DIM), KV_LORA ** -0.5),
        'w_uv': nrm(ks[17], (DEPTH, KV_LORA, N_MLA_HEADS * MLA_V_DIM), KV_LORA ** -0.5),
        'diff_lq1': nrm(ks[18], (DEPTH, DIFF_HEAD_DIM), 0.1),
        'diff_lk1': nrm(ks[19], (DEPTH, DIFF_HEAD_DIM), 0.1),
        'diff_lq2': nrm(ks[20], (DEPTH, DIFF_HEAD_DIM), 0.1),
        'diff_lk2': nrm(ks[21], (DEPTH, DIFF_HEAD_DIM), 0.1),
        'diff_subln_g': gain(ks[22], (DEPTH, DIFF_V_DIM)),
        'w_o': nrm(ks[23], (DEPTH, D_MIX, D), D_MIX ** -0.5),
        'w_gate': nrm(ks[24], (N_DENSE, D, D_FF), D ** -0.5),
        'w_up': nrm(ks[25], (N_DENSE, D, D_FF), D ** -0.5),
        'w_down': nrm(ks[26], (N_DENSE, D_FF, D), D_FF ** -0.5),
        'router': nrm(ks[27], (N_MOE, D, N_EXPERTS), D ** -0.5),
        'moe_w_gate': nrm(ks[28], (N_MOE, N_EXPERTS, D, D_FF_EXPERT), D ** -0.5),
        'moe_w_up': nrm(ks[29], (N_MOE, N_EXPERTS, D, D_FF_EXPERT), D ** -0.5),
        'moe_w_down': nrm(ks[30], (N_MOE, N_EXPERTS, D_FF_EXPERT, D), D_FF_EXPERT ** -0.5),
        'final_norm_g': gain(ks[31], (D,)),
    }

def reference(x_prompt, x_sample, cache_diff_k, cache_diff_v, cache_mla_ckv, cache_mla_krope,
              c, c_ctx, w_ada, b_ada, norm_mix_g, norm_ffn_g, w_in, mla_q_norm_g, mla_kv_norm_g,
              w_uq, w_uk, w_uv, diff_lq1, diff_lk1, diff_lq2, diff_lk2, diff_subln_g, w_o,
              w_gate, w_up, w_down, router, moe_w_gate, moe_w_up, moe_w_down, final_norm_g):
    P = {'w_ada': w_ada, 'b_ada': b_ada, 'norm_mix_g': norm_mix_g, 'norm_ffn_g': norm_ffn_g,
         'w_in': w_in, 'mla_q_norm_g': mla_q_norm_g, 'mla_kv_norm_g': mla_kv_norm_g,
         'w_uq': w_uq, 'w_uk': w_uk, 'w_uv': w_uv, 'diff_lq1': diff_lq1, 'diff_lk1': diff_lk1,
         'diff_lq2': diff_lq2, 'diff_lk2': diff_lk2, 'diff_subln_g': diff_subln_g, 'w_o': w_o,
         'w_gate': w_gate, 'w_up': w_up, 'w_down': w_down, 'router': router,
         'moe_w_gate': moe_w_gate, 'moe_w_up': moe_w_up, 'moe_w_down': moe_w_down}

    xp = x_prompt
    ks_, vs_, ckvs_, krs_ = [], [], [], []
    for l in range(DEPTH):
        xp, own = _layer(xp, _ada(c_ctx[None, :], l, P), l, P, None, None)
        ks_.append(own[0]); vs_.append(own[1]); ckvs_.append(own[2]); krs_.append(own[3])
    y_prompt = _rmsnorm(xp, final_norm_g)
    new_diff_k = jnp.stack(ks_, axis=1)
    new_diff_v = jnp.stack(vs_, axis=1)
    new_mla_ckv = jnp.stack(ckvs_, axis=1)
    new_mla_krope = jnp.stack(krs_, axis=1)

    T = x_sample.shape[1]
    n_rows = T // GRID_W
    rows = jnp.repeat(jnp.arange(n_rows, dtype=jnp.int32), GRID_W)
    cols = jnp.tile(jnp.arange(GRID_W, dtype=jnp.int32), n_rows)
    xs = x_sample
    for l in range(DEPTH):
        ctx = (cache_diff_k[:, l], cache_diff_v[:, l], cache_mla_ckv[:, l], cache_mla_krope[:, l])
        xs, _ = _layer(xs, _ada(c, l, P), l, P, (rows, cols), ctx)
    y_sample = _rmsnorm(xs, final_norm_g)

    return (y_prompt, y_sample, new_diff_k, new_diff_v, new_mla_ckv, new_mla_krope)


_drawn_inputs = setup_inputs


def setup_inputs(seed=0):
    import zlib

    import numpy as np

    out = dict(_drawn_inputs(seed))
    spreads = {}
    factors = {'cache_mla_ckv': 3.869,
     'cache_mla_krope': 6.377,
     'mla_q_norm_g': 6.985,
     'diff_lq1': 3.824,
     'diff_lk1': 7.133,
     'diff_lq2': 6.559,
     'diff_subln_g': 3.816}
    for name, (base, spread) in spreads.items():
        noise = np.random.default_rng([zlib.crc32(name.encode()), seed]).standard_normal(out[name].shape)
        drawn = base * np.exp(spread * noise) if base else spread * noise
        out[name] = __import__('jax').numpy.asarray(drawn.astype(out[name].dtype))
    for name, factor in factors.items():
        out[name] = (out[name] * factor).astype(out[name].dtype)
    return out
```

```python
import math
from contextlib import ExitStack

import numpy as np

import concourse.bass as bass
from concourse import mybir

P = 128
D_MODEL, KC = 1024, 8
N_LAT, N_PROMPT = 512, 128
T = N_LAT + N_PROMPT
TT = T // P
PAST = 256
NKEY = PAST + T
KT = NKEY // P
LAT_KEYS = PAST + N_LAT
DEPTH = 2
HEADS, HD = 4, 64
QL, KVL, ROPE, NOPE = 256, 128, 32, 64
MQK = NOPE + ROPE
D_FF, FC = 2816, 22
NE, D_FFE, FCE = 8, 1408, 11
SLOTS = 17
XTILES = SLOTS + 2
GRID_W, THETA, EPS = 64, 10000.0, 1e-6
D_SCALE, M_SCALE = HD ** -0.5, MQK ** -0.5
ITEMS = HEADS * TT

V_BADA, V_MIX, V_FFN, V_FIN, V_QN, V_KVN, V_SUB = 0, 96, 112, 128, 136, 140, 142
NV = 144

RING, RING_F = 6, 2048
MRING, MRING_F = 6, 3072
FCH = [384, 384, 384, 256]


def lam_init(l):
    return 0.8 - 0.6 * math.exp(-0.3 * l)


def weight_pieces():
    out = []
    for c in range(8):
        out.append(("ada", 0, c))
    rest = [("ada", 0, c) for c in range(8, 24)] + [("ada", 1, c) for c in range(8)]
    late = [("ada", 1, c) for c in range(8, 24)]
    for l in range(DEPTH):
        out += [("in", l, 1792, 128), ("in", l, 1536, 256)]
        out += [("in", l, c, 256) for c in (512, 768, 0, 256, 1024, 1280)]
        for u in range(8):
            out += rest[3 * u:3 * u + 3] if l == 0 else late[2 * u:2 * u + 2]
        out += [("o", l, c) for c in range(4)]
        if l == 0:
            for j in range(FC // 2):
                out += [("gate", j), ("up", j)]
            for d in range(KC):
                out += [("down", d, 0), ("down", d, 1)]
    return out


PIECES = weight_pieces()
PIECE_AT = {p: n for n, p in enumerate(PIECES)}


def ada_after_head(l, u):
    if l == 0:
        a = [(0, c) for c in range(8, 24)] + [(1, c) for c in range(8)]
        return a[3 * u:3 * u + 3]
    return [(1, c) for c in range(8 + 2 * u, 10 + 2 * u)]


SQ_LAYER = [("mix", k) for k in range(8)] + [("lora", k) for k in range(3)] \
    + [("head", k) for k in range(4)] + [("ffn", k) for k in range(8)]


def sq_at(l, kind, k):
    if l == DEPTH:
        return DEPTH * len(SQ_LAYER) + k
    return l * len(SQ_LAYER) + SQ_LAYER.index((kind, k))


def plan():
    main, aux = {}, {}
    main_freed, aux_freed = [], []

    def m(label, sem, val):
        main[label] = len(main_freed)
        main_freed.append((sem, val))

    def x(label, sem, val):
        aux[label] = len(aux_freed)
        aux_freed.append((sem, val))

    m(("lam",), "lam_exp", 1)
    m(("ada0", 0), "ada_rows", 1)
    m(("ada0", 1), "ada_rows", 2)
    m(("ada0t",), "mod_ready", 1)
    for l in range(DEPTH):
        x(("norm", l, "mix"), "var_ready", 4 * l + 1)
        for g in range(3):
            m(("lora", l, g), "lora_ready", 3 * l + g + 1)
        for r in range(9):
            m(("rope", l, r), "raw_ready", 13 * l + r + 1)
        x(("norm", l, "ckv"), "var_ready", 4 * l + 2)
        x(("norm", l, "cq"), "var_ready", 4 * l + 3)
        for r in range(9):
            x(("rot", l, r), "rot_used", 13 * l + r + 1)
        for v in range(10):
            m(("vd", l, v), "vd_ready", 10 * l + v + 1)
        for h in range(4):
            x(("norm", l, "head", h), "hvar_ready", 4 * l + h + 1)
            if h:
                x(("rot", l, 8 + h), "rot_used", 13 * l + 9 + h)
        x(("rot", l, 12), "rot_used", 13 * l + 13)
        for r in range(9, 13):
            m(("rope", l, r), "raw_ready", 13 * l + r + 1)
        for h in range(4):
            m(("uk", l, h), "km_ready", 4 * l + h + 1)
        for v in range(KT):
            m(("uv", l, v), "vm_ready", KT * l + v + 1)
        for d in range(KC):
            m(("o", l, d), "x_upd", (16 if l else 0) + d + 1)
        x(("norm", l, "ffn"), "var_ready", 4 * l + 4)
        if l == 0:
            for j in range(FC):
                m(("gate", j), "silu_ready", j + 1)
                m(("up", j), "hid_ready", j + 1)
            for d in range(KC):
                m(("down", d), "x_upd", 8 + d + 1)
        else:
            x(("router",), "lg_ready", 1)
            for t in range(TT):
                m(("htok", t), "htok_ready", t + 1)
            x(("rank",), "rank_ready", 1)
            for t in range(TT):
                m(("comb", t), "x_upd", 24 + t + 1)
    x(("norm", DEPTH, "fin"), "var_ready", 4 * DEPTH + 1)
    return main, aux, main_freed, aux_freed


MAIN, AUX, MAIN_FREED, AUX_FREED = plan()


def n_tr_b(it):
    n = it + 1
    return (n // TT) * (TT - 1) + min(n % TT, TT - 1)


def build(nc, d):
    f32, i32, u32 = mybir.dt.float32, mybir.dt.int32, mybir.dt.uint32
    ACT, ALU, AXX = mybir.ActivationFunctionType, mybir.AluOpType, mybir.AxisListType.X

    xperm = nc.dram_tensor("xperm", (XTILES * P, D_MODEL), f32).ap()
    yslots = nc.dram_tensor("yslots", (SLOTS * P, D_MODEL), f32).ap()

    w_ada = d["w_ada"].rearrange("l (k p) n -> l p k n", p=P)
    w_in = d["w_in"].rearrange("l (k p) n -> l p k n", p=P)
    w_o = d["w_o"].rearrange("l (k p) n -> l p k n", p=P)
    w_gate = d["w_gate"].rearrange("l (k p) n -> l p k n", p=P)
    w_up = d["w_up"].rearrange("l (k p) n -> l p k n", p=P)
    w_down = d["w_down"].rearrange("l (k p) n -> l p k n", p=P)
    m_gate = d["moe_w_gate"].rearrange("m e (k p) n -> p (m e k) n", p=P)
    m_up = d["moe_w_up"].rearrange("m e (k p) n -> p (m e k) n", p=P)
    m_down = d["moe_w_down"].rearrange("m e (k p) n -> p (m e k) n", p=P)

    ctx = ExitStack()
    with ctx:
        def sb(name, shape, dt=f32):
            return ctx.enter_context(nc.sbuf_tensor(name, shape, dt))

        sems = {}

        def sem(name):
            sems[name] = ctx.enter_context(nc.semaphore(name))
            return sems[name]

        x_t = sb("x_t", [P, KC, T])
        h_t = sb("h_t", [P, KC, T])
        mixed = h_t
        vecs = sb("vecs", [P, NV])
        mod = sb("mod", [P, DEPTH, 48, 2])
        gain = sb("gain", [P, DEPTH, 2, KC, 2])
        cond = sb("cond", [P, KC, 2])
        lam_in = sb("lam_in", [HD, DEPTH, 2, 2])
        lam_prod = sb("lam_prod", [HD, DEPTH, 2])
        lam_e = sb("lam_e", [P, DEPTH, 2])
        neg_lam = sb("neg_lam", [P, DEPTH])
        subg = sb("subg", [P, DEPTH])
        cos_d, sin_d = sb("cos_d", [P, N_LAT]), sb("sin_d", [P, N_LAT])
        cos_m, sin_m = sb("cos_m", [MQK, N_LAT]), sb("sin_m", [MQK, N_LAT])
        swap_d, swap_m = sb("swap_d", [P, P]), sb("swap_m", [MQK, MQK])
        ident, ones, before = sb("ident", [P, P]), sb("ones", [P, P]), sb("before", [P, P])
        small = sb("small", [P, 64 + 5 + SLOTS])
        tri8 = small[:, 0:64].rearrange("p (a b) -> p a b", a=8)
        steps = small[:, 64:69]
        slot_rows = small[:, 69:69 + SLOTS]
        sq = sb("sq", [P, 2, T])
        rb = sb("rb", [P, T])
        stat = sb("stat", [P, 2, 12])
        diag = sb("diag", [P, 2, P])
        ada_row = sb("ada_row", [2, 3 * 256])
        router_w = sb("router_w", [P, KC, NE])
        lg = sb("lg", [P, TT, NE])
        cmp_a, cmp_b = sb("cmp_a", [P, TT, NE, NE]), sb("cmp_b", [P, TT, NE, NE])
        rt = sb("rt", [P, 8, TT, NE])
        rv = sb("rv", [P, 12, TT])
        cnt = sb("cnt", [P, 4, NE])
        rowi = sb("rowi", [P, 2, TT], u32)
        slot_e = sb("slot_e", [P, SLOTS])
        slot_i = sb("slot_i", [P, SLOTS], i32)

        SMALL_W = 2 * 384 + 256 + 512 + KC * MQK
        ATT = 4 * NKEY + 4 * T + 4 * NKEY + NKEY + 2 * T + NKEY + 4 * LAT_KEYS + 2 * LAT_KEYS
        AR = ATT + 2 * 512 + RING * RING_F + SMALL_W
        arena = sb("arena", [P, AR])
        at = [0]

        def cut(n, pat=None, **kw):
            a = arena[:, at[0]:at[0] + n]
            at[0] += n
            return a.rearrange(pat, **kw) if pat else a

        k_t = cut(4 * NKEY, "p (h n) -> p h n", h=4)
        q_t = cut(4 * T, "p (h n) -> p h n", h=4)
        v_n = cut(4 * NKEY, "p (t n) -> p t n", t=KT)
        ckv_t = cut(NKEY)
        cq_t = cut(2 * T, "p (c n) -> p c n", c=2)
        kr_t = cut(NKEY)
        e_buf = cut(4 * LAT_KEYS, "p (s m n) -> p s m n", s=2, m=2)
        pt_buf = cut(2 * LAT_KEYS, "p (s k n) -> p s k n", s=2, k=6)
        rtmp = cut(1024, "p (s n) -> p s n", s=2)
        ring = cut(RING * RING_F, "p (s n) -> p s n", s=RING)
        wuq = cut(2 * 384, "p (k n) -> p k n", k=2)
        wuk = cut(256)
        wuv = cut(512)
        wkr = cut(KC * MQK, "p (k n) -> p k n", k=KC)
        ada_row0 = e_buf.rearrange("p s m n -> p (s m n)")[0:2, 0:2048]
        e_at = 4 * NKEY + 4 * T + 4 * NKEY + NKEY + 2 * T + NKEY
        lora_raw = arena[:, e_at:e_at + 3 * T].rearrange("p (c n) -> p c n", c=3)
        hrb = arena[:, e_at:e_at + 4 * T].rearrange("p (c n) -> p c n", c=4)
        pt_at = e_at + 4 * LAT_KEYS
        raw = arena[:, pt_at:pt_at + 2 * T].rearrange("p (s n) -> p s n", s=2)
        hid = arena[:, 0:FC * T].rearrange("p (j n) -> p j n", j=FC)
        sil = arena[:, FC * T:FC * T + 2 * T].rearrange("p (s n) -> p s n", s=2)
        at[0] = 0
        mring = cut(MRING * MRING_F, "p (s n) -> p s n", s=MRING)
        xs = cut(D_MODEL)
        xs_t = cut(D_MODEL, "p (k n) -> p k n", k=KC)
        eact = cut(D_FFE)
        eact_t = cut(D_FFE, "p (k n) -> p k n", k=FCE)
        esil = cut(2 * 384, "p (s n) -> p s n", s=2)
        ybuf = cut(D_MODEL)
        htok = cut(TT * D_MODEL, "p (t n) -> p t n", t=TT)
        assert at[0] <= AR
        picked = arena[:, 0:4 * D_MODEL].rearrange("p (s c n) -> p s c n", s=2, c=2)
        zero = ring[:, RING - 1, 0:D_MODEL]

        ps = ctx.enter_context(nc.psum_tensor("ps", [P, 8 * 512], f32))

        def pair(n):
            return ps[:, 1024 * n:1024 * n + T]

        def main_pair(label):
            return pair(MAIN[label] % 3)

        AUXP = pair(3)

        const_in, vec_in, x_in, cond_in = sem("const_in"), sem("vec_in"), sem("x_in"), sem("cond_in")
        w_in_ring = [sem(f"w_arrived{i}") for i in range(RING)]
        w_used = sem("w_used")
        zeroed, zero_rows = sem("zeroed"), sem("zero_rows")
        layer_w_in = sem("layer_w_in")
        cache_k_in, cache_v_in, cache_c_in = sem("cache_k_in"), sem("cache_v_in"), sem("cache_c_in")
        kr_zero = sem("kr_zero")
        main_done, aux_done = sem("main_done"), sem("aux_done")
        cond_ready, lam_exp, lam_prod_ready, mod_ready = sem("cond_ready"), sem("lam_exp"), sem("lam_prod_ready"), sem("mod_ready")
        mod_late = sem("mod_late")
        ada_rows, late_rows, late_rows_done = sem("ada_rows"), sem("late_rows"), sem("late_rows_done")
        ada_done = sem("ada_done")
        sq_ready, sq_used = sem("sq_ready"), sem("sq_used")
        var_ready, std_ready, xn_ready, h_ready = sem("var_ready"), sem("std_ready"), sem("xn_ready"), sem("h_ready")
        hvar_ready, hstd_ready, heads_normed = sem("hvar_ready"), sem("hstd_ready"), sem("heads_normed")
        lora_ready, raw_ready, rot_used, rope_part, rope_done = (sem(n) for n in ("lora_ready", "raw_ready", "rot_used", "rope_part", "rope_done"))
        lat_normed = sem("lat_normed")
        vd_ready, km_ready, vm_ready, kr_spread = sem("vd_ready"), sem("km_ready"), sem("vm_ready"), sem("kr_spread")
        scores_done, max_ready, exp_done, p_ready = (sem(n) for n in ("scores_done", "max_ready", "exp_done", "p_ready"))
        tr_a_done, tr_b_done, pt_a_ready, pt_b_ready, pv_done, pv_evac = (sem(n) for n in ("tr_a_done", "tr_b_done", "pt_a_ready", "pt_b_ready", "pv_done", "pv_evac"))
        mid_bank = sem("mid_bank")
        x_upd = sem("x_upd")
        silu_ready, hid_ready = sem("silu_ready"), sem("hid_ready")
        lg_ready, lmax_ready, lexp_ready, sel_ready, rank_ready, rows_ready = (sem(n) for n in ("lg_ready", "lmax_ready", "lexp_ready", "sel_ready", "rank_ready", "rows_ready"))
        htok_ready, scattered = sem("htok_ready"), sem("scattered")
        m_arrived = [sem(f"m_arrived{i}") for i in range(MRING)]
        m_free, xs_in, gate_done, up_done, esilu_ready, eact_ready = (sem(n) for n in ("m_free", "xs_in", "gate_done", "up_done", "esilu_ready", "eact_ready"))
        etr_done, etr_evac, y_done, y_evac, y_stored = (sem(n) for n in ("etr_done", "etr_evac", "y_done", "y_evac", "y_stored"))
        y_left = sem("y_left")
        gathered = [sem(f"gathered{i}") for i in range(2)]
        comb_ready = sem("comb_ready")
        y_out, kv_out = sem("y_out"), sem("kv_out")
        dve_step, pool_step = sem("dve_step"), sem("pool_step")

        G_EACT, G_ETR = 2, 6
        TR_OF = {0: 0, 1: 1, 2: 2, "xa": 3, "xb": 4, 3: 5}

        N_LAYER_W = 4
        N_CACHE_C = 2
        block = ctx.enter_context(nc.Block())

        @block.sync
        def _(sp):
            sp.dma_start(cond[:], d["cond"]).then_inc(cond_in, 16)
            sp.dma_start(vecs[:], d["vecs"]).then_inc(vec_in, 16)
            sp.dma_start(lam_in[:], d["lam"]).then_inc(vec_in, 16)

            def piece(n):
                kind = PIECES[n]
                slot = ring[:, n % RING, :]
                if n >= RING:
                    sp.wait_ge(w_used, n - RING + 1)
                if n == RING - 1:
                    sp.wait_ge(zero_rows, 16 * XTILES)
                if kind[0] == "ada":
                    src, c, w, kk = w_ada[kind[1]], kind[2] * 256, 256, KC
                elif kind[0] == "in":
                    src, c, w, kk = w_in[kind[1]], kind[2], kind[3], KC
                elif kind[0] == "o":
                    src, c, w, kk = w_o[kind[1]], kind[2] * 256, 256, KC
                elif kind[0] in ("gate", "up"):
                    src, c, w, kk = (w_gate if kind[0] == "gate" else w_up)[0], kind[1] * 256, 256, KC
                else:
                    src = w_down[0, :, kind[2] * FCE:(kind[2] + 1) * FCE, :]
                    c, w, kk = kind[1] * P, P, FCE
                dst = slot[:, 0:kk * w].rearrange("p (k n) -> p k n", k=kk)
                sp.dma_start(dst, src[:, :, c:c + w]).then_inc(w_in_ring[n % RING], 16)

            for n in range(2):
                piece(n)
            sp.dma_start(x_t[:], d["x_t"]).then_inc(x_in, 16)
            for dst, name in ((cos_d, "cos_d"), (sin_d, "sin_d"), (cos_m, "cos_m"), (sin_m, "sin_m"),
                              (swap_d, "swap_d"), (swap_m, "swap_m"), (ident, "ident"), (before, "before"),
                              (small, "small")):
                sp.dma_start(dst[:], d[name]).then_inc(const_in, 16)
            sp.dma_start(router_w[:], d["router"].rearrange("m (k p) n -> (m p) k n", p=P)).then_inc(const_in, 16)
            for n in range(2, len(PIECES)):
                piece(n)

            sp.wait_ge(rows_ready, 2)
            with sp.Fori(0, SLOTS) as s:
                e = sp.value_load(slot_i[0:1, bass.ds(s, 1)], min_val=0, max_val=NE - 1)
                for n in range(12):
                    sp.wait_ge(m_free, 12 * s + n + 1)
                    if n < 8:
                        c, w = sum(FCH[:n // 2]), FCH[n // 2]
                        src = (m_up if n % 2 else m_gate)[:, bass.ds(e * KC, KC), c:c + w]
                        dst = mring[:, n % MRING, 0:KC * w].rearrange("p (k n) -> p k n", k=KC)
                    else:
                        k0, kn = 3 * (n - 8), FCH[n - 8] // P
                        src = m_down[:, bass.ds(e * FCE + k0, kn), :]
                        dst = mring[:, n % MRING, 0:kn * D_MODEL].rearrange("p (k n) -> p k n", k=kn)
                    sp.dma_start(dst, src).then_inc(m_arrived[n % MRING], 16)

            sp.wait_ge(h_ready, 8 * 5)
            yt = d["y_t"]
            sp.dma_start(yt, h_t[:]).then_inc(y_out, 16)
            sp.wait_ge(y_out, 16)
            sp.wait_ge(kv_out, 16 * 4 * DEPTH)

        @block.gpsimd
        def _(pool):
            steps_done = [0]

            def link(ins):
                steps_done[0] += 1
                ins.then_inc(pool_step, 1)
                pool.wait_ge(pool_step, steps_done[0])

            nc.gpsimd.memset(ones[:], 1.0).then_inc(zeroed, 1)
            nc.gpsimd.memset(zero, 0.0).then_inc(zeroed, 1)
            nc.gpsimd.memset(wkr[:, :, 0:NOPE], 0.0).then_inc(kr_zero, 1)
            pool.wait_ge(const_in, 16 * 10)

            def rope_item(l, r):
                n = 13 * l + r
                rows = MQK if r in (0, 9, 10, 11, 12) else P
                cs = cos_m if rows == MQK else cos_d
                src = raw[0:rows, n % 2, :]
                if r == 0:
                    out = kr_t[0:rows, PAST:NKEY]
                elif r <= 4:
                    out = k_t[0:rows, r - 1, PAST:NKEY]
                elif r <= 8:
                    out = q_t[0:rows, r - 5, :]
                else:
                    out = q_t[0:rows, r - 9, :]
                pool.wait_ge(raw_ready, n + 1)
                if r == 9:
                    pool.wait_ge(scores_done, (2 * l + 1) * ITEMS)
                nc.gpsimd.tensor_copy(out[:, N_LAT:T], src[:, N_LAT:T])
                link(nc.gpsimd.tensor_tensor(out[:, 0:N_LAT], src[:, 0:N_LAT], cs[0:rows, :], ALU.mult))
                pool.wait_ge(rot_used, n + 1)
                nc.gpsimd.tensor_tensor(out[:, 0:N_LAT], out[:, 0:N_LAT], rtmp[0:rows, n % 2, :],
                                        ALU.add).then_inc(rope_done, 1)

            for l in range(DEPTH):
                for r in range(9):
                    rope_item(l, r)
                for r in range(9, 13):
                    rope_item(l, r)
                pool.wait_ge(rope_done, 13 * l + 13)
                pool.wait_ge(cache_c_in, 16 * N_CACHE_C * (l + 1))
                pool.wait_ge(kv_out, 16 * 4 * (l + 1))
                for h in range(HEADS):
                    nc.gpsimd.tensor_copy(k_t[NOPE:MQK, h, :], kr_t[NOPE:MQK, :]).then_inc(kr_spread, 1)

            pool.wait_ge(rows_ready, 1)
            pool.wait_ge(zero_rows, 16 * XTILES)
            for t in range(TT):
                pool.wait_ge(htok_ready, t + 1)
                for c in range(2):
                    pool.indirect_dma_start(
                        out=xperm, out_offset=bass.IndirectOffsetOnAxis(ap=rowi[:, c, t:t + 1], axis=0),
                        in_=htok[:, t, :], in_offset=None).then_inc(scattered, 16)
            pool.wait_ge(scattered, 16 * 2 * TT)
            pool.dma_start(xs, xperm[0:P, :]).then_inc(xs_in, 16)
            pool.wait_ge(etr_done, 2)
            pool.dma_start(xs, xperm[P:2 * P, :]).then_inc(xs_in, 16)
            pool.drain().then_inc(y_left, 1)
            with pool.Fori(0, SLOTS) as s:
                pool.wait_ge(etr_done, 2 + G_ETR + 6 * s + TR_OF["xb"] + 1)
                pool.dma_start(xs, xperm[bass.ds((s + 2) * P, P), :]).then_inc(xs_in, 16)
                pool.wait_ge(y_evac, s + 2)
                pool.dma_start(yslots[bass.ds(s * P, P), :], ybuf).then_inc(y_stored, 16)
                pool.wait_ge(y_stored, 16 * (s + 1))
                pool.sem_inc(y_left, 1)
            pool.wait_ge(y_stored, 16 * SLOTS)
            pool.wait_ge(xs_in, 16 * (SLOTS + 2))
            for t in range(TT):
                if t >= 2:
                    pool.wait_ge(comb_ready, t - 1)
                    pool.wait_ge(main_done, MAIN[("comb", t - 2)] + 1)
                for c in range(2):
                    pool.indirect_dma_start(
                        out=picked[:, t % 2, c, :], out_offset=None, in_=yslots,
                        in_offset=bass.IndirectOffsetOnAxis(ap=rowi[:, c, t:t + 1], axis=0)).then_inc(gathered[t % 2], 16)

        @block.scalar
        def _(act):
            act.wait_ge(zeroed, 2)
            for t in range(XTILES):
                act.dma_start(xperm[t * P:(t + 1) * P, :], zero).then_inc(zero_rows, 16)
            act.wait_ge(cond_in, 16)
            nc.scalar.activation(cond[:], cond[:], ACT.Silu).then_inc(cond_ready, 1)
            act.wait_ge(main_done, MAIN[("lam",)] + 1)
            nc.scalar.activation(lam_e[:].rearrange("p l m -> p (l m)"), main_pair(("lam",))[:, 0:4],
                                 ACT.Exp).then_inc(lam_exp, 1)

            def square(l, kind, k, src):
                n = sq_at(l, kind, k)
                if n >= 2:
                    act.wait_ge(sq_used, n - 1)
                nc.scalar.activation(sq[:, n % 2, :], src, ACT.Square).then_inc(sq_ready, 1)

            def root(v):
                act.wait_ge(var_ready, v)
                nc.scalar.activation(rb[:], rb[:], ACT.Sqrt).then_inc(std_ready, 1)

            def modulate(n, l, which):
                for k in range(KC):
                    act.wait_ge(xn_ready, 8 * n + k + 1)
                    s0 = 0 if which == 0 else 24
                    for c, (a, b) in enumerate(((0, N_LAT), (N_LAT, T))):
                        ins = nc.scalar.activation(h_t[:, k, a:b], h_t[:, k, a:b], ACT.Identity,
                                                   bias=mod[:, l, s0 + k, c:c + 1],
                                                   scale=gain[:, l, which, k, c:c + 1])
                    ins.then_inc(h_ready, 1)

            def raw_item(l, r):
                n = 13 * l + r
                rows = MQK if r in (0, 9, 10, 11, 12) else P
                act.wait_ge(main_done, MAIN[("rope", l, r)] + 1)
                if n >= 2:
                    act.wait_ge(rope_done, n - 1)
                    act.wait_ge(rot_used, n - 1)
                nc.scalar.activation(raw[0:rows, n % 2, :], main_pair(("rope", l, r))[0:rows, :],
                                     ACT.Copy).then_inc(raw_ready, 1)

            for l in range(DEPTH):
                if l:
                    act.wait_ge(pv_done, 2 * ITEMS * l)
                    act.wait_ge(main_done, MAIN[("uv", l - 1, KT - 1)] + 1)
                act.dma_start(wuq, d["w_uq"][l].rearrange("(k p) n -> p k n", p=P)).then_inc(layer_w_in, 16)
                act.dma_start(wuk, d["w_uk"][l]).then_inc(layer_w_in, 16)
                act.dma_start(wuv, d["w_uv"][l]).then_inc(layer_w_in, 16)
                if l == 0:
                    act.wait_ge(kr_zero, 1)
                act.dma_start(wkr[:, :, NOPE:MQK], w_in[l, :, :, 1920:1952]).then_inc(layer_w_in, 16)
                for k in range(KC):
                    if l == 0 and k == 0:
                        act.wait_ge(x_in, 16)
                    if l:
                        act.wait_ge(x_upd, 8 + k + 1)
                    square(l, "mix", k, x_t[:, k, :])
                if l:
                    act.wait_ge(x_upd, 16)
                act.dma_start(ckv_t[:, 0:PAST], d["cache_ckv"][l]).then_inc(cache_c_in, 16)
                act.dma_start(kr_t[NOPE:MQK, 0:PAST], d["cache_kr"][l]).then_inc(cache_c_in, 16)
                act.dma_start(k_t[:, :, 0:PAST], d["cache_k"][l]).then_inc(cache_k_in, 16)
                act.dma_start(v_n[:, 0:2, :], d["cache_v"][l]).then_inc(cache_v_in, 16)
                root(4 * l + 1)
                modulate(2 * l, l, 0)
                for g in range(3):
                    src = main_pair(("lora", l, g))
                    act.wait_ge(main_done, MAIN[("lora", l, g)] + 1)
                    square(l, "lora", g, src)
                    if l and g == 0:
                        act.wait_ge(x_upd, 16)
                    nc.scalar.activation(lora_raw[:, g, :], src, ACT.Copy).then_inc(lora_ready, 1)
                raw_item(l, 0)
                root(4 * l + 2)
                raw_item(l, 1)
                root(4 * l + 3)
                for r in range(2, 9):
                    raw_item(l, r)
                act.wait_ge(rope_done, 13 * l + 9)
                act.dma_start(d["new_k"][l], k_t[:, :, NKEY - N_PROMPT:NKEY]).then_inc(kv_out, 16)
                act.dma_start(d["new_kr"][l], kr_t[NOPE:MQK, NKEY - N_PROMPT:NKEY]).then_inc(kv_out, 16)
                act.wait_ge(lat_normed, 2 * l + 1)
                act.dma_start(d["new_ckv"][l], ckv_t[:, NKEY - N_PROMPT:NKEY]).then_inc(kv_out, 16)
                act.wait_ge(vd_ready, 10 * l + 10)
                act.dma_start(d["new_v"][l], v_n[:, KT - 1, :]).then_inc(kv_out, 16)

                def attention(f):
                    base = (2 * l + f) * ITEMS
                    maps, scale = (2, D_SCALE) if f == 0 else (1, M_SCALE)

                    def exps(i):
                        it = base + i
                        nk = LAT_KEYS if i % TT < TT - 1 else N_PROMPT
                        sc = ps[:, 1536 * (it % 2):1536 * (it % 2) + 1536].rearrange("p (m n) -> p m n", m=2)
                        if it >= 2:
                            act.wait_ge(tr_a_done, it - 1)
                            act.wait_ge(tr_b_done, n_tr_b(it - 2))
                        if f == 0 and i < 2:
                            act.wait_ge(lat_normed, 2 * l + 2)
                            act.wait_ge(rope_done, 13 * l + 9)
                        act.wait_ge(max_ready, it + 1)
                        for m in range(maps):
                            ins = nc.scalar.activation(e_buf[:, it % 2, m, 0:nk], sc[:, m, 0:nk], ACT.Exp,
                                                       bias=stat[:, it % 2, 2 + m:3 + m], scale=scale,
                                                       accum_out=stat[:, it % 2, 4 + m:5 + m])
                        ins.then_inc(exp_done, 1)

                    exps(0)
                    for i in range(ITEMS):
                        it = base + i
                        if i + 1 < ITEMS:
                            exps(i + 1)
                        nt = 4 if i % TT < TT - 1 else 1
                        act.wait_ge(tr_a_done, it + 1)
                        if it >= 2:
                            act.wait_ge(pv_done, it - 1)
                        nc.scalar.activation(pt_buf[:, it % 2, 0:nt, :], ps[:, 3072:3072 + nt * P].rearrange("p (k n) -> p k n", k=nt),
                                             ACT.Copy).then_inc(pt_a_ready, 1)

                attention(0)
                for h in range(HEADS):
                    if h == 0:
                        act.wait_ge(pv_evac, (2 * l + 1) * ITEMS)
                    square(l, "head", h, mixed[:, h, :])
                    if h:
                        raw_item(l, 8 + h)
                raw_item(l, 12)
                act.wait_ge(hvar_ready, 4 * l + 4)
                nc.scalar.activation(hrb, hrb, ACT.Sqrt).then_inc(hstd_ready, 1)
                for v in range(KT):
                    act.wait_ge(main_done, MAIN[("uv", l, v)] + 1)
                    nc.scalar.activation(v_n[:, v, :], main_pair(("uv", l, v))[:, 0:512], ACT.Copy).then_inc(vm_ready, 1)
                act.wait_ge(heads_normed, 4 * l + 4)
                attention(1)
                for k in range(KC):
                    act.wait_ge(x_upd, (16 if l else 0) + k + 1)
                    square(l, "ffn", k, x_t[:, k, :])
                root(4 * l + 4)
                modulate(2 * l + 1, l, 1)
                if l == 0:
                    for j in range(FC):
                        act.wait_ge(main_done, MAIN[("gate", j)] + 1)
                        if j >= 2:
                            act.wait_ge(hid_ready, j - 1)
                        nc.scalar.activation(sil[:, j % 2, :], main_pair(("gate", j)), ACT.Silu).then_inc(silu_ready, 1)

            act.wait_ge(lmax_ready, 1)
            nc.scalar.activation(rt[:, 0], rt[:, 0], ACT.Exp).then_inc(lexp_ready, 1)
            for t in range(TT):
                act.wait_ge(main_done, MAIN[("htok", t)] + 1)
                src = ps[:, 1024 * (MAIN[("htok", t)] % 3):1024 * (MAIN[("htok", t)] % 3) + 1024]
                nc.scalar.activation(htok[:, t, :], src, ACT.Copy).then_inc(htok_ready, 1)

            def x_evac(half, n_done, n_bank):
                bank = 4 + (TR_OF["xa"] + half + 0) % 2
                nc.scalar.activation(xs_t[:, 4 * half:4 * half + 4, :],
                                     ps[:, 512 * bank:512 * bank + 512].rearrange("p (k n) -> p k n", k=4),
                                     ACT.Copy).then_inc(etr_evac, 1)

            for half in range(2):
                act.wait_ge(etr_done, half + 1)
                x_evac(half, 0, 0)
            with act.Fori(0, SLOTS) as s:
                def tr_evac(c):
                    j = TR_OF[c]
                    bank = 4 + j % 2
                    act.wait_ge(etr_done, 2 + G_ETR + 6 * s + j + 1)
                    if c in ("xa", "xb"):
                        x_evac(j - TR_OF["xa"], 0, 0)
                        return
                    if c == 0:
                        act.wait_ge(y_done, s + 1)
                    kn = FCH[c] // P
                    nc.scalar.activation(eact_t[:, 3 * c:3 * c + kn, :],
                                         ps[:, 512 * bank:512 * bank + kn * P].rearrange("p (k n) -> p k n", k=kn),
                                         ACT.Copy).then_inc(etr_evac, 1)

                def silu(c):
                    bank = (2 * c) % 4
                    act.wait_ge(gate_done, 4 * s + c + 1)
                    act.wait_ge(eact_ready, 4 * s + c + 1)
                    nc.scalar.activation(esil[:, c % 2, 0:FCH[c]], ps[:, 512 * bank:512 * bank + FCH[c]],
                                         ACT.Silu).then_inc(esilu_ready, 1)

                silu(0)
                silu(1)
                tr_evac(0)
                silu(2)
                tr_evac(1)
                silu(3)
                tr_evac(2)
                tr_evac("xa")
                tr_evac("xb")
                tr_evac(3)

            for k in range(KC):
                act.wait_ge(x_upd, 24 + TT)
                square(DEPTH, "fin", k, x_t[:, k, :])
            root(4 * DEPTH + 1)
            for k in range(KC):
                act.wait_ge(xn_ready, 8 * 4 + k + 1)
                nc.scalar.activation(h_t[:, k, :], h_t[:, k, :], ACT.Copy, scale=vecs[:, V_FIN + k:V_FIN + k + 1]).then_inc(h_ready, 1)

        @block.vector
        def _(dve):
            steps_done = [0]

            def link(ins):
                steps_done[0] += 1
                ins.then_inc(dve_step, 1)
                dve.wait_ge(dve_step, steps_done[0])

            dve.wait_ge(vec_in, 32)
            nc.vector.tensor_tensor(lam_prod[:], lam_in[:, :, :, 0], lam_in[:, :, :, 1], ALU.mult).then_inc(lam_prod_ready, 1)
            for l in range(DEPTH):
                link(nc.vector.tensor_scalar(subg[:, l:l + 1], vecs[:, V_SUB + l:V_SUB + l + 1], 1.0 - lam_init(l), None, ALU.mult))
            dve.wait_ge(lam_exp, 1)
            for l in range(DEPTH):
                link(nc.vector.tensor_tensor(neg_lam[:, l:l + 1], lam_e[:, l, 1:2], lam_e[:, l, 0:1], ALU.subtract))
                link(nc.vector.tensor_scalar(neg_lam[:, l:l + 1], neg_lam[:, l:l + 1], -lam_init(l), None, ALU.add))

            def add_bias(l, c0, n, src):
                b = vecs[:, V_BADA + 48 * l + c0:V_BADA + 48 * l + c0 + n]
                return nc.vector.tensor_tensor(mod[:, l, c0:c0 + n, :], src.rearrange("p (c g) -> p c g", g=2),
                                               b.unsqueeze(2).to_broadcast([P, n, 2]), ALU.add)

            def make_gain(l, which):
                g = vecs[:, (V_MIX, V_FFN)[which] + 8 * l:(V_MIX, V_FFN)[which] + 8 * l + 8]
                s0 = (8, 32)[which]
                link(nc.vector.scalar_tensor_tensor(gain[:, l, which], mod[:, l, s0:s0 + 8, :], 1.0,
                                                    g.unsqueeze(2).to_broadcast([P, KC, 2]), ALU.add, ALU.mult))

            for n in range(2):
                dve.wait_ge(main_done, MAIN[("ada0", n)] + 1)
                o = 1024 * (MAIN[("ada0", n)] % 3)
                nc.vector.tensor_copy(ada_row0[:, 1024 * n:1024 * n + 1024], ps[0:2, o:o + 1024]).then_inc(ada_rows, 1)
            dve.wait_ge(main_done, MAIN[("ada0t",)] + 1)
            add_bias(0, 0, 16, main_pair(("ada0t",))[:, 0:32]).then_inc(mod_ready, 1)
            dve.wait_ge(mod_ready, 1)
            make_gain(0, 0)

            def norm(n, l, v, aux_label):
                dve.wait_ge(aux_done, AUX[aux_label] + 1)
                nc.vector.tensor_scalar(rb[:], AUXP, 1.0 / D_MODEL, EPS, ALU.mult, ALU.add).then_inc(var_ready, 1)
                dve.wait_ge(std_ready, v)
                link(nc.vector.reciprocal(rb[:], rb[:]))
                for k in range(KC):
                    nc.vector.tensor_tensor(h_t[:, k, :], x_t[:, k, :], rb[:], ALU.mult).then_inc(xn_ready, 1)

            def rot(l, r):
                n = 13 * l + r
                rows = MQK if r in (0, 9, 10, 11, 12) else P
                sn = sin_m if rows == MQK else sin_d
                dve.wait_ge(aux_done, AUX[("rot", l, r)] + 1)
                if n >= 2:
                    dve.wait_ge(rope_done, n - 1)
                nc.vector.tensor_tensor(rtmp[0:rows, n % 2, :], AUXP[0:rows, 0:N_LAT], sn[0:rows, :],
                                        ALU.mult).then_inc(rot_used, 1)

            def residual(l, label, d_, g0):
                dve.wait_ge(main_done, MAIN[label] + 1)
                src = main_pair(label)
                for c, (a, b) in enumerate(((0, N_LAT), (N_LAT, T))):
                    ins = nc.vector.scalar_tensor_tensor(x_t[:, d_, a:b], src[:, a:b], mod[:, l, g0 + d_, c:c + 1],
                                                         x_t[:, d_, a:b], ALU.mult, ALU.add)
                ins.then_inc(x_upd, 1)

            for l in range(DEPTH):
                if l == 0:
                    dve.wait_ge(x_in, 16)
                    dve.wait_ge(const_in, 160)
                norm(2 * l, l, 4 * l + 1, ("norm", l, "mix"))
                dve.wait_ge(lora_ready, 3 * l + 3)
                dve.wait_ge(aux_done, AUX[("norm", l, "ckv")] + 1)
                nc.vector.tensor_scalar(rb[:], AUXP, 1.0 / KVL, EPS, ALU.mult, ALU.add).then_inc(var_ready, 1)
                dve.wait_ge(std_ready, 4 * l + 2)
                link(nc.vector.reciprocal(rb[:], rb[:]))
                nc.vector.scalar_tensor_tensor(ckv_t[:, PAST:NKEY], lora_raw[:, 0, :], vecs[:, V_KVN + l:V_KVN + l + 1],
                                               rb[:], ALU.mult, ALU.mult).then_inc(lat_normed, 1)
                dve.wait_ge(lat_normed, 2 * l + 1)
                dve.wait_ge(aux_done, AUX[("norm", l, "cq")] + 1)
                nc.vector.tensor_scalar(rb[:], AUXP, 1.0 / QL, EPS, ALU.mult, ALU.add).then_inc(var_ready, 1)
                dve.wait_ge(std_ready, 4 * l + 3)
                link(nc.vector.reciprocal(rb[:], rb[:]))
                for c in range(2):
                    ins = nc.vector.scalar_tensor_tensor(cq_t[:, c, :], lora_raw[:, 1 + c, :],
                                                         vecs[:, V_QN + 2 * l + c:V_QN + 2 * l + c + 1],
                                                         rb[:], ALU.mult, ALU.mult)
                ins.then_inc(lat_normed, 1)
                for r in range(7):
                    rot(l, r)

                def vd(v):
                    half, t = v // TT, v % TT
                    dve.wait_ge(main_done, MAIN[("vd", l, v)] + 1)
                    nc.vector.tensor_copy(v_n[:, 2 + t, 256 * half:256 * half + 256],
                                          main_pair(("vd", l, v))[:, 0:256]).then_inc(vd_ready, 1)

                vd(0)
                rot(l, 7)
                vd(1)
                rot(l, 8)
                for v in range(2, 10):
                    vd(v)

                def attention(f):
                    base = (2 * l + f) * ITEMS
                    maps, scale = (2, D_SCALE) if f == 0 else (1, M_SCALE)

                    def item(i):
                        return base + i, (base + i) % 2, LAT_KEYS if i % TT < TT - 1 else N_PROMPT

                    def maxes(i):
                        it, b, nk = item(i)
                        sc = ps[:, 1536 * b:1536 * b + 1536].rearrange("p (m n) -> p m n", m=2)
                        dve.wait_ge(scores_done, it + 1)
                        if it >= 2:
                            dve.wait_ge(exp_done, it - 1)
                        link(nc.vector.reduce_max(stat[:, b, 0:maps], sc[:, 0:maps, 0:nk], AXX))
                        nc.vector.tensor_scalar(stat[:, b, 2:2 + maps], stat[:, b, 0:maps], -scale, None,
                                                ALU.mult).then_inc(max_ready, 1)

                    def combine(i):
                        it, b, nk = item(i)
                        dve.wait_ge(exp_done, it + 1)
                        if it >= 2:
                            dve.wait_ge(tr_a_done, it - 1)
                            dve.wait_ge(tr_b_done, n_tr_b(it - 2))
                        link(nc.vector.reciprocal(stat[:, b, 6:6 + maps], stat[:, b, 4:4 + maps]))
                        ins = nc.vector.tensor_scalar(diag[:, b, :], ident[:], stat[:, b, 6:7], None, ALU.mult)
                        if f == 0:
                            link(nc.vector.scalar_tensor_tensor(stat[:, b, 8:9], stat[:, b, 4:5], neg_lam[:, l:l + 1],
                                                                stat[:, b, 7:8], ALU.mult, ALU.mult))
                            e1 = e_buf[:, b, 0, 0:nk]
                            ins = nc.vector.scalar_tensor_tensor(e1, e_buf[:, b, 1, 0:nk], stat[:, b, 8:9], e1,
                                                                 ALU.mult, ALU.add)
                        ins.then_inc(p_ready, 1)

                    def pv_out(i):
                        it, b, nk = item(i)
                        h, qt = i // TT, i % TT
                        dve.wait_ge(pv_done, it + 1)
                        nc.vector.tensor_copy(mixed[:, 4 * f + h, qt * P:(qt + 1) * P], ps[:, 3840:3968]).then_inc(pv_evac, 1)

                    def pt_b(i):
                        it, b, nk = item(i)
                        dve.wait_ge(tr_b_done, n_tr_b(it))
                        if it >= 2:
                            dve.wait_ge(pv_done, it - 1)
                        nc.vector.tensor_copy(pt_buf[:, b, 4:6, :], ps[:, 3584:3840].rearrange("p (k n) -> p k n", k=2)).then_inc(pt_b_ready, 1)

                    def late_row_copy(u, b):
                        n = len(ada_after_head(l, u))
                        dve.wait_ge(late_rows_done, 8 * l + u + 1)
                        if 8 * l + u:
                            dve.wait_ge(ada_done, 8 * l + u)
                        src = ps[0:2, 1536 * b:1536 * b + 512 * n].rearrange("p (n c) -> p n c", n=n)[:, :, 0:256]
                        nc.vector.tensor_copy(ada_row[:, 0:256 * n].rearrange("p (n c) -> p n c", n=n), src).then_inc(late_rows, 1)

                    def late_mods(u):
                        todo = ada_after_head(l, u)
                        dve.wait_ge(ada_done, 8 * l + u + 1)
                        src = ps[:, 3968:3968 + 4 * len(todo)]
                        for n, (ll, c) in enumerate(todo):
                            ins = add_bias(ll, 2 * c, 2, src[:, 4 * n:4 * n + 4])
                        ins.then_inc(mod_late, 1)

                    maxes(0)
                    combine(0)
                    for i in range(ITEMS):
                        if i + 1 < ITEMS:
                            maxes(i + 1)
                        if i:
                            pv_out(i - 1)
                        if i % TT == TT - 1:
                            late_row_copy(4 * f + i // TT, (base + i) % 2)
                        if i % TT == 0 and i:
                            late_mods(4 * f + i // TT - 1)
                        if i % TT < TT - 1:
                            pt_b(i)
                        if i + 1 < ITEMS:
                            combine(i + 1)
                    pv_out(ITEMS - 1)
                    late_mods(4 * f + HEADS - 1)

                attention(0)
                for h in range(HEADS):
                    dve.wait_ge(aux_done, AUX[("norm", l, "head", h)] + 1)
                    if h == 0:
                        dve.wait_ge(tr_a_done, (2 * l + 1) * ITEMS)
                        dve.wait_ge(tr_b_done, n_tr_b((2 * l + 1) * ITEMS - 1))
                    nc.vector.tensor_scalar(hrb[:, h, :], AUXP, 1.0 / P, EPS, ALU.mult, ALU.add).then_inc(hvar_ready, 1)
                    if h:
                        rot(l, 8 + h)
                rot(l, 12)
                for h in range(HEADS):
                    if h == 0:
                        dve.wait_ge(kv_out, 16 * 4 * (l + 1))
                    dve.wait_ge(main_done, MAIN[("uk", l, h)] + 1)
                    src = ps[0:NOPE, 1024 * (MAIN[("uk", l, h)] % 3):1024 * (MAIN[("uk", l, h)] % 3) + 1024]
                    nc.vector.tensor_copy(k_t[0:NOPE, h, :].rearrange("p (c n) -> p c n", c=2),
                                          src.rearrange("p (c n) -> p c n", c=2)[:, :, 0:448]).then_inc(km_ready, 1)
                dve.wait_ge(hstd_ready, l + 1)
                link(nc.vector.reciprocal(hrb, hrb))
                for h in range(HEADS):
                    nc.vector.scalar_tensor_tensor(mixed[:, h, :], mixed[:, h, :], subg[:, l:l + 1], hrb[:, h, :],
                                                   ALU.mult, ALU.mult).then_inc(heads_normed, 1)
                attention(1)
                dve.wait_ge(mod_late, 8 * l + 8)
                make_gain(l, 1)
                if l + 1 < DEPTH:
                    make_gain(l + 1, 0)
                for d_ in range(KC):
                    residual(l, ("o", l, d_), d_, 16)
                norm(2 * l + 1, l, 4 * l + 4, ("norm", l, "ffn"))
                if l == 0:
                    for j in range(FC):
                        dve.wait_ge(main_done, MAIN[("up", j)] + 1)
                        dve.wait_ge(silu_ready, j + 1)
                        nc.vector.tensor_tensor(hid[:, j, :], sil[:, j % 2, :], main_pair(("up", j)), ALU.mult).then_inc(hid_ready, 1)
                    for d_ in range(KC):
                        residual(l, ("down", d_), d_, 40)

            dve.wait_ge(aux_done, AUX[("router",)] + 1)
            nc.vector.tensor_copy(lg[:].rearrange("p t e -> p (t e)"), AUXP[:, 0:TT * NE]).then_inc(lg_ready, 1)
            dve.wait_ge(lg_ready, 1)
            by_e = lg[:].unsqueeze(3).to_broadcast([P, TT, NE, NE])
            by_o = lg[:].unsqueeze(2).to_broadcast([P, TT, NE, NE])

            def flat(a):
                return a.rearrange("p t e o -> p t (e o)")

            link(nc.vector.reduce_max(rv[:, 0], lg[:], AXX))
            link(nc.vector.tensor_tensor(rt[:, 0], lg[:], rv[:, 0].unsqueeze(2).to_broadcast([P, TT, NE]), ALU.subtract))
            nc.vector.drain().then_inc(lmax_ready, 1)
            link(nc.vector.tensor_tensor(cmp_a[:], by_o, by_e, ALU.is_gt))
            link(nc.vector.tensor_tensor(cmp_b[:], by_o, by_e, ALU.is_equal))
            for t in range(TT):
                link(nc.vector.tensor_tensor(cmp_b[:, t], cmp_b[:, t], tri8, ALU.mult))
            link(nc.vector.tensor_tensor(flat(cmp_a[:]), flat(cmp_a[:]), flat(cmp_b[:]), ALU.add))
            link(nc.vector.reduce_sum(rt[:, 1], cmp_a[:], AXX))
            nc.vector.tensor_scalar(rt[:, 4], rt[:, 1], 2.0, None, ALU.is_lt).then_inc(sel_ready, 1)
            link(nc.vector.tensor_scalar(rt[:, 2], rt[:, 1], 0.0, None, ALU.is_equal))
            link(nc.vector.tensor_scalar(rt[:, 3], rt[:, 1], 1.0, None, ALU.is_equal))
            dve.wait_ge(aux_done, AUX[("rank",)] + 1)
            nc.vector.tensor_copy(rt[:, 5].rearrange("p t e -> p (t e)"), AUXP[:, 0:TT * NE])
            nc.vector.tensor_copy(cnt[:, 0], AUXP[:, TT * NE:TT * NE + NE]).then_inc(rank_ready, 1)
            dve.wait_ge(rank_ready, 1)
            c58 = cmp_a[:, 0].rearrange("p a b -> p (a b)")[:, 0:NE * TT].rearrange("p (a b) -> p a b", a=NE)
            link(nc.vector.tensor_tensor(c58, cnt[:, 0].unsqueeze(2).to_broadcast([P, NE, TT]),
                                         steps.unsqueeze(1).to_broadcast([P, NE, TT]), ALU.is_gt))
            link(nc.vector.reduce_sum(cnt[:, 1], c58, AXX))
            link(nc.vector.tensor_tensor(cmp_a[:, 0], cnt[:, 1].unsqueeze(1).to_broadcast([P, NE, NE]), tri8, ALU.mult))
            link(nc.vector.reduce_sum(cnt[:, 2], cmp_a[:, 0], AXX))
            link(nc.vector.tensor_scalar(cnt[:, 3], cnt[:, 2], float(P), None, ALU.mult))
            link(nc.vector.tensor_tensor(rt[:, 5], rt[:, 5], cnt[:, 3].unsqueeze(1).to_broadcast([P, TT, NE]), ALU.add))
            for c in range(2):
                link(nc.vector.tensor_tensor(rt[:, 6], rt[:, 2 + c], rt[:, 5], ALU.mult))
                link(nc.vector.reduce_sum(rv[:, 1 + c], rt[:, 6], AXX))
            nc.vector.tensor_copy(rowi[:], rv[:, 1:3]).then_inc(rows_ready, 1)
            c17 = cmp_b[:, 0:2].rearrange("p t a b -> p (t a b)")[:, 0:SLOTS * 7].rearrange("p (a b) -> p a b", a=SLOTS)
            link(nc.vector.tensor_tensor(c17, slot_rows.unsqueeze(2).to_broadcast([P, SLOTS, 7]),
                                         cnt[:, 3, 1:8].unsqueeze(1).to_broadcast([P, SLOTS, 7]), ALU.is_ge))
            link(nc.vector.reduce_sum(slot_e[:], c17, AXX))
            nc.vector.tensor_copy(slot_i[:], slot_e[:]).then_inc(rows_ready, 1)
            dve.wait_ge(lexp_ready, 1)
            link(nc.vector.reduce_sum(rv[:, 3], rt[:, 0], AXX))
            link(nc.vector.reciprocal(rv[:, 4], rv[:, 3]))
            link(nc.vector.tensor_tensor(rt[:, 0], rt[:, 0], rv[:, 4].unsqueeze(2).to_broadcast([P, TT, NE]), ALU.mult))
            for c in range(2):
                link(nc.vector.tensor_tensor(rt[:, 6], rt[:, 2 + c], rt[:, 0], ALU.mult))
                link(nc.vector.reduce_sum(rv[:, 5 + c], rt[:, 6], AXX))
            link(nc.vector.tensor_tensor(rv[:, 7], rv[:, 5], rv[:, 6], ALU.add))
            link(nc.vector.reciprocal(rv[:, 8], rv[:, 7]))
            for c in range(2):
                link(nc.vector.tensor_tensor(rv[:, 9 + c], rv[:, 5 + c], rv[:, 8], ALU.mult))

            nc.vector.drain().then_inc(eact_ready, G_EACT)
            nc.vector.drain().then_inc(y_evac, 1)
            with dve.Fori(0, SLOTS) as s:
                for c in range(4):
                    bank, c0 = (2 * c + 1) % 4, sum(FCH[:c])
                    dve.wait_ge(up_done, 4 * s + c + 1)
                    dve.wait_ge(esilu_ready, 4 * s + c + 1)
                    dve.wait_ge(etr_done, 2 + 6 * s + TR_OF[c] + 1)
                    nc.vector.tensor_tensor(eact[:, c0:c0 + FCH[c]], esil[:, c % 2, 0:FCH[c]],
                                            ps[:, 512 * bank:512 * bank + FCH[c]], ALU.mult).then_inc(eact_ready, 1)
                dve.wait_ge(y_done, s + 2)
                dve.wait_ge(y_left, s + 1)
                nc.vector.tensor_copy(ybuf, ps[:, 3072:4096]).then_inc(y_evac, 1)

            for t in range(TT):
                dve.wait_ge(gathered[t % 2], 32 * (t // 2 + 1))
                y1, y2 = picked[:, t % 2, 0, :], picked[:, t % 2, 1, :]
                link(nc.vector.tensor_scalar(y2, y2, rv[:, 10, t:t + 1], None, ALU.mult))
                nc.vector.scalar_tensor_tensor(y1, y1, rv[:, 9, t:t + 1], y2, ALU.mult, ALU.add).then_inc(comb_ready, 1)
                m = MAIN[("comb", t)]
                dve.wait_ge(main_done, m + 1)
                g = 0 if t < TT - 1 else 1
                for k in range(KC):
                    ins = nc.vector.scalar_tensor_tensor(
                        x_t[:, k, t * P:(t + 1) * P], ps[:, 1024 * (m % 3) + k * P:1024 * (m % 3) + (k + 1) * P],
                        mod[:, 1, 40 + k, g:g + 1], x_t[:, k, t * P:(t + 1) * P], ALU.mult, ALU.add)
                ins.then_inc(x_upd, 1)
            dve.wait_ge(x_upd, 24 + TT)
            norm(4, DEPTH, 4 * DEPTH + 1, ("norm", DEPTH, "fin"))

        @block.tensor
        def _(pe):
            LAT, PRM = slice(0, N_LAT), slice(N_LAT, T)

            def claim_main(label):
                m = MAIN[label]
                if m >= 3:
                    name, val = MAIN_FREED[m - 3]
                    pe.wait_ge(sems[name], val)
                return main_pair(label)

            def claim_aux(label):
                n = AUX[label]
                if n >= 1:
                    name, val = AUX_FREED[n - 1]
                    pe.wait_ge(sems[name], val)
                return AUXP

            def arrived(p):
                n = PIECE_AT[p]
                pe.wait_ge(w_in_ring[n % RING], 16 * (n // RING + 1))
                return ring[:, n % RING, :]

            def both(out, lhs, rhs, start, stop):
                nc.tensor.matmul(out[:, LAT], lhs, rhs[:, LAT], start=start, stop=stop)
                return nc.tensor.matmul(out[:, PRM], lhs, rhs[:, PRM], start=start, stop=stop)

            def sum_square(l, kind, k, first, last):
                n = sq_at(l, kind, k)
                pe.wait_ge(sq_ready, n + 1)
                return both(AUXP, ones[:], sq[:, n % 2, :], first, last)

            pe.wait_ge(lam_prod_ready, 1)
            pe.wait_ge(zeroed, 2)
            lam_ps = claim_main(("lam",))
            nc.tensor.matmul(lam_ps[:, 0:4], ones[0:HD, :], lam_prod[:].rearrange("p l m -> p (l m)"),
                             start=True, stop=True).then_inc(main_done, 1)
            pe.wait_ge(cond_ready, 1)

            def ada(l, c, out):
                w = arrived(("ada", l, c))[:, 0:KC * 256].rearrange("p (k n) -> p k n", k=KC)
                for k in range(KC):
                    ins = nc.tensor.matmul(out, cond[:, k, :], w[:, k, :], start=k == 0, stop=k == KC - 1)
                return ins.then_inc(w_used, 1)

            def ada_turn(row, out, n):
                for j in range(n):
                    ins = nc.tensor.matmul(out[:, 2 * j:2 * j + 2], row[:, j * P:(j + 1) * P], ident[0:2, 0:2],
                                           start=True, stop=True)
                return ins

            for n in range(2):
                claim_main(("ada0", n))
                o = 1024 * (MAIN[("ada0", n)] % 3)
                for c in range(4):
                    ada(0, 4 * n + c, ps[0:2, o + 256 * c:o + 256 * c + 256])
                pe.drain().then_inc(main_done, 1)
            claim_main(("ada0t",))
            pe.wait_ge(ada_rows, 2)
            pe.wait_ge(const_in, 160)
            ada_turn(ada_row0, main_pair(("ada0t",)), 16).then_inc(main_done, 1)

            for l in range(DEPTH):
                if l == 0:
                    claim_aux(("norm", 0, "mix"))
                    for k in range(KC):
                        ins = sum_square(0, "mix", k, k == 0, k == KC - 1)
                        ins.then_inc(sq_used, 1)
                    pe.wait_ge(sq_used, 8)
                    pe.drain().then_inc(aux_done, 1)

                def project(label, w, c0, width, h_first=False):
                    out = claim_main(label)
                    for k in range(KC):
                        if h_first:
                            pe.wait_ge(h_ready, 16 * l + k + 1)
                        ins = both(out[0:width], w[:, k, c0:c0 + width], h_t[:, k, :], k == 0, k == KC - 1)
                    return ins

                def wpiece(c, n):
                    return arrived(("in", l, c, n))[:, 0:KC * n].rearrange("p (k n) -> p k n", k=KC)

                def done_with_piece():
                    pe.drain().then_inc(w_used, 1)

                def rot(r):
                    rows = MQK if r in (0, 9, 10, 11, 12) else P
                    sw = swap_m if rows == MQK else swap_d
                    n = 13 * l + r
                    claim_aux(("rot", l, r))
                    pe.wait_ge(raw_ready, n + 1)
                    nc.tensor.matmul(AUXP[0:rows, LAT], sw[:], raw[0:rows, n % 2, LAT], start=True, stop=True).then_inc(aux_done, 1)

                w = wpiece(1792, 128)
                project(("lora", l, 0), w, 0, P, True).then_inc(main_done, 1)
                done_with_piece()
                w = wpiece(1536, 256)
                project(("lora", l, 1), w, 0, P).then_inc(main_done, 1)
                project(("lora", l, 2), w, P, P).then_inc(main_done, 1)
                done_with_piece()
                pe.wait_ge(layer_w_in, 16 * N_LAYER_W * (l + 1))
                project(("rope", l, 0), wkr, 0, MQK).then_inc(main_done, 1)
                claim_aux(("norm", l, "ckv"))
                sum_square(l, "lora", 0, True, True).then_inc(sq_used, 1)
                pe.drain().then_inc(aux_done, 1)
                w = wpiece(512, 256)
                project(("rope", l, 1), w, 0, P).then_inc(main_done, 1)
                claim_aux(("norm", l, "cq"))
                for g in (1, 2):
                    sum_square(l, "lora", g, g == 1, g == 2).then_inc(sq_used, 1)
                pe.drain().then_inc(aux_done, 1)
                if l == 0:
                    pe.wait_ge(const_in, 160)
                project(("rope", l, 2), w, P, P).then_inc(main_done, 1)
                done_with_piece()
                rot(0)
                for r in range(3, 9):
                    c0 = ((r - 1) % 2) * P
                    if c0 == 0:
                        w = wpiece({3: 768, 5: 0, 7: 256}[r], 256)
                    project(("rope", l, r), w, c0, P).then_inc(main_done, 1)
                    if c0:
                        done_with_piece()
                    rot(r - 2)
                for v in range(10):
                    half, t = v // TT, v % TT
                    if t == 0:
                        w = wpiece(1024 + 256 * half, 256)
                    out = claim_main(("vd", l, v))
                    for k in range(KC):
                        ins = nc.tensor.matmul(out[:, 0:256], h_t[:, k, t * P:(t + 1) * P], w[:, k, :],
                                               start=k == 0, stop=k == KC - 1)
                    ins.then_inc(main_done, 1)
                    if t == TT - 1:
                        done_with_piece()
                    if v == 0:
                        rot(7)
                    if v == 1:
                        rot(8)

                def attention(f):
                    base = (2 * l + f) * ITEMS

                    def item(i):
                        h, qt = i // TT, i % TT
                        lat = qt < TT - 1
                        return base + i, (base + i) % 2, h, qt, lat

                    def scores(i):
                        it, b, h, qt, lat = item(i)
                        if it >= 2:
                            pe.wait_ge(exp_done, it - 1)
                        if i >= 2 and (i - 2) % TT == TT - 1:
                            pe.wait_ge(late_rows, 8 * l + 4 * f + (i - 2) // TT + 1)
                        o = 1536 * b
                        rows = [(0, HD), (HD, P)] if f == 0 else [(0, MQK)]
                        for m, (r0, r1) in enumerate(rows):
                            q = q_t[r0:r1, h, qt * P:(qt + 1) * P]
                            if lat:
                                parts = ((512, 768), (0, 512)) if m == 0 else ((256, 768), (0, 256))
                                for n, (a, z) in enumerate(parts):
                                    if m == 1 and n == 1:
                                        pe.wait_ge(mid_bank, (4 * l + h) * (TT - 1) + qt + 1)
                                    ins = nc.tensor.matmul(ps[:, o + 768 * m + a:o + 768 * m + z], q, k_t[r0:r1, h, a:z],
                                                           start=True, stop=True)
                                    if f == 0 and m == 0 and n == 0:
                                        ins.then_inc(mid_bank, 1)
                            else:
                                ins = nc.tensor.matmul(ps[:, o + 768 * m:o + 768 * m + P], q, k_t[r0:r1, h, LAT_KEYS:NKEY],
                                                       start=True, stop=True)
                        ins.then_inc(scores_done, 1)

                    def turn(h):
                        u = 4 * f + h
                        pe.wait_ge(late_rows, 8 * l + u + 1)
                        ada_turn(ada_row, ps[:, 3968:4096], 2 * len(ada_after_head(l, u))).then_inc(ada_done, 1)

                    def transposes(i):
                        it, b, h, qt, lat = item(i)
                        pe.wait_ge(p_ready, it + 1)
                        if it:
                            pe.wait_ge(pt_a_ready, it)
                        for k in range(4 if lat else 1):
                            ins = nc.tensor.matmul(ps[:, 3072 + k * P:3072 + (k + 1) * P], e_buf[:, b, 0, k * P:(k + 1) * P], diag[:, b, :],
                                                   start=True, stop=True)
                        ins.then_inc(tr_a_done, 1)
                        if it:
                            pe.wait_ge(pv_evac, it)
                        if qt == TT - 1:
                            for n, (ll, c) in enumerate(ada_after_head(l, 4 * f + h)):
                                ada(ll, c, ps[0:2, 1536 * b + 512 * n:1536 * b + 512 * n + 256])
                            pe.drain().then_inc(late_rows_done, 1)
                        if qt == 0 and h:
                            turn(h - 1)
                        if lat:
                            if qt == 0 and h:
                                pe.wait_ge(mod_late, 8 * l + 4 * f + h)
                            for k in range(4, 6):
                                ins = nc.tensor.matmul(ps[:, 3584 + (k - 4) * P:3584 + (k - 3) * P], e_buf[:, b, 0, k * P:(k + 1) * P],
                                                       diag[:, b, :], start=True, stop=True)
                            ins.then_inc(tr_b_done, 1)

                    def values(i):
                        it, b, h, qt, lat = item(i)
                        pe.wait_ge(pt_a_ready, it + 1)
                        if lat:
                            pe.wait_ge(pt_b_ready, n_tr_b(it))
                        if it:
                            pe.wait_ge(pv_evac, it)
                        kts = range(6) if lat else (KT - 1,)
                        for n, kt in enumerate(kts):
                            ins = nc.tensor.matmul(ps[:, 3840:3968], v_n[:, kt, h * P:(h + 1) * P], pt_buf[:, b, n, :],
                                                   start=n == 0, stop=n == len(kts) - 1)
                        ins.then_inc(pv_done, 1)

                    scores(0)
                    for i in range(ITEMS):
                        if i + 1 < ITEMS:
                            scores(i + 1)
                        if i:
                            values(i - 1)
                        transposes(i)
                    values(ITEMS - 1)
                    pe.wait_ge(pv_evac, base + ITEMS)
                    turn(HEADS - 1)
                    pe.wait_ge(mod_late, 8 * l + 4 * f + HEADS)

                pe.wait_ge(rope_done, 13 * l + 9)
                pe.wait_ge(vd_ready, 10 * l + 10)
                pe.wait_ge(cache_k_in, 16 * (l + 1))
                pe.wait_ge(cache_v_in, 16 * (l + 1))
                pe.wait_ge(rot_used, 13 * l + 9)
                attention(0)

                pe.wait_ge(pv_evac, (2 * l + 1) * ITEMS)
                pe.wait_ge(exp_done, (2 * l + 1) * ITEMS)
                for h in range(HEADS):
                    claim_aux(("norm", l, "head", h))
                    sum_square(l, "head", h, True, True).then_inc(sq_used, 1)
                    pe.drain().then_inc(aux_done, 1)
                    out = claim_main(("rope", l, 9 + h))
                    pe.wait_ge(lat_normed, 2 * l + 2)
                    for k in range(2):
                        ins = both(out[0:MQK], wuq[:, k, h * MQK:(h + 1) * MQK], cq_t[:, k, :], k == 0, k == 1)
                    ins.then_inc(main_done, 1)
                    if h:
                        rot(8 + h)
                rot(12)
                pe.wait_ge(cache_c_in, 16 * N_CACHE_C * (l + 1))
                for h in range(HEADS):
                    claim_main(("uk", l, h))
                    o = 1024 * (MAIN[("uk", l, h)] % 3)
                    for c in range(2):
                        ins = nc.tensor.matmul(ps[0:NOPE, o + 512 * c:o + 512 * c + 448], wuk[:, h * NOPE:(h + 1) * NOPE],
                                               ckv_t[:, 448 * c:448 * c + 448], start=True, stop=True)
                    ins.then_inc(main_done, 1)
                for v in range(KT):
                    o = 1024 * (MAIN[("uv", l, v)] % 3)
                    claim_main(("uv", l, v))
                    nc.tensor.matmul(ps[:, o:o + 512], ckv_t[:, v * P:(v + 1) * P], wuv, start=True, stop=True).then_inc(main_done, 1)
                pe.wait_ge(rope_done, 13 * l + 13)
                pe.wait_ge(vm_ready, KT * (l + 1))
                pe.wait_ge(km_ready, 4 * (l + 1))
                pe.wait_ge(kr_spread, 4 * (l + 1))
                attention(1)

                pe.wait_ge(pv_evac, (2 * l + 2) * ITEMS)
                pe.wait_ge(exp_done, (2 * l + 2) * ITEMS)
                pe.wait_ge(heads_normed, 4 * (l + 1))
                claim_aux(("norm", l, "ffn"))
                for d_ in range(KC):
                    if d_ % 2 == 0:
                        w = arrived(("o", l, d_ // 2))[:, 0:KC * 256].rearrange("p (k n) -> p k n", k=KC)
                    out = claim_main(("o", l, d_))
                    for k in range(KC):
                        ins = both(out, w[:, k, (d_ % 2) * P:(d_ % 2) * P + P], mixed[:, k, :], k == 0, k == KC - 1)
                    ins.then_inc(main_done, 1)
                    if d_ % 2:
                        done_with_piece()
                    if d_ >= 2:
                        sum_square(l, "ffn", d_ - 2, d_ == 2, False).then_inc(sq_used, 1)
                for d_ in (KC - 2, KC - 1):
                    sum_square(l, "ffn", d_, False, d_ == KC - 1).then_inc(sq_used, 1)
                pe.drain().then_inc(aux_done, 1)

                if l == 0:
                    for j in range(FC):
                        if j % 2 == 0:
                            wg = arrived(("gate", j // 2))[:, 0:KC * 256].rearrange("p (k n) -> p k n", k=KC)
                        out = claim_main(("gate", j))
                        for k in range(KC):
                            if j == 0:
                                pe.wait_ge(h_ready, 8 + k + 1)
                            ins = both(out, wg[:, k, (j % 2) * P:(j % 2) * P + P], h_t[:, k, :], k == 0, k == KC - 1)
                        ins.then_inc(main_done, 1)
                        if j % 2:
                            done_with_piece()
                        if j % 2 == 0:
                            wu = arrived(("up", j // 2))[:, 0:KC * 256].rearrange("p (k n) -> p k n", k=KC)
                        out = claim_main(("up", j))
                        for k in range(KC):
                            ins = both(out, wu[:, k, (j % 2) * P:(j % 2) * P + P], h_t[:, k, :], k == 0, k == KC - 1)
                        ins.then_inc(main_done, 1)
                        if j % 2:
                            done_with_piece()
                    claim_aux(("norm", 1, "mix"))
                    pe.wait_ge(hid_ready, FC)
                    for d_ in range(KC):
                        out = claim_main(("down", d_))
                        for half in range(2):
                            w = arrived(("down", d_, half))[:, 0:FCE * P].rearrange("p (k n) -> p k n", k=FCE)
                            for k in range(FCE):
                                kk = half * FCE + k
                                ins = both(out, w[:, k, :], hid[:, kk, :], kk == 0, kk == FC - 1)
                            if half == 0:
                                ins.then_inc(w_used, 1)
                        ins.then_inc(main_done, 1)
                        done_with_piece()
                        if d_ >= 2:
                            sum_square(1, "mix", d_ - 2, d_ == 2, False).then_inc(sq_used, 1)
                    for d_ in (KC - 2, KC - 1):
                        sum_square(1, "mix", d_, False, d_ == KC - 1).then_inc(sq_used, 1)
                    pe.drain().then_inc(aux_done, 1)

            claim_aux(("router",))
            for k in range(KC):
                pe.wait_ge(h_ready, 24 + k + 1)
            for t in range(TT):
                for k in range(KC):
                    ins = nc.tensor.matmul(AUXP[:, t * NE:(t + 1) * NE], h_t[:, k, t * P:(t + 1) * P], router_w[:, k, :],
                                           start=k == 0, stop=k == KC - 1)
            ins.then_inc(aux_done, 1)

            def htok_rows(t):
                claim_main(("htok", t))
                o = 1024 * (MAIN[("htok", t)] % 3)
                for k in range(KC):
                    ins = nc.tensor.transpose(ps[:, o + k * P:o + (k + 1) * P], h_t[:, k, t * P:(t + 1) * P], ident[:])
                ins.then_inc(main_done, 1)

            for t in range(3):
                htok_rows(t)
            claim_aux(("rank",))
            pe.wait_ge(sel_ready, 1)
            for t in range(TT):
                for tt in range(t):
                    nc.tensor.matmul(AUXP[:, t * NE:(t + 1) * NE], ones[:], rt[:, 4, tt, :], start=tt == 0, stop=False)
                nc.tensor.matmul(AUXP[:, t * NE:(t + 1) * NE], before[:], rt[:, 4, t, :], start=t == 0, stop=True)
            for t in range(TT):
                ins = nc.tensor.matmul(AUXP[:, TT * NE:TT * NE + NE], ones[:], rt[:, 4, t, :], start=t == 0, stop=t == TT - 1)
            ins.then_inc(aux_done, 1)
            for t in range(3, TT):
                htok_rows(t)

            pe.wait_ge(htok_ready, TT)
            pe.wait_ge(rank_ready, 1)

            def x_transposes(half):
                bank = 4 + (TR_OF["xa"] + half) % 2
                for k in range(4):
                    ins = nc.tensor.transpose(ps[:, 512 * bank + k * P:512 * bank + (k + 1) * P],
                                              xs[:, (4 * half + k) * P:(4 * half + k + 1) * P], ident[:])
                return ins

            pe.drain().then_inc(m_free, MRING)
            pe.wait_ge(xs_in, 16)
            for half in range(2):
                x_transposes(half).then_inc(etr_done, 1)
            pe.drain().then_inc(etr_done, G_ETR)
            pe.drain().then_inc(y_done, 1)
            with pe.Fori(0, SLOTS) as s:
                def tr(c):
                    j = TR_OF[c]
                    bank = 4 + j % 2
                    pe.wait_ge(etr_evac, 6 * s + j + 1)
                    if c == "xa":
                        pe.wait_ge(xs_in, 16 * (s + 2))
                    if c in ("xa", "xb"):
                        x_transposes(j - TR_OF["xa"]).then_inc(etr_done, 1)
                        return
                    pe.wait_ge(eact_ready, G_EACT + 4 * s + c + 1)
                    c0 = sum(FCH[:c])
                    for k in range(FCH[c] // P):
                        ins = nc.tensor.transpose(ps[:, 512 * bank + k * P:512 * bank + (k + 1) * P],
                                                  eact[:, c0 + k * P:c0 + (k + 1) * P], ident[:])
                    ins.then_inc(etr_done, 1)

                def gate_up(c):
                    pe.wait_ge(eact_ready, 4 * s + c + 1)
                    if c == 0:
                        pe.wait_ge(etr_evac, 6 * s + 2)
                    for u in range(2):
                        n = 2 * c + u
                        w = mring[:, n % MRING, 0:KC * FCH[c]].rearrange("p (k n) -> p k n", k=KC)
                        pe.wait_ge(m_arrived[n % MRING], 16 * (2 * s + n // MRING + 1))
                        bank = (2 * c + u) % 4
                        for k in range(KC):
                            ins = nc.tensor.matmul(ps[:, 512 * bank:512 * bank + FCH[c]], xs_t[:, k, :], w[:, k, :],
                                                   start=k == 0, stop=k == KC - 1)
                        ins.then_inc(gate_done if u == 0 else up_done, 1)
                        pe.drain().then_inc(m_free, 1)

                gate_up(0)
                gate_up(1)
                tr(0)
                gate_up(2)
                tr(1)
                gate_up(3)
                tr(2)
                tr("xa")
                tr("xb")
                tr(3)
                pe.wait_ge(y_evac, s + 1)
                for n in range(8, 12):
                    c = n - 8
                    kn = FCH[c] // P
                    w = mring[:, n % MRING, 0:kn * D_MODEL].rearrange("p (k n) -> p k n", k=kn)
                    pe.wait_ge(m_arrived[n % MRING], 16 * (2 * s + n // MRING + 1))
                    pe.wait_ge(etr_evac, 2 + 6 * s + TR_OF[c] + 1)
                    for k in range(kn):
                        for u in range(2):
                            ins = nc.tensor.matmul(ps[:, 3072 + 512 * u:3584 + 512 * u], eact_t[:, 3 * c + k, :],
                                                   w[:, k, 512 * u:512 * u + 512],
                                                   start=n == 8 and k == 0, stop=n == 11 and k == kn - 1)
                    ins.then_inc(m_free, 1)
                pe.drain().then_inc(y_done, 1)

            pe.wait_ge(y_evac, SLOTS + 1)
            for t in range(TT):
                claim_main(("comb", t))
                o = 1024 * (MAIN[("comb", t)] % 3)
                pe.wait_ge(comb_ready, t + 1)
                for k in range(KC):
                    ins = nc.tensor.transpose(ps[:, o + k * P:o + (k + 1) * P], picked[:, t % 2, 0, k * P:(k + 1) * P], ident[:])
                ins.then_inc(main_done, 1)
            claim_aux(("norm", DEPTH, "fin"))
            for k in range(KC):
                sum_square(DEPTH, "fin", k, k == 0, k == KC - 1).then_inc(sq_used, 1)
            pe.drain().then_inc(aux_done, 1)


def constants():
    t = np.arange(N_LAT)
    rows, cols = (t // GRID_W).astype(np.float32), (t % GRID_W).astype(np.float32)

    def axial(width):
        half = width // 4
        freqs = np.float32(THETA) ** (-np.arange(half, dtype=np.float32) / np.float32(half))
        cos, sin, partner = [], [], []
        for block, pos in enumerate((rows, cols)):
            for side in range(2):
                for j in range(half):
                    ang = pos * freqs[j]
                    cos.append(np.cos(ang))
                    sin.append(np.sin(ang) * (-1.0, 1.0)[side])
                    partner.append(block * 2 * half + (1 - side) * half + j)
        return np.array(cos, np.float32), np.array(sin, np.float32), partner

    def swap(partner):
        m = np.zeros((len(partner),) * 2, np.float32)
        m[partner, np.arange(len(partner))] = 1.0
        return m

    c, s, p = axial(HD)
    out = {"cos_d": np.concatenate([c, c]), "sin_d": np.concatenate([s, s]),
           "swap_d": swap(p + [HD + i for i in p])}
    c, s, p = axial(ROPE)
    out["cos_m"] = np.concatenate([np.ones((NOPE, N_LAT), np.float32), c])
    out["sin_m"] = np.concatenate([np.zeros((NOPE, N_LAT), np.float32), s])
    out["swap_m"] = swap(list(range(NOPE)) + [NOPE + i for i in p])
    out["ident"] = np.eye(P, dtype=np.float32)
    out["before"] = np.triu(np.ones((P, P), np.float32), 1)
    small = np.concatenate([np.tril(np.ones((NE, NE)), -1).ravel(), np.arange(TT) * P, np.arange(SLOTS) * P])
    out["small"] = np.broadcast_to(small.astype(np.float32), (P, small.size)).copy()
    return out


_WEIGHTS = ["w_ada", "w_in", "w_uq", "w_uk", "w_uv", "w_o", "w_gate", "w_up", "w_down", "router",
            "moe_w_gate", "moe_w_up", "moe_w_down"]
_OUTS = {"y_t": (P, KC, T), "new_k": (DEPTH, P, HEADS, N_PROMPT), "new_v": (DEPTH, N_PROMPT, HEADS * P),
         "new_ckv": (DEPTH, P, N_PROMPT), "new_kr": (DEPTH, ROPE, N_PROMPT)}


def layout(x):
    def col(a):
        return np.ascontiguousarray(a.reshape(-1, P).T)

    a = {n: x[n] for n in _WEIGHTS}
    tokens = np.concatenate([x["x_sample"][0], x["x_prompt"][0]], axis=0)
    a["x_t"] = tokens.T.reshape(KC, P, T).transpose(1, 0, 2)
    a["cond"] = np.stack([col(x["c"][0]), col(x["c_ctx"])], axis=2)
    a["vecs"] = np.concatenate([col(x[n].reshape(-1)) for n in
                                ("b_ada", "norm_mix_g", "norm_ffn_g", "final_norm_g", "mla_q_norm_g",
                                 "mla_kv_norm_g", "diff_subln_g")], axis=1)
    lam = np.stack([np.stack([x["diff_lq1"], x["diff_lk1"]], -1), np.stack([x["diff_lq2"], x["diff_lk2"]], -1)], 2)
    a["lam"] = lam.transpose(1, 0, 2, 3)
    a["cache_k"] = x["cache_diff_k"][0].transpose(0, 3, 2, 1)
    v = x["cache_diff_v"][0].reshape(DEPTH, PAST // P, P, HEADS * P)
    a["cache_v"] = v.transpose(0, 2, 1, 3)
    a["cache_ckv"] = x["cache_mla_ckv"][0].transpose(0, 2, 1)
    a["cache_kr"] = x["cache_mla_krope"][0].transpose(0, 2, 1)
    return a


def kernel(**inputs):
    import concourse.bacc as _bacc
    from concourse.bass_utils import run_bass_kernel_spmd as _run

    nc = _bacc.Bacc("TRN2", target_bir_lowering=False, num_devices=1)
    arrays = {}
    aps = {}
    laid = layout({n: np.asarray(v) for n, v in inputs.items()})
    for name, a in {**laid, **constants()}.items():
        a = np.ascontiguousarray(a)
        arrays[f"in_{name}"] = a
        aps[name] = nc.dram_tensor(f"in_{name}", a.shape, mybir.dt.from_np(a.dtype), kind="ExternalInput").ap()
    for name, shape in _OUTS.items():
        aps[name] = nc.dram_tensor(f"out_{name}", shape, mybir.dt.float32, kind="ExternalOutput").ap()
    build(nc, aps)
    r = _run(nc, [arrays], core_ids=[0]).results[0]
    y = np.asarray(r["out_y_t"]).transpose(2, 1, 0).reshape(T, D_MODEL)
    new_k = np.asarray(r["out_new_k"]).transpose(0, 3, 2, 1)[None]
    new_v = np.asarray(r["out_new_v"]).reshape(1, DEPTH, N_PROMPT, HEADS, P)
    new_ckv = np.asarray(r["out_new_ckv"]).transpose(0, 2, 1)[None]
    new_kr = np.asarray(r["out_new_kr"]).transpose(0, 2, 1)[None]
    return (np.ascontiguousarray(y[N_LAT:])[None], np.ascontiguousarray(y[:N_LAT])[None],
            np.ascontiguousarray(new_k), np.ascontiguousarray(new_v), np.ascontiguousarray(new_ckv),
            np.ascontiguousarray(new_kr))
```

```python
import math
from contextlib import ExitStack

import numpy as np

import concourse.bass as bass
from concourse import mybir

P = 128
D_MODEL, KC = 1024, 8
N_LAT, N_PROMPT = 512, 128
T = N_LAT + N_PROMPT
TT = T // P
PAST = 256
NKEY = PAST + T
KT = NKEY // P
LAT_KEYS = PAST + N_LAT
DEPTH = 2
HEADS, HD = 4, 64
QL, KVL, ROPE, NOPE = 256, 128, 32, 64
MQK = NOPE + ROPE
D_FF, FC = 2816, 22
NE, D_FFE, FCE = 8, 1408, 11
SLOTS = 17
XTILES = SLOTS + 2
GRID_W, THETA, EPS = 64, 10000.0, 1e-6
D_SCALE, M_SCALE = HD ** -0.5, MQK ** -0.5
ITEMS = HEADS * TT

V_BADA, V_MIX, V_FFN, V_FIN, V_QN, V_KVN, V_SUB = 0, 96, 112, 128, 136, 140, 142
NV = 144

RING, RING_F = 3, 2048
SUBS_KEPT, SUB_F = 2, 1024
TH = T // 2
FF_HALF = (range(0, 12), range(12, FC))
MRING, PIECE_F = 4, 2816
SPLITS = 3
NPC, NGU, HCH, DCH = 12, 8, 352, 256
BLK = [(0, 2), (2, 5), (5, 8), (8, 11)]


def lam_init(l):
    return 0.8 - 0.6 * math.exp(-0.3 * l)


def weight_pieces():
    out = []
    for c in range(8):
        out.append(("ada", 0, c))
    rest = [("ada", 0, c) for c in range(8, 24)] + [("ada", 1, c) for c in range(8)]
    late = [("ada", 1, c) for c in range(8, 24)]
    for l in range(DEPTH):
        out += [("in", l, 1792, 128), ("in", l, 1536, 256)]
        out += [("in", l, c, 256) for c in (512, 768, 0, 256, 1024, 1280)]
        for u in range(8):
            out += rest[3 * u:3 * u + 3] if l == 0 else late[2 * u:2 * u + 2]
        out += [("o", l, c) for c in range(4)]
        if l == 0:
            for half, js in enumerate(FF_HALF):
                for j in js[::2]:
                    out += [("gate", j // 2), ("up", j // 2)]
                out += [("down", half, d) for d in range(KC)]
    return out


PIECES = weight_pieces()
PIECE_AT = {p: n for n, p in enumerate(PIECES)}


def ada_after_head(l, u):
    if l == 0:
        a = [(0, c) for c in range(8, 24)] + [(1, c) for c in range(8)]
        return a[3 * u:3 * u + 3]
    return [(1, c) for c in range(8 + 2 * u, 10 + 2 * u)]


SQ_LAYER = [("mix", k) for k in range(8)] + [("lora", k) for k in range(3)] \
    + [("head", k) for k in range(4)] + [("ffn", k) for k in range(8)]


def sq_at(l, kind, k):
    if l == DEPTH:
        return DEPTH * len(SQ_LAYER) + k
    return l * len(SQ_LAYER) + SQ_LAYER.index((kind, k))


def plan():
    main, aux = {}, {}
    main_freed, aux_freed = [], []

    def m(label, sem, val):
        main[label] = len(main_freed)
        main_freed.append((sem, val))

    def x(label, sem, val):
        aux[label] = len(aux_freed)
        aux_freed.append((sem, val))

    m(("lam",), "lam_exp", 1)
    m(("ada0", 0), "ada_rows", 1)
    m(("ada0", 1), "ada_rows", 2)
    m(("ada0t",), "mod_ready", 1)
    for l in range(DEPTH):
        x(("norm", l, "mix"), "var_ready", 4 * l + 1)
        for g in range(3):
            m(("lora", l, g), "lora_ready", 3 * l + g + 1)
        for r in range(9):
            m(("rope", l, r), "raw_ready", 13 * l + r + 1)
        x(("norm", l, "ckv"), "var_ready", 4 * l + 2)
        x(("norm", l, "cq"), "var_ready", 4 * l + 3)
        for r in range(9):
            x(("rot", l, r), "rot_used", 13 * l + r + 1)
        for v in range(10):
            m(("vd", l, v), "vd_ready", 10 * l + v + 1)
        for h in range(4):
            x(("norm", l, "head", h), "hvar_ready", 4 * l + h + 1)
            if h:
                x(("rot", l, 8 + h), "rot_used", 13 * l + 9 + h)
        x(("rot", l, 12), "rot_used", 13 * l + 13)
        for r in range(9, 13):
            m(("rope", l, r), "raw_ready", 13 * l + r + 1)
        for h in range(4):
            m(("uk", l, h), "km_ready", 4 * l + h + 1)
        for v in range(KT):
            m(("uv", l, v), "vm_ready", KT * l + v + 1)
        for d in range(KC):
            m(("o", l, d), "x_upd", (24 if l else 0) + d + 1)
        x(("norm", l, "ffn"), "var_ready", 4 * l + 4)
        if l == 0:
            for half, js in enumerate(FF_HALF):
                for j in js:
                    m(("gate", j), "silu_ready", j + 1)
                    m(("up", j), "hid_product", j + 1)
                for d in range(KC):
                    m(("down", half, d), "x_upd", 8 + 8 * half + d + 1)
        else:
            x(("router",), "lg_ready", 1)
            for t in range(TT):
                m(("htok", t), "htok_ready", t + 1)
            x(("rank",), "rank_ready", 1)
            for t in range(TT):
                m(("comb", t), "x_upd", 32 + t + 1)
    x(("norm", DEPTH, "fin"), "var_ready", 4 * DEPTH + 1)
    return main, aux, main_freed, aux_freed


MAIN, AUX, MAIN_FREED, AUX_FREED = plan()


def sub_pieces():
    subs, labels = [], []
    n_first = 0

    def add(label, piece, ks, cs, group, sem="main_done"):
        labels.append(label)
        subs.append((piece, ks, cs, (sem, MAIN[group] + 1 if sem == "main_done" else group)))

    for l in range(DEPTH):
        add(("lora", l, 0), ("in", l, 1792, 128), (0, KC), (0, P), ("lora", l, 0))
        for g in (1, 2):
            add(("lora", l, g), ("in", l, 1536, 256), (0, KC), ((g - 1) * P, g * P), ("lora", l, g))
        add(("rope", l, 0), None, (0, KC), (0, P), ("rope", l, 0))
        for r in range(1, 9):
            c = (512, 768, 0, 256)[(r - 1) // 2]
            o = (r - 1) % 2 * P
            add(("rope", l, r), ("in", l, c, 256), (0, KC), (o, o + P), ("rope", l, r))
        for half in range(2):
            for kh in range(2):
                add(("vd", l, half, kh), ("in", l, 1024 + 256 * half, 256), (4 * kh, 4 * kh + 4), (0, 256),
                    ("vd", l, TT * half + TT - 1))
        for d in range(KC):
            add(("o", l, d), ("o", l, d // 2), (0, KC), (d % 2 * P, d % 2 * P + P), ("o", l, d))
        if l == 0:
            for half, js in enumerate(FF_HALF):
                for j in js:
                    for u in ("gate", "up"):
                        add((u, j), (u, j // 2), (0, KC), (j % 2 * P, j % 2 * P + P), (u, j))
                kn = len(js) // 2
                for d in range(KC):
                    n_first += 1
                    add(("down", half, d, 0), ("down", half, d), (0, kn), (0, P), n_first, "down_first")
                    add(("down", half, d, 1), ("down", half, d), (kn, 2 * kn), (0, P), ("down", half, d))
    return subs, {label: n for n, label in enumerate(labels)}


SUBS, SUB_AT = sub_pieces()


def piece_freed(n):
    if PIECES[n][0] == "ada":
        return "w_used", sum(p[0] == "ada" for p in PIECES[:n + 1])
    return "t_split", max(q for q, sub in enumerate(SUBS) if sub[0] == PIECES[n]) + 1


def n_tr_b(it):
    n = it + 1
    return (n // TT) * (TT - 1) + min(n % TT, TT - 1)


def build(nc, d):
    f32, i32, u32 = mybir.dt.float32, mybir.dt.int32, mybir.dt.uint32
    ACT, ALU, AXX = mybir.ActivationFunctionType, mybir.AluOpType, mybir.AxisListType.X

    xperm = nc.dram_tensor("xperm", (XTILES * P, D_MODEL), f32).ap()
    yslots = nc.dram_tensor("yslots", (SLOTS * P, D_MODEL), f32).ap()

    w_ada = d["w_ada"].rearrange("l (k p) n -> l p k n", p=P)
    w_in = d["w_in"].rearrange("l (k p) n -> l p k n", p=P)
    w_o = d["w_o"].rearrange("l (k p) n -> l p k n", p=P)
    w_gate = d["w_gate"].rearrange("l (k p) n -> l p k n", p=P)
    w_up = d["w_up"].rearrange("l (k p) n -> l p k n", p=P)
    w_down = d["w_down"].rearrange("l (k p) n -> l p k n", p=P)
    m_gate = d["moe_w_gate"].rearrange("m e (k p) n -> p (m e k) n", p=P)
    m_up = d["moe_w_up"].rearrange("m e (k p) n -> p (m e k) n", p=P)
    m_down = d["moe_w_down"].rearrange("m e (k p) n -> p (m e k) n", p=P)

    ctx = ExitStack()
    with ctx:
        def sb(name, shape, dt=f32):
            return ctx.enter_context(nc.sbuf_tensor(name, shape, dt))

        sems = {}

        def sem(name):
            sems[name] = ctx.enter_context(nc.semaphore(name))
            return sems[name]

        x_t = sb("x_t", [P, KC, T])
        vecs = sb("vecs", [P, NV])
        mod = sb("mod", [P, DEPTH, 48, 2])
        gain = sb("gain", [P, DEPTH, 2, KC, 2])
        cond = sb("cond", [P, KC, 2])
        lam_in = sb("lam_in", [HD, DEPTH, 2, 2])
        lam_prod = sb("lam_prod", [HD, DEPTH, 2])
        lam_e = sb("lam_e", [P, DEPTH, 2])
        neg_lam = sb("neg_lam", [P, DEPTH])
        subg = sb("subg", [P, DEPTH])
        cos_d, sin_d = sb("cos_d", [P, N_LAT]), sb("sin_d", [P, N_LAT])
        cos_m, sin_m = sb("cos_m", [MQK, N_LAT]), sb("sin_m", [MQK, N_LAT])
        swap_d, swap_m = sb("swap_d", [P, P]), sb("swap_m", [MQK, MQK])
        ident, ones, before = sb("ident", [P, P]), sb("ones", [P, P]), sb("before", [P, P])
        small = sb("small", [P, 64 + 5 + SLOTS])
        tri8 = small[:, 0:64].rearrange("p (a b) -> p a b", a=8)
        steps = small[:, 64:69]
        slot_rows = small[:, 69:69 + SLOTS]
        sq = sb("sq", [P, 2, T])
        rb = sb("rb", [P, T])
        stat = sb("stat", [P, 2, 12])
        diag = sb("diag", [P, 2, P])
        ada_row = sq[0:2].rearrange("p s n -> p (s n)")[:, 0:3 * 256]
        zeros = sb("zeros", [P, D_MODEL // 2])
        router_w = sb("router_w", [P, KC, NE])
        lg = sb("lg", [P, TT, NE])
        rt = sb("rt", [P, 8, TT, NE])
        rv = sb("rv", [P, 12, TT])
        cnt = sb("cnt", [P, 4, NE])
        rowi = sb("rowi", [P, 2, TT], u32)
        slot_e = sb("slot_e", [P, SLOTS])
        slot_i = sb("slot_i", [P, SLOTS], i32)

        SMALL_W = 2 * 384 + 256 + 512 + KC * P
        ATT = 4 * NKEY + 4 * T + 4 * NKEY + NKEY + 2 * T + NKEY + 4 * LAT_KEYS + 2 * LAT_KEYS
        AR = ATT + 2 * 512 + RING * RING_F + SMALL_W + KC * T + 2 * SUBS_KEPT * SUB_F
        HT = KC * T
        zone_at = (nc.sbuf_base + 31) // 32 * 32
        zone = sb("zone", [P, HT + AR])
        h_t = zone[:, 0:HT].rearrange("p (k n) -> p k n", k=KC)
        mixed = h_t
        arena = zone[:, HT:HT + AR]
        at = [0]

        def cut(n, pat=None, **kw):
            a = arena[:, at[0]:at[0] + n]
            at[0] += n
            return a.rearrange(pat, **kw) if pat else a

        k_t = cut(4 * NKEY, "p (h n) -> p h n", h=4)
        q_t = cut(4 * T, "p (h n) -> p h n", h=4)
        v_n = cut(4 * NKEY, "p (t n) -> p t n", t=KT)
        ckv_t = cut(NKEY)
        cq_t = cut(2 * T, "p (c n) -> p c n", c=2)
        kr_t = cut(NKEY)
        e_buf = cut(4 * LAT_KEYS, "p (s m n) -> p s m n", s=2, m=2)
        pt_buf = cut(2 * LAT_KEYS, "p (s k n) -> p s k n", s=2, k=6)
        rtmp = cut(1024, "p (s n) -> p s n", s=2)
        ring = cut(RING * RING_F, "p (s n) -> p s n", s=RING)
        wuq = cut(2 * 384, "p (k n) -> p k n", k=2)
        wuk = cut(256)
        wuv = cut(512)
        wkr = cut(KC * P, "p (k n) -> p k n", k=KC)
        h_split_at, sub_at = at[0], at[0] + KC * T
        ada_row0 = e_buf.rearrange("p s m n -> p (s m n)")[0:2, 0:2048]
        e_at = 4 * NKEY + 4 * T + 4 * NKEY + NKEY + 2 * T + NKEY
        lora_raw = arena[:, e_at:e_at + 3 * T].rearrange("p (c n) -> p c n", c=3)
        hrb = arena[:, e_at:e_at + 4 * T].rearrange("p (c n) -> p c n", c=4)
        pt_at = e_at + 4 * LAT_KEYS
        raw = arena[:, pt_at:pt_at + 2 * T].rearrange("p (s n) -> p s n", s=2)
        sil = sq
        cmp_a, cmp_b = (arena[:, sub_at + i * TT * NE * NE:sub_at + (i + 1) * TT * NE * NE].rearrange(
            "p (t a b) -> p t a b", t=TT, a=NE) for i in range(2))
        f32r = mybir.dt.float32r

        def split_at(name, shape, el):
            return nc.alloc_sbuf_tensor_at(name, shape, f32r, offset=zone_at + 4 * (HT + el))

        h_lo = split_at("h_lo", [P, KC, T], -HT)
        h_hi = split_at("h_hi", [P, KC, T], h_split_at)
        sub_hi = split_at("sub_hi", [P, SUBS_KEPT, SUB_F], sub_at)
        sub_lo = split_at("sub_lo", [P, SUBS_KEPT, SUB_F], sub_at + SUBS_KEPT * SUB_F)
        HJ = len(FF_HALF[0])
        hid_hi = split_at("hid_hi", [P, HJ, T], 0)
        hid_lo = split_at("hid_lo", [P, HJ, T], HJ * T)
        assert 2 * HJ * T <= ATT
        at[0] = 0

        def zcut(n, pat=None, **kw):
            a = zone[:, at[0]:at[0] + n]
            at[0] += n
            return a.rearrange(pat, **kw) if pat else a

        def zsplit(name, shape, dt=f32r):
            n = int(np.prod(shape[1:]))
            a = nc.alloc_sbuf_tensor_at(name, shape, dt, offset=zone_at + 4 * at[0])
            at[0] += n
            return a

        mraw = zsplit("mraw", [P, MRING, PIECE_F], f32)
        htok = zone[:, at[0]:at[0] + TT * D_MODEL].rearrange("p (t n) -> p t n", t=TT)
        w_hi = zsplit("w_hi", [P, SPLITS, PIECE_F])
        w_lo = zsplit("w_lo", [P, SPLITS, PIECE_F])
        xs_hi, xs_lo = zsplit("xs_hi", [P, KC, P]), zsplit("xs_lo", [P, KC, P])
        ea_hi, ea_lo = zsplit("ea_hi", [P, FCE, P]), zsplit("ea_lo", [P, FCE, P])
        xs = zcut(D_MODEL)
        eact = zcut(D_FFE)
        esil = zcut(2 * HCH, "p (s n) -> p s n", s=2)
        ybuf = zcut(D_MODEL)
        assert at[0] <= HT + AR
        picked = arena[:, 0:4 * D_MODEL].rearrange("p (s c n) -> p s c n", s=2, c=2)

        ps = ctx.enter_context(nc.psum_tensor("ps", [P, 8 * 512], f32))

        def pair(n):
            return ps[:, 1024 * n:1024 * n + T]

        def main_pair(label):
            return pair(MAIN[label] % 3)

        AUXP = pair(3)

        def halves(ap):
            return ap.rearrange("p (c n) -> p c n", c=2)[:, :, 0:TH]

        def main_halves(label):
            n = MAIN[label] % 3
            return halves(ps[:, 1024 * n:1024 * n + 1024])

        const_in, vec_in, x_in, cond_in = sem("const_in"), sem("vec_in"), sem("x_in"), sem("cond_in")
        w_in_ring = [sem(f"w_arrived{i}") for i in range(RING)]
        w_used = sem("w_used")
        zeroed, zero_rows = sem("zeroed"), sem("zero_rows")
        layer_w_in = sem("layer_w_in")
        cache_k_in, cache_v_in, cache_c_in = sem("cache_k_in"), sem("cache_v_in"), sem("cache_c_in")
        kr_zero = sem("kr_zero")
        main_done, aux_done = sem("main_done"), sem("aux_done")
        cond_ready, lam_exp, lam_prod_ready, mod_ready = sem("cond_ready"), sem("lam_exp"), sem("lam_prod_ready"), sem("mod_ready")
        mod_late = sem("mod_late")
        ada_rows, late_rows, late_rows_done = sem("ada_rows"), sem("late_rows"), sem("late_rows_done")
        ada_done = sem("ada_done")
        sq_ready, sq_used = sem("sq_ready"), sem("sq_used")
        var_ready, std_ready, xn_ready, h_ready = sem("var_ready"), sem("std_ready"), sem("xn_ready"), sem("h_ready")
        hvar_ready, hstd_ready, heads_normed = sem("hvar_ready"), sem("hstd_ready"), sem("heads_normed")
        lora_ready, raw_ready, rot_used, rope_part, rope_done = (sem(n) for n in ("lora_ready", "raw_ready", "rot_used", "rope_part", "rope_done"))
        lat_normed = sem("lat_normed")
        vd_ready, km_ready, vm_ready, kr_spread = sem("vd_ready"), sem("km_ready"), sem("vm_ready"), sem("kr_spread")
        scores_done, max_ready, exp_done, p_ready = (sem(n) for n in ("scores_done", "max_ready", "exp_done", "p_ready"))
        tr_a_done, tr_b_done, pt_a_ready, pt_b_ready, pv_done, pv_evac = (sem(n) for n in ("tr_a_done", "tr_b_done", "pt_a_ready", "pt_b_ready", "pv_done", "pv_evac"))
        mid_bank = sem("mid_bank")
        x_upd = sem("x_upd")
        silu_ready, hid_product, hid_hi_ready, hid_ready = (sem(n) for n in ("silu_ready", "hid_product", "hid_hi_ready", "hid_ready"))
        t_hi, t_split, down_first = sem("t_hi"), sem("t_split"), sem("down_first")
        h_hi_ready, h_split = sem("h_hi_ready"), sem("h_split")
        mixed_hi, mixed_split = sem("mixed_hi"), sem("mixed_split")
        lg_ready, lmax_ready, lexp_ready, sel_ready, rank_ready, rows_ready = (sem(n) for n in ("lg_ready", "lmax_ready", "lexp_ready", "sel_ready", "rank_ready", "rows_ready"))
        htok_ready, scattered = sem("htok_ready"), sem("scattered")
        m_arrived = [sem(f"m_arrived{i}") for i in range(MRING)]
        w_hi_ready, w_split, pc_done = sem("w_hi_ready"), sem("w_split"), sem("pc_done")
        xs_in, esilu_ready, eact_ready = sem("xs_in"), sem("esilu_ready"), sem("eact_ready")
        etr_done, ehi_ready, etr_evac, y_evac, y_stored = (sem(n) for n in ("etr_done", "ehi_ready", "etr_evac", "y_evac", "y_stored"))
        y_left = sem("y_left")
        gathered = [sem(f"gathered{i}") for i in range(2)]
        comb_ready = sem("comb_ready")
        y_out, kv_out = sem("y_out"), sem("kv_out")
        dve_step, pool_step = sem("dve_step"), sem("pool_step")

        G_EACT, G_ETR = 2, 6
        TR_OF = {0: 0, 1: 1, 2: 2, 3: 3, "xa": 4, "xb": 5}

        def pieces_done(s, n):
            return SPLITS + NPC * s + n + 1

        N_LAYER_W = 4

        def wait_named(eng, freed):
            eng.wait_ge(sems[freed[0]], freed[1])

        def sub_raw(q):
            piece, (k0, k1), (c0, c1), _ = SUBS[q]
            if piece is None:
                l = 0 if q < SUB_AT[("rope", 1, 0)] else 1
                return wkr, (layer_w_in, 16 * N_LAYER_W * (l + 1))
            n = PIECE_AT[piece]
            w = P if piece[0] == "down" else (piece[3] if piece[0] == "in" else 256)
            kk = len(FF_HALF[piece[1]]) if piece[0] == "down" else KC
            src = ring[:, n % RING, 0:kk * w].rearrange("p (k n) -> p k n", k=kk)
            return src[:, k0:k1, c0:c1], (w_in_ring[n % RING], 16 * (n // RING + 1))

        def sub_of(t, q):
            _, (k0, k1), (c0, c1), _ = SUBS[q]
            n = (k1 - k0) * (c1 - c0)
            return t[:, q % SUBS_KEPT, 0:n].rearrange("p (k n) -> p k n", k=k1 - k0)
        N_CACHE_C = 2
        block = ctx.enter_context(nc.Block())

        @block.sync
        def _(sp):
            sp.dma_start(cond[:], d["cond"]).then_inc(cond_in, 16)
            sp.dma_start(vecs[:], d["vecs"]).then_inc(vec_in, 16)
            sp.dma_start(lam_in[:], d["lam"]).then_inc(vec_in, 16)

            def piece(n):
                kind = PIECES[n]
                slot = ring[:, n % RING, :]
                if n >= RING:
                    wait_named(sp, piece_freed(n - RING))
                if kind[0] == "ada":
                    src, c, w, kk = w_ada[kind[1]], kind[2] * 256, 256, KC
                elif kind[0] == "in":
                    src, c, w, kk = w_in[kind[1]], kind[2], kind[3], KC
                elif kind[0] == "o":
                    src, c, w, kk = w_o[kind[1]], kind[2] * 256, 256, KC
                elif kind[0] in ("gate", "up"):
                    src, c, w, kk = (w_gate if kind[0] == "gate" else w_up)[0], kind[1] * 256, 256, KC
                else:
                    js = FF_HALF[kind[1]]
                    src, c, w, kk = w_down[0, :, js[0]:js[-1] + 1, :], kind[2] * P, P, len(js)
                dst = slot[:, 0:kk * w].rearrange("p (k n) -> p k n", k=kk)
                sp.dma_start(dst, src[:, :, c:c + w]).then_inc(w_in_ring[n % RING], 16)

            for n in range(2):
                piece(n)
            sp.dma_start(x_t[:], d["x_t"]).then_inc(x_in, 16)
            for dst, name in ((cos_d, "cos_d"), (sin_d, "sin_d"), (cos_m, "cos_m"), (sin_m, "sin_m"),
                              (swap_d, "swap_d"), (swap_m, "swap_m"), (ident, "ident"), (before, "before"),
                              (small, "small")):
                sp.dma_start(dst[:], d[name]).then_inc(const_in, 16)
            sp.dma_start(router_w[:], d["router"].rearrange("m (k p) n -> (m p) k n", p=P)).then_inc(const_in, 16)
            for n in range(2, len(PIECES)):
                if n == PIECE_AT[("o", 0, 0)]:
                    sp.wait_ge(zeroed, 2)
                    for t in range(XTILES):
                        for h in range(2):
                            sp.dma_start(xperm[t * P:(t + 1) * P, 512 * h:512 * h + 512], zeros[:]).then_inc(zero_rows, 16)
                piece(n)

            sp.wait_ge(rows_ready, 2)
            with sp.Fori(0, SLOTS) as s:
                e = sp.value_load(slot_i[0:1, bass.ds(s, 1)], min_val=0, max_val=NE - 1)
                for n in range(NPC):
                    sp.wait_ge(w_split, NPC * s + n + 1)
                    if n < NGU:
                        c = HCH * (n // 2)
                        src = (m_up if n % 2 else m_gate)[:, bass.ds(e * KC, KC), c:c + HCH]
                    else:
                        c = DCH * (n - NGU)
                        src = m_down[:, bass.ds(e * FCE, FCE), c:c + DCH]
                    dst = mraw[:, n % MRING, :].rearrange("p (k n) -> p k n", k=KC if n < NGU else FCE)
                    sp.dma_start(dst, src).then_inc(m_arrived[n % MRING], 16)

            sp.wait_ge(h_ready, 8 * 5)
            yt = d["y_t"]
            sp.dma_start(yt, h_t[:]).then_inc(y_out, 16)
            sp.wait_ge(y_out, 16)
            sp.wait_ge(kv_out, 16 * 4 * DEPTH)

        @block.gpsimd
        def _(pool):
            steps_done = [0]

            def link(ins):
                steps_done[0] += 1
                ins.then_inc(pool_step, 1)
                pool.wait_ge(pool_step, steps_done[0])

            nc.gpsimd.memset(ones[:], 1.0).then_inc(zeroed, 1)
            nc.gpsimd.memset(zeros[:], 0.0).then_inc(zeroed, 1)
            nc.gpsimd.memset(wkr, 0.0).then_inc(kr_zero, 1)
            pool.wait_ge(const_in, 16 * 10)

            def rope_item(l, r):
                n = 13 * l + r
                rows = MQK if r in (0, 9, 10, 11, 12) else P
                cs = cos_m if rows == MQK else cos_d
                src = raw[0:rows, n % 2, :]
                if r == 0:
                    out = kr_t[0:rows, PAST:NKEY]
                elif r <= 4:
                    out = k_t[0:rows, r - 1, PAST:NKEY]
                elif r <= 8:
                    out = q_t[0:rows, r - 5, :]
                else:
                    out = q_t[0:rows, r - 9, :]
                pool.wait_ge(raw_ready, n + 1)
                if r == 9:
                    pool.wait_ge(scores_done, (2 * l + 1) * ITEMS)
                nc.gpsimd.tensor_copy(out[:, N_LAT:T], src[:, N_LAT:T])
                link(nc.gpsimd.tensor_tensor(out[:, 0:N_LAT], src[:, 0:N_LAT], cs[0:rows, :], ALU.mult))
                pool.wait_ge(rot_used, n + 1)
                nc.gpsimd.tensor_tensor(out[:, 0:N_LAT], out[:, 0:N_LAT], rtmp[0:rows, n % 2, :],
                                        ALU.add).then_inc(rope_done, 1)

            for l in range(DEPTH):
                for r in range(9):
                    rope_item(l, r)
                for r in range(9, 13):
                    rope_item(l, r)
                pool.wait_ge(rope_done, 13 * l + 13)
                pool.wait_ge(cache_c_in, 16 * N_CACHE_C * (l + 1))
                pool.wait_ge(kv_out, 16 * 4 * (l + 1))
                for h in range(HEADS):
                    nc.gpsimd.tensor_copy(k_t[NOPE:MQK, h, :], kr_t[NOPE:MQK, :]).then_inc(kr_spread, 1)

            pool.wait_ge(rows_ready, 1)
            pool.wait_ge(zero_rows, 16 * 2 * XTILES)
            for t in range(TT):
                pool.wait_ge(htok_ready, t + 1)
                for c in range(2):
                    pool.indirect_dma_start(
                        out=xperm, out_offset=bass.IndirectOffsetOnAxis(ap=rowi[:, c, t:t + 1], axis=0),
                        in_=htok[:, t, :], in_offset=None).then_inc(scattered, 16)
            pool.wait_ge(scattered, 16 * 2 * TT)
            pool.dma_start(xs, xperm[0:P, :]).then_inc(xs_in, 16)
            pool.wait_ge(etr_done, 2)
            pool.dma_start(xs, xperm[P:2 * P, :]).then_inc(xs_in, 16)
            pool.drain().then_inc(y_left, 1)
            with pool.Fori(0, SLOTS) as s:
                pool.wait_ge(etr_done, 2 + G_ETR + 6 * s + TR_OF["xb"] + 1)
                pool.dma_start(xs, xperm[bass.ds((s + 2) * P, P), :]).then_inc(xs_in, 16)
                pool.wait_ge(y_evac, s + 2)
                pool.dma_start(yslots[bass.ds(s * P, P), :], ybuf).then_inc(y_stored, 16)
                pool.wait_ge(y_stored, 16 * (s + 1))
                pool.sem_inc(y_left, 1)
            pool.wait_ge(y_stored, 16 * SLOTS)
            pool.wait_ge(xs_in, 16 * (SLOTS + 2))
            for t in range(TT):
                if t >= 2:
                    pool.wait_ge(comb_ready, t - 1)
                    pool.wait_ge(main_done, MAIN[("comb", t - 2)] + 1)
                for c in range(2):
                    pool.indirect_dma_start(
                        out=picked[:, t % 2, c, :], out_offset=None, in_=yslots,
                        in_offset=bass.IndirectOffsetOnAxis(ap=rowi[:, c, t:t + 1], axis=0)).then_inc(gathered[t % 2], 16)

        @block.scalar
        def _(act):
            act.wait_ge(cond_in, 16)
            nc.scalar.activation(cond[:], cond[:], ACT.Silu).then_inc(cond_ready, 1)
            act.wait_ge(main_done, MAIN[("lam",)] + 1)
            nc.scalar.activation(lam_e[:].rearrange("p l m -> p (l m)"), main_pair(("lam",))[:, 0:4],
                                 ACT.Exp).then_inc(lam_exp, 1)

            def square(l, kind, k, src, view=lambda a: a):
                n = sq_at(l, kind, k)
                if n >= 2:
                    act.wait_ge(sq_used, n - 1)
                nc.scalar.activation(view(sq[:, n % 2, :]), src, ACT.Square).then_inc(sq_ready, 1)

            def root(v):
                act.wait_ge(var_ready, v)
                nc.scalar.activation(rb[:], rb[:], ACT.Sqrt).then_inc(std_ready, 1)

            def sub_hi_part(q):
                raw_w, arrival = sub_raw(q)
                act.wait_ge(*arrival)
                if q >= SUBS_KEPT:
                    wait_named(act, SUBS[q - SUBS_KEPT][3])
                nc.scalar.activation(sub_of(sub_hi, q), raw_w, ACT.Copy).then_inc(t_hi, 1)

            def modulate(n, l, which, split=True):
                for k in range(KC):
                    act.wait_ge(xn_ready, 8 * n + k + 1)
                    s0 = 0 if which == 0 else 24
                    for c, (a, b) in enumerate(((0, N_LAT), (N_LAT, T))):
                        ins = nc.scalar.activation(h_t[:, k, a:b], h_t[:, k, a:b], ACT.Identity,
                                                   bias=mod[:, l, s0 + k, c:c + 1],
                                                   scale=gain[:, l, which, k, c:c + 1])
                    ins.then_inc(h_ready, 1)
                    if split:
                        act.wait_ge(h_ready, 8 * n + k + 1)
                        nc.scalar.activation(h_hi[:, k, :], h_t[:, k, :], ACT.Copy).then_inc(h_hi_ready, 1)

            def raw_item(l, r):
                n = 13 * l + r
                rows = MQK if r in (0, 9, 10, 11, 12) else P
                act.wait_ge(main_done, MAIN[("rope", l, r)] + 1)
                if n >= 2:
                    act.wait_ge(rope_done, n - 1)
                    act.wait_ge(rot_used, n - 1)
                if r < 9:
                    nc.scalar.activation(halves(raw[0:rows, n % 2, :]), main_halves(("rope", l, r))[0:rows],
                                         ACT.Copy).then_inc(raw_ready, 1)
                else:
                    nc.scalar.activation(raw[0:rows, n % 2, :], main_pair(("rope", l, r))[0:rows, :],
                                         ACT.Copy).then_inc(raw_ready, 1)

            for l in range(DEPTH):
                if l:
                    act.wait_ge(pv_done, 2 * ITEMS * l)
                    act.wait_ge(main_done, MAIN[("uv", l - 1, KT - 1)] + 1)
                act.dma_start(wuq, d["w_uq"][l].rearrange("(k p) n -> p k n", p=P)).then_inc(layer_w_in, 16)
                act.dma_start(wuk, d["w_uk"][l]).then_inc(layer_w_in, 16)
                act.dma_start(wuv, d["w_uv"][l]).then_inc(layer_w_in, 16)
                if l == 0:
                    act.wait_ge(kr_zero, 1)
                else:
                    act.wait_ge(t_split, SUB_AT[("rope", 0, 0)] + 1)
                act.dma_start(wkr[:, :, NOPE:MQK], w_in[l, :, :, 1920:1952]).then_inc(layer_w_in, 16)
                if l == 0:
                    act.wait_ge(x_in, 16)
                    for k in range(KC):
                        square(l, "mix", k, x_t[:, k, :])
                if l:
                    act.wait_ge(x_upd, 24)
                act.dma_start(ckv_t[:, 0:PAST], d["cache_ckv"][l]).then_inc(cache_c_in, 16)
                act.dma_start(kr_t[NOPE:MQK, 0:PAST], d["cache_kr"][l]).then_inc(cache_c_in, 16)
                act.dma_start(k_t[:, :, 0:PAST], d["cache_k"][l]).then_inc(cache_k_in, 16)
                act.dma_start(v_n[:, 0:2, :], d["cache_v"][l]).then_inc(cache_v_in, 16)
                q = SUB_AT[("lora", l, 0)]
                sub_hi_part(q)
                sub_hi_part(q + 1)
                root(4 * l + 1)
                modulate(2 * l, l, 0)
                for g in range(3):
                    src = main_halves(("lora", l, g))
                    act.wait_ge(main_done, MAIN[("lora", l, g)] + 1)
                    square(l, "lora", g, src, halves)
                    if l and g == 0:
                        act.wait_ge(x_upd, 24)
                    nc.scalar.activation(halves(lora_raw[:, g, :]), src, ACT.Copy).then_inc(lora_ready, 1)
                    sub_hi_part(q + 2 + g)
                raw_item(l, 0)
                sub_hi_part(q + 5)
                root(4 * l + 2)
                raw_item(l, 1)
                sub_hi_part(q + 6)
                root(4 * l + 3)
                sub_hi_part(q + 7)
                for r in range(2, 9):
                    raw_item(l, r)
                    if r < 8:
                        sub_hi_part(q + 6 + r)
                for n in range(14, 16):
                    sub_hi_part(q + n)
                act.wait_ge(rope_done, 13 * l + 9)
                act.dma_start(d["new_k"][l], k_t[:, :, NKEY - N_PROMPT:NKEY]).then_inc(kv_out, 16)
                act.dma_start(d["new_kr"][l], kr_t[NOPE:MQK, NKEY - N_PROMPT:NKEY]).then_inc(kv_out, 16)
                act.wait_ge(lat_normed, 2 * l + 1)
                act.dma_start(d["new_ckv"][l], ckv_t[:, NKEY - N_PROMPT:NKEY]).then_inc(kv_out, 16)
                act.wait_ge(vd_ready, 10 * l + 10)
                act.dma_start(d["new_v"][l], v_n[:, KT - 1, :]).then_inc(kv_out, 16)

                def attention(f):
                    base = (2 * l + f) * ITEMS
                    maps, scale = (2, D_SCALE) if f == 0 else (1, M_SCALE)

                    def exps(i):
                        it = base + i
                        nk = LAT_KEYS if i % TT < TT - 1 else N_PROMPT
                        sc = ps[:, 1536 * (it % 2):1536 * (it % 2) + 1536].rearrange("p (m n) -> p m n", m=2)
                        if it >= 2:
                            act.wait_ge(tr_a_done, it - 1)
                            act.wait_ge(tr_b_done, n_tr_b(it - 2))
                        if f == 0 and i < 2:
                            act.wait_ge(lat_normed, 2 * l + 2)
                            act.wait_ge(rope_done, 13 * l + 9)
                        act.wait_ge(max_ready, it + 1)
                        for m in range(maps):
                            ins = nc.scalar.activation(e_buf[:, it % 2, m, 0:nk], sc[:, m, 0:nk], ACT.Exp,
                                                       bias=stat[:, it % 2, 2 + m:3 + m], scale=scale,
                                                       accum_out=stat[:, it % 2, 4 + m:5 + m])
                        ins.then_inc(exp_done, 1)

                    exps(0)
                    for i in range(ITEMS):
                        it = base + i
                        if i + 1 < ITEMS:
                            exps(i + 1)
                        nt = 4 if i % TT < TT - 1 else 1
                        act.wait_ge(tr_a_done, it + 1)
                        if it >= 2:
                            act.wait_ge(pv_done, it - 1)
                        nc.scalar.activation(pt_buf[:, it % 2, 0:nt, :], ps[:, 3072:3072 + nt * P].rearrange("p (k n) -> p k n", k=nt),
                                             ACT.Copy).then_inc(pt_a_ready, 1)

                attention(0)
                for h in range(HEADS):
                    if h == 0:
                        act.wait_ge(pv_evac, (2 * l + 1) * ITEMS)
                        act.wait_ge(mod_late, 8 * l + 4)
                    square(l, "head", h, mixed[:, h, :])
                    if h:
                        raw_item(l, 8 + h)
                raw_item(l, 12)
                act.wait_ge(hvar_ready, 4 * l + 4)
                nc.scalar.activation(hrb, hrb, ACT.Sqrt).then_inc(hstd_ready, 1)
                for v in range(KT):
                    act.wait_ge(main_done, MAIN[("uv", l, v)] + 1)
                    nc.scalar.activation(v_n[:, v, :], main_pair(("uv", l, v))[:, 0:512], ACT.Copy).then_inc(vm_ready, 1)
                act.wait_ge(heads_normed, 4 * l + 4)

                def head_hi(h):
                    nc.scalar.activation(h_hi[:, h, :], mixed[:, h, :], ACT.Copy).then_inc(mixed_hi, 1)

                for h in range(HEADS):
                    head_hi(h)
                attention(1)
                q = SUB_AT[("o", l, 0)]
                sub_hi_part(q)
                sub_hi_part(q + 1)
                for h in range(HEADS, 2 * HEADS):
                    act.wait_ge(pv_evac, (2 * l + 1) * ITEMS + TT * (h - HEADS + 1))
                    head_hi(h)
                for k in range(KC):
                    act.wait_ge(x_upd, (24 if l else 0) + k + 1)
                    if k == 0:
                        act.wait_ge(mod_late, 8 * l + 8)
                    square(l, "ffn", k, x_t[:, k, :])
                    if k + 2 < KC:
                        sub_hi_part(q + k + 2)
                if l == 0:
                    q = SUB_AT[("gate", 0)]
                    sub_hi_part(q)
                    sub_hi_part(q + 1)
                root(4 * l + 4)
                modulate(2 * l + 1, l, 1, l == 0)
                if l == 0:
                    for half, js in enumerate(FF_HALF):
                        for j in js:
                            act.wait_ge(main_done, MAIN[("gate", j)] + 1)
                            if j >= 2:
                                act.wait_ge(hid_ready, j - 1)
                            nc.scalar.activation(halves(sil[:, j % 2, :]), main_halves(("gate", j)),
                                                 ACT.Silu).then_inc(silu_ready, 1)
                            q += 1
                            sub_hi_part(q + 1)
                            act.wait_ge(hid_product, j + 1)
                            if j == FF_HALF[1][0]:
                                act.wait_ge(main_done, MAIN[("down", 0, KC - 1)] + 1)
                            nc.scalar.activation(hid_hi[:, j - js[0], :], sil[:, j % 2, :], ACT.Copy).then_inc(hid_hi_ready, 1)
                            q += 1
                            sub_hi_part(q + 1)
                        for d_ in range(KC):
                            for _ in range(2):
                                q += 1
                                if not (half and d_ == KC - 1):
                                    sub_hi_part(q + 1)
                            if half:
                                act.wait_ge(x_upd, 16 + d_ + 1)
                                square(1, "mix", d_, x_t[:, d_, :])

            act.wait_ge(lmax_ready, 1)
            nc.scalar.activation(rt[:, 0], rt[:, 0], ACT.Exp).then_inc(lexp_ready, 1)
            for t in range(TT):
                act.wait_ge(main_done, MAIN[("htok", t)] + 1)
                src = ps[:, 1024 * (MAIN[("htok", t)] % 3):1024 * (MAIN[("htok", t)] % 3) + 1024]
                nc.scalar.activation(htok[:, t, :], src, ACT.Copy).then_inc(htok_ready, 1)

            def tr_hi(dst, bank, n, kn):
                act.wait_ge(etr_done, n)
                nc.scalar.activation(dst, ps[:, 512 * bank:512 * bank + kn * P].rearrange("p (k n) -> p k n", k=kn),
                                     ACT.Copy).then_inc(ehi_ready, 1)

            for half in range(2):
                act.wait_ge(scattered, 16 * 2 * TT)
                tr_hi(xs_hi[:, 4 * half:4 * half + 4, :], 4 + TR_OF[("xa", "xb")[half]] % 2, half + 1, 4)

            def piece_hi(s, n):
                act.wait_ge(m_arrived[n % MRING], 16 * (NPC // MRING * s + n // MRING + 1))
                act.wait_ge(pc_done, NPC * s + n + 1)
                nc.scalar.activation(w_hi[:, n % SPLITS, :], mraw[:, n % MRING, :], ACT.Copy).then_inc(w_hi_ready, 1)

            def expert_hi(s, last):
                def ahead(n):
                    if not (last and n >= NPC):
                        piece_hi(s, n)

                def silu(c):
                    act.wait_ge(pc_done, pieces_done(s, 2 * c))
                    act.wait_ge(eact_ready, 4 * s + c + 1)
                    nc.scalar.activation(esil[:, c % 2, :], ps[:, 512 * (2 * c % 4):512 * (2 * c % 4) + HCH],
                                         ACT.Silu).then_inc(esilu_ready, 1)

                def turned(c):
                    j = TR_OF[c]
                    if c in ("xa", "xb"):
                        dst, kn = xs_hi[:, 4 * (j - 4):4 * (j - 4) + 4, :], 4
                    else:
                        dst, kn = ea_hi[:, BLK[c][0]:BLK[c][1], :], BLK[c][1] - BLK[c][0]
                        act.wait_ge(pc_done, pieces_done(s, -1))
                    tr_hi(dst, 4 + j % 2, 2 + G_ETR + 6 * s + j + 1, kn)

                ahead(2)
                for c in range(3):
                    silu(c)
                    if c:
                        turned(c - 1)
                    ahead(2 * c + 3)
                    ahead(2 * c + 4)
                silu(3)
                turned(2)
                ahead(9)
                ahead(10)
                turned(3)
                ahead(11)
                turned("xa")
                ahead(12)
                turned("xb")
                ahead(13)

            piece_hi(0, 0)
            piece_hi(0, 1)
            with act.Fori(0, SLOTS - 1) as s:
                expert_hi(s, False)
            expert_hi(SLOTS - 1, True)

            for k in range(KC):
                act.wait_ge(x_upd, 32 + TT)
                square(DEPTH, "fin", k, x_t[:, k, :])
            root(4 * DEPTH + 1)
            for k in range(KC):
                act.wait_ge(xn_ready, 8 * 4 + k + 1)
                nc.scalar.activation(h_t[:, k, :], h_t[:, k, :], ACT.Copy, scale=vecs[:, V_FIN + k:V_FIN + k + 1]).then_inc(h_ready, 1)

        @block.vector
        def _(dve):
            steps_done = [0]

            def link(ins):
                steps_done[0] += 1
                ins.then_inc(dve_step, 1)
                dve.wait_ge(dve_step, steps_done[0])

            dve.wait_ge(vec_in, 32)
            nc.vector.tensor_tensor(lam_prod[:], lam_in[:, :, :, 0], lam_in[:, :, :, 1], ALU.mult).then_inc(lam_prod_ready, 1)
            for l in range(DEPTH):
                link(nc.vector.tensor_scalar(subg[:, l:l + 1], vecs[:, V_SUB + l:V_SUB + l + 1], 1.0 - lam_init(l), None, ALU.mult))
            dve.wait_ge(lam_exp, 1)
            for l in range(DEPTH):
                link(nc.vector.tensor_tensor(neg_lam[:, l:l + 1], lam_e[:, l, 1:2], lam_e[:, l, 0:1], ALU.subtract))
                link(nc.vector.tensor_scalar(neg_lam[:, l:l + 1], neg_lam[:, l:l + 1], -lam_init(l), None, ALU.add))

            def add_bias(l, c0, n, src):
                b = vecs[:, V_BADA + 48 * l + c0:V_BADA + 48 * l + c0 + n]
                return nc.vector.tensor_tensor(mod[:, l, c0:c0 + n, :], src.rearrange("p (c g) -> p c g", g=2),
                                               b.unsqueeze(2).to_broadcast([P, n, 2]), ALU.add)

            def make_gain(l, which):
                g = vecs[:, (V_MIX, V_FFN)[which] + 8 * l:(V_MIX, V_FFN)[which] + 8 * l + 8]
                s0 = (8, 32)[which]
                link(nc.vector.scalar_tensor_tensor(gain[:, l, which], mod[:, l, s0:s0 + 8, :], 1.0,
                                                    g.unsqueeze(2).to_broadcast([P, KC, 2]), ALU.add, ALU.mult))

            for n in range(2):
                dve.wait_ge(main_done, MAIN[("ada0", n)] + 1)
                o = 1024 * (MAIN[("ada0", n)] % 3)
                nc.vector.tensor_copy(ada_row0[:, 1024 * n:1024 * n + 1024], ps[0:2, o:o + 1024]).then_inc(ada_rows, 1)
            dve.wait_ge(main_done, MAIN[("ada0t",)] + 1)
            add_bias(0, 0, 16, main_pair(("ada0t",))[:, 0:32]).then_inc(mod_ready, 1)
            dve.wait_ge(mod_ready, 1)
            make_gain(0, 0)

            def sub_rest(q):
                raw_w, arrival = sub_raw(q)
                dve.wait_ge(*arrival)
                dve.wait_ge(t_hi, q + 1)
                nc.vector.tensor_tensor(sub_of(sub_lo, q), raw_w, sub_of(sub_hi, q).bitcast(f32),
                                        ALU.subtract).then_inc(t_split, 1)

            def norm(n, l, v, aux_label, split=None):
                dve.wait_ge(aux_done, AUX[aux_label] + 1)
                nc.vector.tensor_scalar(rb[:], AUXP, 1.0 / D_MODEL, EPS, ALU.mult, ALU.add).then_inc(var_ready, 1)
                dve.wait_ge(std_ready, v)
                link(nc.vector.reciprocal(rb[:], rb[:]))
                for k in range(KC + 2):
                    if k < KC:
                        nc.vector.tensor_tensor(h_t[:, k, :], x_t[:, k, :], rb[:], ALU.mult).then_inc(xn_ready, 1)
                    if k >= 2 and split is not None:
                        dve.wait_ge(h_hi_ready, split + k - 1)
                        nc.vector.tensor_tensor(h_lo[:, k - 2, :], h_t[:, k - 2, :], h_hi[:, k - 2, :].bitcast(f32),
                                                ALU.subtract).then_inc(h_split, 1)

            def rot(l, r):
                n = 13 * l + r
                rows = MQK if r in (0, 9, 10, 11, 12) else P
                sn = sin_m if rows == MQK else sin_d
                dve.wait_ge(aux_done, AUX[("rot", l, r)] + 1)
                if n >= 2:
                    dve.wait_ge(rope_done, n - 1)
                nc.vector.tensor_tensor(rtmp[0:rows, n % 2, :], AUXP[0:rows, 0:N_LAT], sn[0:rows, :],
                                        ALU.mult).then_inc(rot_used, 1)

            def residual(l, label, d_, g0):
                dve.wait_ge(main_done, MAIN[label] + 1)
                o = 1024 * (MAIN[label] % 3)
                for a, b, bank, c in ((0, TH, 0, 0), (TH, N_LAT, 1, 0), (N_LAT, T, 1, 1)):
                    src = ps[:, o + 512 * bank + a - TH * bank:o + 512 * bank + b - TH * bank]
                    ins = nc.vector.scalar_tensor_tensor(x_t[:, d_, a:b], src, mod[:, l, g0 + d_, c:c + 1],
                                                         x_t[:, d_, a:b], ALU.mult, ALU.add)
                ins.then_inc(x_upd, 1)

            for l in range(DEPTH):
                if l == 0:
                    dve.wait_ge(x_in, 16)
                    dve.wait_ge(const_in, 160)
                q = SUB_AT[("lora", l, 0)]
                sub_rest(q)
                sub_rest(q + 1)
                norm(2 * l, l, 4 * l + 1, ("norm", l, "mix"), 16 * l)
                sub_rest(q + 2)
                sub_rest(q + 3)
                dve.wait_ge(lora_ready, 3 * l + 3)
                sub_rest(q + 4)
                sub_rest(q + 5)
                dve.wait_ge(aux_done, AUX[("norm", l, "ckv")] + 1)
                nc.vector.tensor_scalar(rb[:], AUXP, 1.0 / KVL, EPS, ALU.mult, ALU.add).then_inc(var_ready, 1)
                dve.wait_ge(std_ready, 4 * l + 2)
                link(nc.vector.reciprocal(rb[:], rb[:]))
                nc.vector.scalar_tensor_tensor(ckv_t[:, PAST:NKEY], lora_raw[:, 0, :], vecs[:, V_KVN + l:V_KVN + l + 1],
                                               rb[:], ALU.mult, ALU.mult).then_inc(lat_normed, 1)
                dve.wait_ge(lat_normed, 2 * l + 1)
                sub_rest(q + 6)
                dve.wait_ge(aux_done, AUX[("norm", l, "cq")] + 1)
                nc.vector.tensor_scalar(rb[:], AUXP, 1.0 / QL, EPS, ALU.mult, ALU.add).then_inc(var_ready, 1)
                dve.wait_ge(std_ready, 4 * l + 3)
                link(nc.vector.reciprocal(rb[:], rb[:]))
                for c in range(2):
                    ins = nc.vector.scalar_tensor_tensor(cq_t[:, c, :], lora_raw[:, 1 + c, :],
                                                         vecs[:, V_QN + 2 * l + c:V_QN + 2 * l + c + 1],
                                                         rb[:], ALU.mult, ALU.mult)
                ins.then_inc(lat_normed, 1)
                sub_rest(q + 7)
                for r in range(7):
                    rot(l, r)
                    if r < 6:
                        sub_rest(q + 8 + r)

                def vd(v):
                    half, t = v // TT, v % TT
                    dve.wait_ge(main_done, MAIN[("vd", l, v)] + 1)
                    nc.vector.tensor_copy(v_n[:, 2 + t, 256 * half:256 * half + 256],
                                          main_pair(("vd", l, v))[:, 0:256]).then_inc(vd_ready, 1)

                vd(0)
                rot(l, 7)
                vd(1)
                rot(l, 8)
                for v in range(2, 10):
                    vd(v)
                    if v == 4:
                        sub_rest(q + 14)
                        sub_rest(q + 15)

                def attention(f):
                    base = (2 * l + f) * ITEMS
                    maps, scale = (2, D_SCALE) if f == 0 else (1, M_SCALE)

                    def item(i):
                        return base + i, (base + i) % 2, LAT_KEYS if i % TT < TT - 1 else N_PROMPT

                    def maxes(i):
                        it, b, nk = item(i)
                        sc = ps[:, 1536 * b:1536 * b + 1536].rearrange("p (m n) -> p m n", m=2)
                        dve.wait_ge(scores_done, it + 1)
                        if it >= 2:
                            dve.wait_ge(exp_done, it - 1)
                        link(nc.vector.reduce_max(stat[:, b, 0:maps], sc[:, 0:maps, 0:nk], AXX))
                        nc.vector.tensor_scalar(stat[:, b, 2:2 + maps], stat[:, b, 0:maps], -scale, None,
                                                ALU.mult).then_inc(max_ready, 1)

                    def combine(i):
                        it, b, nk = item(i)
                        dve.wait_ge(exp_done, it + 1)
                        if it >= 2:
                            dve.wait_ge(tr_a_done, it - 1)
                            dve.wait_ge(tr_b_done, n_tr_b(it - 2))
                        link(nc.vector.reciprocal(stat[:, b, 6:6 + maps], stat[:, b, 4:4 + maps]))
                        ins = nc.vector.tensor_scalar(diag[:, b, :], ident[:], stat[:, b, 6:7], None, ALU.mult)
                        if f == 0:
                            link(nc.vector.scalar_tensor_tensor(stat[:, b, 8:9], stat[:, b, 4:5], neg_lam[:, l:l + 1],
                                                                stat[:, b, 7:8], ALU.mult, ALU.mult))
                            e1 = e_buf[:, b, 0, 0:nk]
                            ins = nc.vector.scalar_tensor_tensor(e1, e_buf[:, b, 1, 0:nk], stat[:, b, 8:9], e1,
                                                                 ALU.mult, ALU.add)
                        ins.then_inc(p_ready, 1)

                    def pv_out(i):
                        it, b, nk = item(i)
                        h, qt = i // TT, i % TT
                        dve.wait_ge(pv_done, it + 1)
                        nc.vector.tensor_copy(mixed[:, 4 * f + h, qt * P:(qt + 1) * P], ps[:, 3840:3968]).then_inc(pv_evac, 1)

                    def pt_b(i):
                        it, b, nk = item(i)
                        dve.wait_ge(tr_b_done, n_tr_b(it))
                        if it >= 2:
                            dve.wait_ge(pv_done, it - 1)
                        nc.vector.tensor_copy(pt_buf[:, b, 4:6, :], ps[:, 3584:3840].rearrange("p (k n) -> p k n", k=2)).then_inc(pt_b_ready, 1)

                    def late_row_copy(u, b):
                        n = len(ada_after_head(l, u))
                        dve.wait_ge(late_rows_done, 8 * l + u + 1)
                        if 8 * l + u:
                            dve.wait_ge(ada_done, 8 * l + u)
                        src = ps[0:2, 1536 * b:1536 * b + 512 * n].rearrange("p (n c) -> p n c", n=n)[:, :, 0:256]
                        nc.vector.tensor_copy(ada_row[:, 0:256 * n].rearrange("p (n c) -> p n c", n=n), src).then_inc(late_rows, 1)

                    def late_mods(u):
                        todo = ada_after_head(l, u)
                        dve.wait_ge(ada_done, 8 * l + u + 1)
                        src = ps[:, 3968:3968 + 4 * len(todo)]
                        for n, (ll, c) in enumerate(todo):
                            ins = add_bias(ll, 2 * c, 2, src[:, 4 * n:4 * n + 4])
                        ins.then_inc(mod_late, 1)

                    maxes(0)
                    combine(0)
                    for i in range(ITEMS):
                        if i + 1 < ITEMS:
                            maxes(i + 1)
                        if i:
                            pv_out(i - 1)
                        if i % TT == TT - 1:
                            late_row_copy(4 * f + i // TT, (base + i) % 2)
                        if i % TT == 0 and i:
                            late_mods(4 * f + i // TT - 1)
                        if i % TT < TT - 1:
                            pt_b(i)
                        if i + 1 < ITEMS:
                            combine(i + 1)
                    pv_out(ITEMS - 1)
                    late_mods(4 * f + HEADS - 1)

                attention(0)
                for h in range(HEADS):
                    dve.wait_ge(aux_done, AUX[("norm", l, "head", h)] + 1)
                    if h == 0:
                        dve.wait_ge(tr_a_done, (2 * l + 1) * ITEMS)
                        dve.wait_ge(tr_b_done, n_tr_b((2 * l + 1) * ITEMS - 1))
                    nc.vector.tensor_scalar(hrb[:, h, :], AUXP, 1.0 / P, EPS, ALU.mult, ALU.add).then_inc(hvar_ready, 1)
                    if h:
                        rot(l, 8 + h)
                rot(l, 12)
                for h in range(HEADS):
                    if h == 0:
                        dve.wait_ge(kv_out, 16 * 4 * (l + 1))
                    dve.wait_ge(main_done, MAIN[("uk", l, h)] + 1)
                    src = ps[0:NOPE, 1024 * (MAIN[("uk", l, h)] % 3):1024 * (MAIN[("uk", l, h)] % 3) + 1024]
                    nc.vector.tensor_copy(k_t[0:NOPE, h, :].rearrange("p (c n) -> p c n", c=2),
                                          src.rearrange("p (c n) -> p c n", c=2)[:, :, 0:448]).then_inc(km_ready, 1)
                dve.wait_ge(hstd_ready, l + 1)
                link(nc.vector.reciprocal(hrb, hrb))
                for h in range(HEADS):
                    nc.vector.scalar_tensor_tensor(mixed[:, h, :], mixed[:, h, :], subg[:, l:l + 1], hrb[:, h, :],
                                                   ALU.mult, ALU.mult).then_inc(heads_normed, 1)

                def head_rest(h):
                    dve.wait_ge(mixed_hi, 8 * l + h + 1)
                    nc.vector.tensor_tensor(h_lo[:, h, :], mixed[:, h, :], h_hi[:, h, :].bitcast(f32),
                                            ALU.subtract).then_inc(mixed_split, 1)

                for h in range(HEADS):
                    head_rest(h)
                attention(1)
                q = SUB_AT[("o", l, 0)]
                sub_rest(q)
                sub_rest(q + 1)
                for h in range(HEADS, 2 * HEADS):
                    head_rest(h)
                dve.wait_ge(mod_late, 8 * l + 8)
                make_gain(l, 1)
                if l + 1 < DEPTH:
                    make_gain(l + 1, 0)
                for d_ in range(KC):
                    residual(l, ("o", l, d_), d_, 16)
                    if d_ + 2 < KC:
                        sub_rest(q + d_ + 2)
                if l == 0:
                    q = SUB_AT[("gate", 0)]
                    sub_rest(q)
                    sub_rest(q + 1)
                norm(2 * l + 1, l, 4 * l + 4, ("norm", l, "ffn"), 8 if l == 0 else None)
                if l == 0:
                    for half, js in enumerate(FF_HALF):
                        for j in js:
                            q += 1
                            sub_rest(q + 1)
                            dve.wait_ge(main_done, MAIN[("up", j)] + 1)
                            dve.wait_ge(silu_ready, j + 1)
                            nc.vector.tensor_tensor(halves(sil[:, j % 2, :]), halves(sil[:, j % 2, :]), main_halves(("up", j)),
                                                    ALU.mult).then_inc(hid_product, 1)
                            dve.wait_ge(hid_hi_ready, j + 1)
                            nc.vector.tensor_tensor(hid_lo[:, j - js[0], :], sil[:, j % 2, :],
                                                    hid_hi[:, j - js[0], :].bitcast(f32), ALU.subtract).then_inc(hid_ready, 1)
                            q += 1
                            sub_rest(q + 1)
                        for d_ in range(KC):
                            for _ in range(2):
                                q += 1
                                if not (half and d_ == KC - 1):
                                    sub_rest(q + 1)
                            residual(l, ("down", half, d_), d_, 40)

            dve.wait_ge(aux_done, AUX[("router",)] + 1)
            nc.vector.tensor_copy(lg[:].rearrange("p t e -> p (t e)"), AUXP[:, 0:TT * NE]).then_inc(lg_ready, 1)
            dve.wait_ge(lg_ready, 1)
            by_e = lg[:].unsqueeze(3).to_broadcast([P, TT, NE, NE])
            by_o = lg[:].unsqueeze(2).to_broadcast([P, TT, NE, NE])

            def flat(a):
                return a.rearrange("p t e o -> p t (e o)")

            link(nc.vector.reduce_max(rv[:, 0], lg[:], AXX))
            link(nc.vector.tensor_tensor(rt[:, 0], lg[:], rv[:, 0].unsqueeze(2).to_broadcast([P, TT, NE]), ALU.subtract))
            nc.vector.drain().then_inc(lmax_ready, 1)
            link(nc.vector.tensor_tensor(cmp_a[:], by_o, by_e, ALU.is_gt))
            link(nc.vector.tensor_tensor(cmp_b[:], by_o, by_e, ALU.is_equal))
            for t in range(TT):
                link(nc.vector.tensor_tensor(cmp_b[:, t], cmp_b[:, t], tri8, ALU.mult))
            link(nc.vector.tensor_tensor(flat(cmp_a[:]), flat(cmp_a[:]), flat(cmp_b[:]), ALU.add))
            link(nc.vector.reduce_sum(rt[:, 1], cmp_a[:], AXX))
            nc.vector.tensor_scalar(rt[:, 4], rt[:, 1], 2.0, None, ALU.is_lt).then_inc(sel_ready, 1)
            link(nc.vector.tensor_scalar(rt[:, 2], rt[:, 1], 0.0, None, ALU.is_equal))
            link(nc.vector.tensor_scalar(rt[:, 3], rt[:, 1], 1.0, None, ALU.is_equal))
            dve.wait_ge(aux_done, AUX[("rank",)] + 1)
            nc.vector.tensor_copy(rt[:, 5].rearrange("p t e -> p (t e)"), AUXP[:, 0:TT * NE])
            nc.vector.tensor_copy(cnt[:, 0], AUXP[:, TT * NE:TT * NE + NE]).then_inc(rank_ready, 1)
            dve.wait_ge(rank_ready, 1)
            c58 = cmp_a[:, 0].rearrange("p a b -> p (a b)")[:, 0:NE * TT].rearrange("p (a b) -> p a b", a=NE)
            link(nc.vector.tensor_tensor(c58, cnt[:, 0].unsqueeze(2).to_broadcast([P, NE, TT]),
                                         steps.unsqueeze(1).to_broadcast([P, NE, TT]), ALU.is_gt))
            link(nc.vector.reduce_sum(cnt[:, 1], c58, AXX))
            link(nc.vector.tensor_tensor(cmp_a[:, 0], cnt[:, 1].unsqueeze(1).to_broadcast([P, NE, NE]), tri8, ALU.mult))
            link(nc.vector.reduce_sum(cnt[:, 2], cmp_a[:, 0], AXX))
            link(nc.vector.tensor_scalar(cnt[:, 3], cnt[:, 2], float(P), None, ALU.mult))
            link(nc.vector.tensor_tensor(rt[:, 5], rt[:, 5], cnt[:, 3].unsqueeze(1).to_broadcast([P, TT, NE]), ALU.add))
            for c in range(2):
                link(nc.vector.tensor_tensor(rt[:, 6], rt[:, 2 + c], rt[:, 5], ALU.mult))
                link(nc.vector.reduce_sum(rv[:, 1 + c], rt[:, 6], AXX))
            nc.vector.tensor_copy(rowi[:], rv[:, 1:3]).then_inc(rows_ready, 1)
            c17 = cmp_b[:, 0:2].rearrange("p t a b -> p (t a b)")[:, 0:SLOTS * 7].rearrange("p (a b) -> p a b", a=SLOTS)
            link(nc.vector.tensor_tensor(c17, slot_rows.unsqueeze(2).to_broadcast([P, SLOTS, 7]),
                                         cnt[:, 3, 1:8].unsqueeze(1).to_broadcast([P, SLOTS, 7]), ALU.is_ge))
            link(nc.vector.reduce_sum(slot_e[:], c17, AXX))
            nc.vector.tensor_copy(slot_i[:], slot_e[:]).then_inc(rows_ready, 1)
            dve.wait_ge(lexp_ready, 1)
            link(nc.vector.reduce_sum(rv[:, 3], rt[:, 0], AXX))
            link(nc.vector.reciprocal(rv[:, 4], rv[:, 3]))
            link(nc.vector.tensor_tensor(rt[:, 0], rt[:, 0], rv[:, 4].unsqueeze(2).to_broadcast([P, TT, NE]), ALU.mult))
            for c in range(2):
                link(nc.vector.tensor_tensor(rt[:, 6], rt[:, 2 + c], rt[:, 0], ALU.mult))
                link(nc.vector.reduce_sum(rv[:, 5 + c], rt[:, 6], AXX))
            link(nc.vector.tensor_tensor(rv[:, 7], rv[:, 5], rv[:, 6], ALU.add))
            link(nc.vector.reciprocal(rv[:, 8], rv[:, 7]))
            for c in range(2):
                link(nc.vector.tensor_tensor(rv[:, 9 + c], rv[:, 5 + c], rv[:, 8], ALU.mult))

            def piece_lo(s, n, h):
                if h == 0:
                    dve.wait_ge(m_arrived[n % MRING], 16 * (NPC // MRING * s + n // MRING + 1))
                    dve.wait_ge(w_hi_ready, NPC * s + n + 1)
                a = slice(PIECE_F // 2 * h, PIECE_F // 2 * (h + 1))
                ins = nc.vector.tensor_tensor(w_lo[:, n % SPLITS, a], mraw[:, n % MRING, a],
                                              w_hi[:, n % SPLITS, a].bitcast(f32), ALU.subtract)
                if h:
                    ins.then_inc(w_split, 1)

            def tr_lo(dst, hi, bank, n, kn):
                dve.wait_ge(ehi_ready, n)
                nc.vector.tensor_tensor(dst, ps[:, 512 * bank:512 * bank + kn * P].rearrange("p (k n) -> p k n", k=kn),
                                        hi.bitcast(f32), ALU.subtract).then_inc(etr_evac, 1)

            def expert_lo(s, last):
                def ahead(n, halves=(0, 1)):
                    for h in halves:
                        if not (last and n >= NPC):
                            piece_lo(s, n, h)

                def turned(c):
                    j = TR_OF[c]
                    if c in ("xa", "xb"):
                        a = slice(4 * (j - 4), 4 * (j - 4) + 4)
                        dst, hi, kn = xs_lo[:, a, :], xs_hi[:, a, :], 4
                    else:
                        a = slice(*BLK[c])
                        dst, hi, kn = ea_lo[:, a, :], ea_hi[:, a, :], BLK[c][1] - BLK[c][0]
                    tr_lo(dst, hi, 4 + j % 2, 2 + 6 * s + j + 1, kn)

                def product(c):
                    bank = (2 * c + 1) % 4
                    dve.wait_ge(pc_done, pieces_done(s, 2 * c + 1))
                    dve.wait_ge(esilu_ready, 4 * s + c + 1)
                    dve.wait_ge(etr_done, 2 + 6 * s + TR_OF[min(c + 1, 3)] + 1)
                    nc.vector.tensor_tensor(eact[:, HCH * c:HCH * (c + 1)], esil[:, c % 2, :],
                                            ps[:, 512 * bank:512 * bank + HCH], ALU.mult).then_inc(eact_ready, 1)

                ahead(2)
                for c in range(3):
                    if c:
                        turned(c - 1)
                    ahead(2 * c + 3)
                    product(c)
                    ahead(2 * c + 4)
                turned(2)
                ahead(9, (0,))
                product(3)
                ahead(9, (1,))
                turned(3)
                ahead(10)
                ahead(11)
                turned("xa")
                ahead(12)
                turned("xb")
                ahead(13)
                dve.wait_ge(pc_done, pieces_done(s, NPC - 1))
                dve.wait_ge(y_left, s + 1)
                nc.vector.tensor_copy(ybuf, ps[:, 3072:4096]).then_inc(y_evac, 1)

            dve.wait_ge(htok_ready, TT)
            nc.vector.drain().then_inc(w_split, MRING)
            nc.vector.drain().then_inc(eact_ready, G_EACT)
            nc.vector.drain().then_inc(y_evac, 1)
            for half in range(2):
                a = slice(4 * half, 4 * half + 4)
                tr_lo(xs_lo[:, a, :], xs_hi[:, a, :], 4 + TR_OF[("xa", "xb")[half]] % 2, half + 1, 4)
            for n in range(2):
                for h in range(2):
                    piece_lo(0, n, h)
            with dve.Fori(0, SLOTS - 1) as s:
                expert_lo(s, False)
            expert_lo(SLOTS - 1, True)

            for t in range(TT):
                dve.wait_ge(gathered[t % 2], 32 * (t // 2 + 1))
                y1, y2 = picked[:, t % 2, 0, :], picked[:, t % 2, 1, :]
                link(nc.vector.tensor_scalar(y2, y2, rv[:, 10, t:t + 1], None, ALU.mult))
                nc.vector.scalar_tensor_tensor(y1, y1, rv[:, 9, t:t + 1], y2, ALU.mult, ALU.add).then_inc(comb_ready, 1)
                m = MAIN[("comb", t)]
                dve.wait_ge(main_done, m + 1)
                g = 0 if t < TT - 1 else 1
                for k in range(KC):
                    ins = nc.vector.scalar_tensor_tensor(
                        x_t[:, k, t * P:(t + 1) * P], ps[:, 1024 * (m % 3) + k * P:1024 * (m % 3) + (k + 1) * P],
                        mod[:, 1, 40 + k, g:g + 1], x_t[:, k, t * P:(t + 1) * P], ALU.mult, ALU.add)
                ins.then_inc(x_upd, 1)
            dve.wait_ge(x_upd, 32 + TT)
            norm(4, DEPTH, 4 * DEPTH + 1, ("norm", DEPTH, "fin"))

        @block.tensor
        def _(pe):
            LAT, PRM = slice(0, N_LAT), slice(N_LAT, T)

            def claim_main(label):
                m = MAIN[label]
                if m >= 3:
                    name, val = MAIN_FREED[m - 3]
                    pe.wait_ge(sems[name], val)
                return main_pair(label)

            def claim_aux(label):
                n = AUX[label]
                if n >= 1:
                    name, val = AUX_FREED[n - 1]
                    pe.wait_ge(sems[name], val)
                return AUXP

            def arrived(p):
                n = PIECE_AT[p]
                pe.wait_ge(w_in_ring[n % RING], 16 * (n // RING + 1))
                return ring[:, n % RING, :]

            def both(out, lhs, rhs, start, stop):
                nc.tensor.matmul(out[:, LAT], lhs, rhs[:, LAT], start=start, stop=stop)
                return nc.tensor.matmul(out[:, PRM], lhs, rhs[:, PRM], start=start, stop=stop)

            def sum_square(l, kind, k, first, last):
                n = sq_at(l, kind, k)
                pe.wait_ge(sq_ready, n + 1)
                return both(AUXP, ones[:], sq[:, n % 2, :], first, last)

            pe.wait_ge(lam_prod_ready, 1)
            pe.wait_ge(zeroed, 2)
            lam_ps = claim_main(("lam",))
            nc.tensor.matmul(lam_ps[:, 0:4], ones[0:HD, :], lam_prod[:].rearrange("p l m -> p (l m)"),
                             start=True, stop=True).then_inc(main_done, 1)
            pe.wait_ge(cond_ready, 1)

            def ada(l, c, out):
                w = arrived(("ada", l, c))[:, 0:KC * 256].rearrange("p (k n) -> p k n", k=KC)
                for k in range(KC):
                    ins = nc.tensor.matmul(out, cond[:, k, :], w[:, k, :], start=k == 0, stop=k == KC - 1)
                return ins.then_inc(w_used, 1)

            def ada_turn(row, out, n):
                for j in range(n):
                    ins = nc.tensor.matmul(out[:, 2 * j:2 * j + 2], row[:, j * P:(j + 1) * P], ident[0:2, 0:2],
                                           start=True, stop=True)
                return ins

            for n in range(2):
                claim_main(("ada0", n))
                o = 1024 * (MAIN[("ada0", n)] % 3)
                for c in range(4):
                    ada(0, 4 * n + c, ps[0:2, o + 256 * c:o + 256 * c + 256])
                pe.drain().then_inc(main_done, 1)
            claim_main(("ada0t",))
            pe.wait_ge(ada_rows, 2)
            pe.wait_ge(const_in, 160)
            ada_turn(ada_row0, main_pair(("ada0t",)), 16).then_inc(main_done, 1)

            for l in range(DEPTH):
                if l == 0:
                    claim_aux(("norm", 0, "mix"))
                    for k in range(KC):
                        ins = sum_square(0, "mix", k, k == 0, k == KC - 1)
                        ins.then_inc(sq_used, 1)
                    pe.wait_ge(sq_used, 8)
                    pe.drain().then_inc(aux_done, 1)

                def split_sub(label):
                    q = SUB_AT[label]
                    pe.wait_ge(t_split, q + 1)
                    return sub_of(sub_hi, q), sub_of(sub_lo, q)

                def split_both(label, w, x_hi, x_lo, k0, k1, kn, ready=None):
                    w_hi_, w_lo_ = w
                    o = 1024 * (MAIN[label] % 3)
                    for k in range(k0, k1):
                        if ready:
                            pe.wait_ge(ready[0], ready[1] + k + 1)
                        for n, (a, b) in enumerate(((w_lo_, x_hi), (w_hi_, x_lo), (w_hi_, x_hi))):
                            for half in range(2):
                                ins = nc.tensor.matmul(ps[:, o + 512 * half:o + 512 * half + TH], a[:, k - k0, :],
                                                       b[:, k, TH * half:TH * half + TH],
                                                       start=k == 0 and n == 0, stop=k == kn - 1 and n == 2)
                    return ins

                def project(label, first=False):
                    claim_main(label)
                    split_both(label, split_sub(label), h_hi, h_lo, 0, KC, KC,
                               (h_split, 16 * l) if first else None).then_inc(main_done, 1)

                def rot(r):
                    rows = MQK if r in (0, 9, 10, 11, 12) else P
                    sw = swap_m if rows == MQK else swap_d
                    n = 13 * l + r
                    claim_aux(("rot", l, r))
                    pe.wait_ge(raw_ready, n + 1)
                    nc.tensor.matmul(AUXP[0:rows, LAT], sw[:], raw[0:rows, n % 2, LAT], start=True, stop=True).then_inc(aux_done, 1)

                project(("lora", l, 0), True)
                project(("lora", l, 1))
                project(("lora", l, 2))
                project(("rope", l, 0))
                claim_aux(("norm", l, "ckv"))
                sum_square(l, "lora", 0, True, True).then_inc(sq_used, 1)
                pe.drain().then_inc(aux_done, 1)
                project(("rope", l, 1))
                claim_aux(("norm", l, "cq"))
                for g in (1, 2):
                    sum_square(l, "lora", g, g == 1, g == 2).then_inc(sq_used, 1)
                pe.drain().then_inc(aux_done, 1)
                if l == 0:
                    pe.wait_ge(const_in, 160)
                project(("rope", l, 2))
                rot(0)
                for r in range(3, 9):
                    project(("rope", l, r))
                    rot(r - 2)
                for v in range(10):
                    half, t = v // TT, v % TT
                    claim_main(("vd", l, v))
                    out = main_pair(("vd", l, v))[:, 0:256]
                    for kh in range(2):
                        whi, wlo = split_sub(("vd", l, half, kh))
                        for k in range(4 * kh, 4 * kh + 4):
                            tile = slice(t * P, (t + 1) * P)
                            nc.tensor.matmul(out, h_lo[:, k, tile], whi[:, k % 4, :], start=k == 0, stop=False)
                            nc.tensor.matmul(out, h_hi[:, k, tile], wlo[:, k % 4, :], start=False, stop=False)
                            ins = nc.tensor.matmul(out, h_hi[:, k, tile], whi[:, k % 4, :], start=False, stop=k == KC - 1)
                    ins.then_inc(main_done, 1)
                    if v == 0:
                        rot(7)
                    if v == 1:
                        rot(8)

                def attention(f):
                    base = (2 * l + f) * ITEMS

                    def item(i):
                        h, qt = i // TT, i % TT
                        lat = qt < TT - 1
                        return base + i, (base + i) % 2, h, qt, lat

                    def scores(i):
                        it, b, h, qt, lat = item(i)
                        if it >= 2:
                            pe.wait_ge(exp_done, it - 1)
                        if i >= 2 and (i - 2) % TT == TT - 1:
                            pe.wait_ge(late_rows, 8 * l + 4 * f + (i - 2) // TT + 1)
                        o = 1536 * b
                        rows = [(0, HD), (HD, P)] if f == 0 else [(0, MQK)]
                        for m, (r0, r1) in enumerate(rows):
                            q = q_t[r0:r1, h, qt * P:(qt + 1) * P]
                            if lat:
                                parts = ((512, 768), (0, 512)) if m == 0 else ((256, 768), (0, 256))
                                for n, (a, z) in enumerate(parts):
                                    if m == 1 and n == 1:
                                        pe.wait_ge(mid_bank, (4 * l + h) * (TT - 1) + qt + 1)
                                    ins = nc.tensor.matmul(ps[:, o + 768 * m + a:o + 768 * m + z], q, k_t[r0:r1, h, a:z],
                                                           start=True, stop=True)
                                    if f == 0 and m == 0 and n == 0:
                                        ins.then_inc(mid_bank, 1)
                            else:
                                ins = nc.tensor.matmul(ps[:, o + 768 * m:o + 768 * m + P], q, k_t[r0:r1, h, LAT_KEYS:NKEY],
                                                       start=True, stop=True)
                        ins.then_inc(scores_done, 1)

                    def turn(h):
                        u = 4 * f + h
                        pe.wait_ge(late_rows, 8 * l + u + 1)
                        ada_turn(ada_row, ps[:, 3968:4096], 2 * len(ada_after_head(l, u))).then_inc(ada_done, 1)

                    def transposes(i):
                        it, b, h, qt, lat = item(i)
                        pe.wait_ge(p_ready, it + 1)
                        if it:
                            pe.wait_ge(pt_a_ready, it)
                        for k in range(4 if lat else 1):
                            ins = nc.tensor.matmul(ps[:, 3072 + k * P:3072 + (k + 1) * P], e_buf[:, b, 0, k * P:(k + 1) * P], diag[:, b, :],
                                                   start=True, stop=True)
                        ins.then_inc(tr_a_done, 1)
                        if it:
                            pe.wait_ge(pv_evac, it)
                        if qt == TT - 1:
                            for n, (ll, c) in enumerate(ada_after_head(l, 4 * f + h)):
                                ada(ll, c, ps[0:2, 1536 * b + 512 * n:1536 * b + 512 * n + 256])
                            pe.drain().then_inc(late_rows_done, 1)
                        if qt == 0 and h:
                            turn(h - 1)
                        if lat:
                            if qt == 0 and h:
                                pe.wait_ge(mod_late, 8 * l + 4 * f + h)
                            for k in range(4, 6):
                                ins = nc.tensor.matmul(ps[:, 3584 + (k - 4) * P:3584 + (k - 3) * P], e_buf[:, b, 0, k * P:(k + 1) * P],
                                                       diag[:, b, :], start=True, stop=True)
                            ins.then_inc(tr_b_done, 1)

                    def values(i):
                        it, b, h, qt, lat = item(i)
                        pe.wait_ge(pt_a_ready, it + 1)
                        if lat:
                            pe.wait_ge(pt_b_ready, n_tr_b(it))
                        if it:
                            pe.wait_ge(pv_evac, it)
                        kts = range(6) if lat else (KT - 1,)
                        for n, kt in enumerate(kts):
                            ins = nc.tensor.matmul(ps[:, 3840:3968], v_n[:, kt, h * P:(h + 1) * P], pt_buf[:, b, n, :],
                                                   start=n == 0, stop=n == len(kts) - 1)
                        ins.then_inc(pv_done, 1)

                    scores(0)
                    for i in range(ITEMS):
                        if i + 1 < ITEMS:
                            scores(i + 1)
                        if i:
                            values(i - 1)
                        transposes(i)
                    values(ITEMS - 1)
                    pe.wait_ge(pv_evac, base + ITEMS)
                    turn(HEADS - 1)
                    pe.wait_ge(mod_late, 8 * l + 4 * f + HEADS)

                pe.wait_ge(rope_done, 13 * l + 9)
                pe.wait_ge(vd_ready, 10 * l + 10)
                pe.wait_ge(cache_k_in, 16 * (l + 1))
                pe.wait_ge(cache_v_in, 16 * (l + 1))
                pe.wait_ge(rot_used, 13 * l + 9)
                attention(0)

                pe.wait_ge(pv_evac, (2 * l + 1) * ITEMS)
                pe.wait_ge(exp_done, (2 * l + 1) * ITEMS)
                for h in range(HEADS):
                    claim_aux(("norm", l, "head", h))
                    sum_square(l, "head", h, True, True).then_inc(sq_used, 1)
                    pe.drain().then_inc(aux_done, 1)
                    out = claim_main(("rope", l, 9 + h))
                    pe.wait_ge(lat_normed, 2 * l + 2)
                    for k in range(2):
                        ins = both(out[0:MQK], wuq[:, k, h * MQK:(h + 1) * MQK], cq_t[:, k, :], k == 0, k == 1)
                    ins.then_inc(main_done, 1)
                    if h:
                        rot(8 + h)
                rot(12)
                pe.wait_ge(cache_c_in, 16 * N_CACHE_C * (l + 1))
                for h in range(HEADS):
                    claim_main(("uk", l, h))
                    o = 1024 * (MAIN[("uk", l, h)] % 3)
                    for c in range(2):
                        ins = nc.tensor.matmul(ps[0:NOPE, o + 512 * c:o + 512 * c + 448], wuk[:, h * NOPE:(h + 1) * NOPE],
                                               ckv_t[:, 448 * c:448 * c + 448], start=True, stop=True)
                    ins.then_inc(main_done, 1)
                for v in range(KT):
                    o = 1024 * (MAIN[("uv", l, v)] % 3)
                    claim_main(("uv", l, v))
                    nc.tensor.matmul(ps[:, o:o + 512], ckv_t[:, v * P:(v + 1) * P], wuv, start=True, stop=True).then_inc(main_done, 1)
                pe.wait_ge(rope_done, 13 * l + 13)
                pe.wait_ge(vm_ready, KT * (l + 1))
                pe.wait_ge(km_ready, 4 * (l + 1))
                pe.wait_ge(kr_spread, 4 * (l + 1))
                attention(1)

                pe.wait_ge(pv_evac, (2 * l + 2) * ITEMS)
                pe.wait_ge(exp_done, (2 * l + 2) * ITEMS)
                claim_aux(("norm", l, "ffn"))
                for d_ in range(KC):
                    claim_main(("o", l, d_))
                    split_both(("o", l, d_), split_sub(("o", l, d_)), h_hi, h_lo, 0, KC, KC,
                               (mixed_split, 8 * l) if d_ == 0 else None).then_inc(main_done, 1)
                    if d_ >= 2:
                        sum_square(l, "ffn", d_ - 2, d_ == 2, False).then_inc(sq_used, 1)
                for d_ in (KC - 2, KC - 1):
                    sum_square(l, "ffn", d_, False, d_ == KC - 1).then_inc(sq_used, 1)
                pe.drain().then_inc(aux_done, 1)

                if l == 0:
                    for half, js in enumerate(FF_HALF):
                        for j in js:
                            for u in ("gate", "up"):
                                claim_main((u, j))
                                split_both((u, j), split_sub((u, j)), h_hi, h_lo, 0, KC, KC,
                                           (h_split, 8) if (u, j) == ("gate", 0) else None).then_inc(main_done, 1)
                        if half:
                            claim_aux(("norm", 1, "mix"))
                        kn = len(js)
                        for d_ in range(KC):
                            claim_main(("down", half, d_))
                            for part in range(2):
                                w = split_sub(("down", half, d_, part))
                                ins = split_both(("down", half, d_), w, hid_hi, hid_lo, part * kn // 2, (part + 1) * kn // 2,
                                                 kn, (hid_ready, js[0]) if d_ == 0 else None)
                                ins.then_inc(main_done if part else down_first, 1)
                            if half and d_ >= 2:
                                sum_square(1, "mix", d_ - 2, d_ == 2, False).then_inc(sq_used, 1)
                    for d_ in (KC - 2, KC - 1):
                        sum_square(1, "mix", d_, False, d_ == KC - 1).then_inc(sq_used, 1)
                    pe.drain().then_inc(aux_done, 1)

            claim_aux(("router",))
            for k in range(KC):
                pe.wait_ge(h_ready, 24 + k + 1)
            for t in range(TT):
                for k in range(KC):
                    ins = nc.tensor.matmul(AUXP[:, t * NE:(t + 1) * NE], h_t[:, k, t * P:(t + 1) * P], router_w[:, k, :],
                                           start=k == 0, stop=k == KC - 1)
            ins.then_inc(aux_done, 1)

            def htok_rows(t):
                claim_main(("htok", t))
                o = 1024 * (MAIN[("htok", t)] % 3)
                for k in range(KC):
                    ins = nc.tensor.transpose(ps[:, o + k * P:o + (k + 1) * P], h_t[:, k, t * P:(t + 1) * P], ident[:])
                ins.then_inc(main_done, 1)

            for t in range(3):
                htok_rows(t)
            claim_aux(("rank",))
            pe.wait_ge(sel_ready, 1)
            for t in range(TT):
                for tt in range(t):
                    nc.tensor.matmul(AUXP[:, t * NE:(t + 1) * NE], ones[:], rt[:, 4, tt, :], start=tt == 0, stop=False)
                nc.tensor.matmul(AUXP[:, t * NE:(t + 1) * NE], before[:], rt[:, 4, t, :], start=t == 0, stop=True)
            for t in range(TT):
                ins = nc.tensor.matmul(AUXP[:, TT * NE:TT * NE + NE], ones[:], rt[:, 4, t, :], start=t == 0, stop=t == TT - 1)
            ins.then_inc(aux_done, 1)
            for t in range(3, TT):
                htok_rows(t)

            pe.wait_ge(htok_ready, TT)
            pe.wait_ge(rank_ready, 1)

            def x_transposes(half):
                bank = 4 + TR_OF[("xa", "xb")[half]] % 2
                for k in range(4):
                    ins = nc.tensor.transpose(ps[:, 512 * bank + k * P:512 * bank + (k + 1) * P],
                                              xs[:, (4 * half + k) * P:(4 * half + k + 1) * P], ident[:])
                return ins

            pe.drain().then_inc(pc_done, SPLITS)
            pe.wait_ge(xs_in, 16)
            for half in range(2):
                x_transposes(half).then_inc(etr_done, 1)
            pe.drain().then_inc(etr_done, G_ETR)

            def split_product(out, a_hi, a_lo, b_hi, b_lo, start, stop):
                nc.tensor.matmul(out, a_lo, b_hi, start=start, stop=False)
                nc.tensor.matmul(out, a_hi, b_lo, start=False, stop=False)
                return nc.tensor.matmul(out, a_hi, b_hi, start=False, stop=stop)

            with pe.Fori(0, SLOTS) as s:
                def tr(c):
                    j = TR_OF[c]
                    bank = 4 + j % 2
                    pe.wait_ge(etr_evac, 6 * s + j + 1)
                    if c == "xa":
                        pe.wait_ge(xs_in, 16 * (s + 2))
                    if c in ("xa", "xb"):
                        x_transposes(j - TR_OF["xa"]).then_inc(etr_done, 1)
                        return
                    pe.wait_ge(eact_ready, G_EACT + 4 * s + c + 1)
                    for n, k in enumerate(range(*BLK[c])):
                        ins = nc.tensor.transpose(ps[:, 512 * bank + n * P:512 * bank + (n + 1) * P],
                                                  eact[:, k * P:(k + 1) * P], ident[:])
                    ins.then_inc(etr_done, 1)

                def split_piece(n):
                    pe.wait_ge(w_split, MRING + NPC * s + n + 1)
                    k = KC if n < NGU else FCE
                    return (w_hi[:, n % SPLITS, :].rearrange("p (k n) -> p k n", k=k),
                            w_lo[:, n % SPLITS, :].rearrange("p (k n) -> p k n", k=k))

                def gate_up(n):
                    if n % 2 == 0:
                        pe.wait_ge(eact_ready, 4 * s + n // 2 + 1)
                    if n == 0:
                        pe.wait_ge(etr_evac, 6 * s + 2)
                    hi, lo = split_piece(n)
                    for k in range(KC):
                        ins = split_product(ps[:, 512 * (n % 4):512 * (n % 4) + HCH], xs_hi[:, k, :], xs_lo[:, k, :],
                                            hi[:, k, :], lo[:, k, :], k == 0, k == KC - 1)
                    ins.then_inc(pc_done, 1)

                def down(n, blocks, hi, lo):
                    c = 3072 + DCH * (n - NGU)
                    for k in range(*blocks):
                        ins = split_product(ps[:, c:c + DCH], ea_hi[:, k, :], ea_lo[:, k, :], hi[:, k, :], lo[:, k, :],
                                            k == 0, k == FCE - 1)
                    return ins

                for n in range(3):
                    gate_up(n)
                tr(0)
                gate_up(3)
                gate_up(4)
                tr(1)
                gate_up(5)
                gate_up(6)
                tr(2)
                gate_up(7)
                pe.wait_ge(y_evac, s + 1)
                hi, lo = split_piece(8)
                pe.wait_ge(etr_evac, 2 + 6 * s + TR_OF[1] + 1)
                down(8, (0, 5), hi, lo)
                tr(3)
                pe.wait_ge(etr_evac, 2 + 6 * s + TR_OF[2] + 1)
                down(8, (5, 8), hi, lo)
                pe.wait_ge(etr_evac, 2 + 6 * s + TR_OF[3] + 1)
                down(8, (8, 11), hi, lo).then_inc(pc_done, 1)
                tr("xa")
                for n in range(9, NPC):
                    hi, lo = split_piece(n)
                    down(n, (0, FCE), hi, lo).then_inc(pc_done, 1)
                    if n == 9:
                        tr("xb")

            pe.wait_ge(y_evac, SLOTS + 1)
            for t in range(TT):
                claim_main(("comb", t))
                o = 1024 * (MAIN[("comb", t)] % 3)
                pe.wait_ge(comb_ready, t + 1)
                for k in range(KC):
                    ins = nc.tensor.transpose(ps[:, o + k * P:o + (k + 1) * P], picked[:, t % 2, 0, k * P:(k + 1) * P], ident[:])
                ins.then_inc(main_done, 1)
            claim_aux(("norm", DEPTH, "fin"))
            for k in range(KC):
                sum_square(DEPTH, "fin", k, k == 0, k == KC - 1).then_inc(sq_used, 1)
            pe.drain().then_inc(aux_done, 1)


def constants():
    t = np.arange(N_LAT)
    rows, cols = (t // GRID_W).astype(np.float32), (t % GRID_W).astype(np.float32)

    def axial(width):
        half = width // 4
        freqs = np.float32(THETA) ** (-np.arange(half, dtype=np.float32) / np.float32(half))
        cos, sin, partner = [], [], []
        for block, pos in enumerate((rows, cols)):
            for side in range(2):
                for j in range(half):
                    ang = pos * freqs[j]
                    cos.append(np.cos(ang))
                    sin.append(np.sin(ang) * (-1.0, 1.0)[side])
                    partner.append(block * 2 * half + (1 - side) * half + j)
        return np.array(cos, np.float32), np.array(sin, np.float32), partner

    def swap(partner):
        m = np.zeros((len(partner),) * 2, np.float32)
        m[partner, np.arange(len(partner))] = 1.0
        return m

    c, s, p = axial(HD)
    out = {"cos_d": np.concatenate([c, c]), "sin_d": np.concatenate([s, s]),
           "swap_d": swap(p + [HD + i for i in p])}
    c, s, p = axial(ROPE)
    out["cos_m"] = np.concatenate([np.ones((NOPE, N_LAT), np.float32), c])
    out["sin_m"] = np.concatenate([np.zeros((NOPE, N_LAT), np.float32), s])
    out["swap_m"] = swap(list(range(NOPE)) + [NOPE + i for i in p])
    out["ident"] = np.eye(P, dtype=np.float32)
    out["before"] = np.triu(np.ones((P, P), np.float32), 1)
    small = np.concatenate([np.tril(np.ones((NE, NE)), -1).ravel(), np.arange(TT) * P, np.arange(SLOTS) * P])
    out["small"] = np.broadcast_to(small.astype(np.float32), (P, small.size)).copy()
    return out


_WEIGHTS = ["w_ada", "w_in", "w_uq", "w_uk", "w_uv", "w_o", "w_gate", "w_up", "w_down", "router",
            "moe_w_gate", "moe_w_up", "moe_w_down"]
_OUTS = {"y_t": (P, KC, T), "new_k": (DEPTH, P, HEADS, N_PROMPT), "new_v": (DEPTH, N_PROMPT, HEADS * P),
         "new_ckv": (DEPTH, P, N_PROMPT), "new_kr": (DEPTH, ROPE, N_PROMPT)}


def layout(x):
    def col(a):
        return np.ascontiguousarray(a.reshape(-1, P).T)

    a = {n: x[n] for n in _WEIGHTS}
    tokens = np.concatenate([x["x_sample"][0], x["x_prompt"][0]], axis=0)
    a["x_t"] = tokens.T.reshape(KC, P, T).transpose(1, 0, 2)
    a["cond"] = np.stack([col(x["c"][0]), col(x["c_ctx"])], axis=2)
    a["vecs"] = np.concatenate([col(x[n].reshape(-1)) for n in
                                ("b_ada", "norm_mix_g", "norm_ffn_g", "final_norm_g", "mla_q_norm_g",
                                 "mla_kv_norm_g", "diff_subln_g")], axis=1)
    lam = np.stack([np.stack([x["diff_lq1"], x["diff_lk1"]], -1), np.stack([x["diff_lq2"], x["diff_lk2"]], -1)], 2)
    a["lam"] = lam.transpose(1, 0, 2, 3)
    a["cache_k"] = x["cache_diff_k"][0].transpose(0, 3, 2, 1)
    v = x["cache_diff_v"][0].reshape(DEPTH, PAST // P, P, HEADS * P)
    a["cache_v"] = v.transpose(0, 2, 1, 3)
    a["cache_ckv"] = x["cache_mla_ckv"][0].transpose(0, 2, 1)
    a["cache_kr"] = x["cache_mla_krope"][0].transpose(0, 2, 1)
    return a


def kernel(**inputs):
    import concourse.bacc as _bacc
    from concourse.bass_utils import run_bass_kernel_spmd as _run

    nc = _bacc.Bacc("TRN2", target_bir_lowering=False, num_devices=1)
    arrays = {}
    aps = {}
    laid = layout({n: np.asarray(v) for n, v in inputs.items()})
    for name, a in {**laid, **constants()}.items():
        a = np.ascontiguousarray(a)
        arrays[f"in_{name}"] = a
        aps[name] = nc.dram_tensor(f"in_{name}", a.shape, mybir.dt.from_np(a.dtype), kind="ExternalInput").ap()
    for name, shape in _OUTS.items():
        aps[name] = nc.dram_tensor(f"out_{name}", shape, mybir.dt.float32, kind="ExternalOutput").ap()
    build(nc, aps)
    r = _run(nc, [arrays], core_ids=[0]).results[0]
    y = np.asarray(r["out_y_t"]).transpose(2, 1, 0).reshape(T, D_MODEL)
    new_k = np.asarray(r["out_new_k"]).transpose(0, 3, 2, 1)[None]
    new_v = np.asarray(r["out_new_v"]).reshape(1, DEPTH, N_PROMPT, HEADS, P)
    new_ckv = np.asarray(r["out_new_ckv"]).transpose(0, 2, 1)[None]
    new_kr = np.asarray(r["out_new_kr"]).transpose(0, 2, 1)[None]
    return (np.ascontiguousarray(y[N_LAT:])[None], np.ascontiguousarray(y[:N_LAT])[None],
            np.ascontiguousarray(new_k), np.ascontiguousarray(new_v), np.ascontiguousarray(new_ckv),
            np.ascontiguousarray(new_kr))
```

```python
import math
from contextlib import ExitStack

import numpy as np

import concourse.bass as bass
from concourse import mybir

P = 128
D_MODEL, KC = 1024, 8
N_LAT, N_PROMPT = 512, 128
T = N_LAT + N_PROMPT
TT = T // P
PAST = 256
NKEY = PAST + T
KT = NKEY // P
LAT_KEYS = PAST + N_LAT
DEPTH = 2
HEADS, HD = 4, 64
QL, KVL, ROPE, NOPE = 256, 128, 32, 64
MQK = NOPE + ROPE
D_FF, FC = 2816, 22
NE, D_FFE, FCE = 8, 1408, 11
SLOTS = 17
XTILES = SLOTS + 2
GRID_W, THETA, EPS = 64, 10000.0, 1e-6
D_SCALE, M_SCALE = HD ** -0.5, MQK ** -0.5
ITEMS = HEADS * TT

V_BADA, V_MIX, V_FFN, V_FIN, V_QN, V_KVN, V_SUB = 0, 96, 112, 128, 136, 140, 142
NV = 144

RING, RING_F = 3, 2048
SUBS_KEPT, SUB_F = 2, 1024
TH = T // 2
FF_HALF = (range(0, 12), range(12, FC))
MRING, PIECE_F = 4, 2816
SPLITS = 3
NPC, NGU, HCH, DCH = 12, 8, 352, 256
BLK = [(0, 2), (2, 5), (5, 8), (8, 11)]


def lam_init(l):
    return 0.8 - 0.6 * math.exp(-0.3 * l)


def weight_pieces():
    out = []
    for c in range(8):
        out.append(("ada", 0, c))
    rest = [("ada", 0, c) for c in range(8, 24)] + [("ada", 1, c) for c in range(8)]
    late = [("ada", 1, c) for c in range(8, 24)]
    for l in range(DEPTH):
        out += [("in", l, 1792, 128), ("in", l, 1536, 256)]
        out += [("in", l, c, 256) for c in (512, 768, 0, 256, 1024, 1280)]
        for u in range(8):
            out += rest[3 * u:3 * u + 3] if l == 0 else late[2 * u:2 * u + 2]
        out += [("o", l, c) for c in range(4)]
        if l == 0:
            for half, js in enumerate(FF_HALF):
                for j in js[::2]:
                    out += [("gate", j // 2), ("up", j // 2)]
                out += [("down", half, d) for d in range(KC)]
    return out


PIECES = weight_pieces()
PIECE_AT = {p: n for n, p in enumerate(PIECES)}


def ada_after_head(l, u):
    if l == 0:
        a = [(0, c) for c in range(8, 24)] + [(1, c) for c in range(8)]
        return a[3 * u:3 * u + 3]
    return [(1, c) for c in range(8 + 2 * u, 10 + 2 * u)]


def ada_owners():
    own = {(0, c): "pe" for c in range(8)}
    for l in range(DEPTH):
        for u in range(2 * HEADS):
            todo = ada_after_head(l, u)
            for p, e in zip(todo, ("pe", "dve", "pool")[-len(todo):]):
                own[p] = e
    return own


ADA_OWNER = ada_owners()


SQ_LAYER = [("mix", k) for k in range(8)] + [("lora", k) for k in range(3)] \
    + [("head", k) for k in range(4)] + [("ffn", k) for k in range(8)]


def sq_at(l, kind, k):
    if l == DEPTH:
        return DEPTH * len(SQ_LAYER) + k
    return l * len(SQ_LAYER) + SQ_LAYER.index((kind, k))


def plan():
    main, aux = {}, {}
    main_freed, aux_freed = [], []

    def m(label, sem, val):
        main[label] = len(main_freed)
        main_freed.append((sem, val))

    def x(label, sem, val):
        aux[label] = len(aux_freed)
        aux_freed.append((sem, val))

    m(("lam",), "lam_exp", 1)
    m(("ada0", 0), "ada_rows", 1)
    m(("ada0", 1), "ada_rows", 2)
    m(("ada0t",), "mod_ready", 1)
    for l in range(DEPTH):
        x(("norm", l, "mix"), "var_ready", 4 * l + 1)
        for g in range(3):
            m(("lora", l, g), "lora_ready", 3 * l + g + 1)
        for r in range(9):
            m(("rope", l, r), "raw_ready", 13 * l + r + 1)
        x(("norm", l, "ckv"), "var_ready", 4 * l + 2)
        x(("norm", l, "cq"), "var_ready", 4 * l + 3)
        for r in range(9):
            x(("rot", l, r), "rot_used", 13 * l + r + 1)
        for v in range(2 * TT - 2):
            m(("vd", l, v), "vd_ready", 10 * l + v + 1)
        x(("vd tail", l), "vd_ready", 10 * l + 10)
        for h in range(4):
            x(("norm", l, "head", h), "hvar_ready", 4 * l + h + 1)
            if h:
                x(("rot", l, 8 + h), "rot_used", 13 * l + 9 + h)
        x(("rot", l, 12), "rot_used", 13 * l + 13)
        for r in range(9, 13):
            m(("rope", l, r), "raw_ready", 13 * l + r + 1)
        for h in range(4):
            m(("uk", l, h), "km_ready", 4 * l + h + 1)
        for v in range(KT - 2):
            m(("uv", l, v), "vm_ready", KT * l + v + 1)
        x(("uv tail", l), "vm_ready", KT * (l + 1))
        for d in range(KC):
            m(("o", l, d), "x_upd", (24 if l else 0) + d + 1)
        x(("norm", l, "ffn"), "var_ready", 4 * l + 4)
        if l == 0:
            for half, js in enumerate(FF_HALF):
                for j in js:
                    m(("gate", j), "silu_ready", j + 1)
                    m(("up", j), "hid_product", j + 1)
                for d in range(KC):
                    m(("down", half, d), "x_upd", 8 + 8 * half + d + 1)
        else:
            x(("router",), "lg_ready", 1)
            for t in range(TT):
                m(("htok", t), "htok_ready", t + 1)
            x(("rank",), "rank_ready", 1)
            for t in range(TT):
                m(("comb", t), "x_upd", 32 + t + 1)
    x(("norm", DEPTH, "fin"), "var_ready", 4 * DEPTH + 1)
    return main, aux, main_freed, aux_freed


MAIN, AUX, MAIN_FREED, AUX_FREED = plan()


def sub_pieces():
    subs, labels = [], []
    n_first = 0

    def add(label, piece, ks, cs, group, sem="main_done"):
        labels.append(label)
        value = {"main_done": MAIN, "aux_done": AUX}[sem][group] + 1 if sem != "down_first" else group
        subs.append((piece, ks, cs, (sem, value)))

    for l in range(DEPTH):
        add(("lora", l, 0), ("in", l, 1792, 128), (0, KC), (0, P), ("lora", l, 0))
        for g in (1, 2):
            add(("lora", l, g), ("in", l, 1536, 256), (0, KC), ((g - 1) * P, g * P), ("lora", l, g))
        add(("rope", l, 0), None, (0, KC), (0, P), ("rope", l, 0))
        for r in range(1, 9):
            c = (512, 768, 0, 256)[(r - 1) // 2]
            o = (r - 1) % 2 * P
            add(("rope", l, r), ("in", l, c, 256), (0, KC), (o, o + P), ("rope", l, r))
        for half in range(2):
            for kh in range(2):
                add(("vd", l, half, kh), ("in", l, 1024 + 256 * half, 256), (4 * kh, 4 * kh + 4), (0, 256),
                    *((("vd tail", l), "aux_done") if half else (("vd", l, TT - 1),)))
        for d in range(KC):
            add(("o", l, d), ("o", l, d // 2), (0, KC), (d % 2 * P, d % 2 * P + P), ("o", l, d))
        if l == 0:
            for half, js in enumerate(FF_HALF):
                for j in js:
                    for u in ("gate", "up"):
                        add((u, j), (u, j // 2), (0, KC), (j % 2 * P, j % 2 * P + P), (u, j))
                kn = len(js) // 2
                for d in range(KC):
                    n_first += 1
                    add(("down", half, d, 0), ("down", half, d), (0, kn), (0, P), n_first, "down_first")
                    add(("down", half, d, 1), ("down", half, d), (kn, 2 * kn), (0, P), ("down", half, d))
    return subs, {label: n for n, label in enumerate(labels)}


SUBS, SUB_AT = sub_pieces()


def piece_freed(n):
    if PIECES[n][0] == "ada":
        e = ADA_OWNER[PIECES[n][1:]]
        return {"pe": "w_used", "dve": "w_summed_v", "pool": "w_summed_g"}[e], \
            sum(p[0] == "ada" and ADA_OWNER[p[1:]] == e for p in PIECES[:n + 1])
    return "t_split", max(q for q, sub in enumerate(SUBS) if sub[0] == PIECES[n]) + 1


def n_tr_b(it):
    n = it + 1
    return (n // TT) * (TT - 1) + min(n % TT, TT - 1)


def build(nc, d):
    f32, i32, u32 = mybir.dt.float32, mybir.dt.int32, mybir.dt.uint32
    ACT, ALU, AXX = mybir.ActivationFunctionType, mybir.AluOpType, mybir.AxisListType.X

    xperm = nc.dram_tensor("xperm", (XTILES * P, D_MODEL), f32).ap()
    yslots = nc.dram_tensor("yslots", (SLOTS * P, D_MODEL), f32).ap()

    w_ada = d["w_ada"].rearrange("l (k p) n -> l p k n", p=P)
    w_in = d["w_in"].rearrange("l (k p) n -> l p k n", p=P)
    w_o = d["w_o"].rearrange("l (k p) n -> l p k n", p=P)
    w_gate = d["w_gate"].rearrange("l (k p) n -> l p k n", p=P)
    w_up = d["w_up"].rearrange("l (k p) n -> l p k n", p=P)
    w_down = d["w_down"].rearrange("l (k p) n -> l p k n", p=P)
    m_gate = d["moe_w_gate"].rearrange("m e (k p) n -> p (m e k) n", p=P)
    m_up = d["moe_w_up"].rearrange("m e (k p) n -> p (m e k) n", p=P)
    m_down = d["moe_w_down"].rearrange("m e (k p) n -> p (m e k) n", p=P)

    ctx = ExitStack()
    with ctx:
        def sb(name, shape, dt=f32):
            return ctx.enter_context(nc.sbuf_tensor(name, shape, dt))

        sems = {}

        def sem(name):
            sems[name] = ctx.enter_context(nc.semaphore(name))
            return sems[name]

        x_t = sb("x_t", [P, KC, T])
        vecs = sb("vecs", [P, NV])
        mod = sb("mod", [P, DEPTH, 48, 2])
        gain = sb("gain", [P, DEPTH, 2, KC, 2])
        cond = sb("cond", [P, KC, 2])
        lam_in = sb("lam_in", [HD, DEPTH, 2, 2])
        lam_prod = sb("lam_prod", [HD, DEPTH, 2])
        lam_e = sb("lam_e", [P, DEPTH, 2])
        neg_lam = sb("neg_lam", [P, DEPTH])
        subg = sb("subg", [P, DEPTH])
        cos_d, sin_d = sb("cos_d", [P, N_LAT]), sb("sin_d", [P, N_LAT])
        cos_m, sin_m = sb("cos_m", [MQK, N_LAT]), sb("sin_m", [MQK, N_LAT])
        swap_d, swap_m = sb("swap_d", [P, P]), sb("swap_m", [MQK, MQK])
        ident, ones, before = sb("ident", [P, P]), sb("ones", [P, P]), sb("before", [P, P])
        small = sb("small", [P, 64 + 5 + SLOTS])
        tri8 = small[:, 0:64].rearrange("p (a b) -> p a b", a=8)
        steps = small[:, 64:69]
        slot_rows = small[:, 69:69 + SLOTS]
        sq = sb("sq", [P, 2, T])
        rb = sb("rb", [P, T])
        stat = sb("stat", [P, 2, 12])
        diag = sb("diag", [P, 2, P])
        ada_row = sq[0:2].rearrange("p s n -> p (s n)")[:, 0:3 * 256]
        zeros = sb("zeros", [P, D_MODEL // 2])
        router_w = sb("router_w", [P, KC, NE])
        lg = sb("lg", [P, TT, NE])
        rt = sb("rt", [P, 8, TT, NE])
        rv = sb("rv", [P, 12, TT])
        cnt = sb("cnt", [P, 4, NE])
        rowi = sb("rowi", [P, 2, TT], u32)
        slot_e = sb("slot_e", [P, SLOTS])
        slot_i = sb("slot_i", [P, SLOTS], i32)

        SMALL_W = 2 * 384 + 256 + 512 + KC * P
        ATT = 4 * NKEY + 4 * T + 4 * NKEY + NKEY + 2 * T + NKEY + 4 * LAT_KEYS + 2 * LAT_KEYS
        AR = ATT + 2 * 512 + RING * RING_F + SMALL_W + KC * T + 2 * SUBS_KEPT * SUB_F
        HT = KC * T
        zone_at = (nc.sbuf_base + 31) // 32 * 32
        zone = sb("zone", [P, HT + AR])
        h_t = zone[:, 0:HT].rearrange("p (k n) -> p k n", k=KC)
        mixed = h_t
        arena = zone[:, HT:HT + AR]
        at = [0]

        def cut(n, pat=None, **kw):
            a = arena[:, at[0]:at[0] + n]
            at[0] += n
            return a.rearrange(pat, **kw) if pat else a

        k_t = cut(4 * NKEY, "p (h n) -> p h n", h=4)
        q_t = cut(4 * T, "p (h n) -> p h n", h=4)
        v_n = cut(4 * NKEY, "p (t n) -> p t n", t=KT)
        ckv_t = cut(NKEY)
        cq_t = cut(2 * T, "p (c n) -> p c n", c=2)
        kr_t = cut(NKEY)
        e_buf = cut(4 * LAT_KEYS, "p (s m n) -> p s m n", s=2, m=2)
        pt_buf = cut(2 * LAT_KEYS, "p (s k n) -> p s k n", s=2, k=6)
        rtmp = cut(1024, "p (s n) -> p s n", s=2)
        ring = cut(RING * RING_F, "p (s n) -> p s n", s=RING)
        wuq = cut(2 * 384, "p (k n) -> p k n", k=2)
        wuk = cut(256)
        wuv = cut(512)
        wkr = cut(KC * P, "p (k n) -> p k n", k=KC)
        h_split_at, sub_at = at[0], at[0] + KC * T
        ada_row0 = e_buf.rearrange("p s m n -> p (s m n)")[0:2, 0:2048]
        e_at = 4 * NKEY + 4 * T + 4 * NKEY + NKEY + 2 * T + NKEY
        lora_raw = arena[:, e_at:e_at + 3 * T].rearrange("p (c n) -> p c n", c=3)
        pt_at = e_at + 4 * LAT_KEYS
        raw = arena[:, pt_at:pt_at + 2 * T].rearrange("p (s n) -> p s n", s=2)
        sil = sq
        cmp_a, cmp_b = (arena[:, sub_at + i * TT * NE * NE:sub_at + (i + 1) * TT * NE * NE].rearrange(
            "p (t a b) -> p t a b", t=TT, a=NE) for i in range(2))
        f32r = mybir.dt.float32r

        hrb = arena[:, h_split_at + 4 * T:h_split_at + 8 * T].rearrange("p (c n) -> p c n", c=4)

        part_v, part_g = (arena[:, sub_at + 3072 + 512 * i:sub_at + 3584 + 512 * i].rearrange("p (g n) -> p g n", g=2) for i in range(2))
        part_prod = arena[:, sub_at + 1024:sub_at + 3072].rearrange("p (k n) -> p k n", k=KC)

        def split_at(name, shape, el):
            return nc.alloc_sbuf_tensor_at(name, shape, f32r, offset=zone_at + 4 * (HT + el))

        h_lo = split_at("h_lo", [P, KC, T], -HT)
        h_hi = split_at("h_hi", [P, KC, T], h_split_at)
        sub_hi = split_at("sub_hi", [P, SUBS_KEPT, SUB_F], sub_at)
        sub_lo = split_at("sub_lo", [P, SUBS_KEPT, SUB_F], sub_at + SUBS_KEPT * SUB_F)
        HJ = len(FF_HALF[0])
        hid_hi = split_at("hid_hi", [P, HJ, T], 0)
        hid_lo = split_at("hid_lo", [P, HJ, T], HJ * T)
        assert 2 * HJ * T <= ATT
        at[0] = 0

        def zcut(n, pat=None, **kw):
            a = zone[:, at[0]:at[0] + n]
            at[0] += n
            return a.rearrange(pat, **kw) if pat else a

        def zsplit(name, shape, dt=f32r):
            n = int(np.prod(shape[1:]))
            a = nc.alloc_sbuf_tensor_at(name, shape, dt, offset=zone_at + 4 * at[0])
            at[0] += n
            return a

        mraw = zsplit("mraw", [P, MRING, PIECE_F], f32)
        htok = zone[:, at[0]:at[0] + TT * D_MODEL].rearrange("p (t n) -> p t n", t=TT)
        w_hi = zsplit("w_hi", [P, SPLITS, PIECE_F])
        w_lo = zsplit("w_lo", [P, SPLITS, PIECE_F])
        xs_hi, xs_lo = zsplit("xs_hi", [P, KC, P]), zsplit("xs_lo", [P, KC, P])
        ea_hi, ea_lo = zsplit("ea_hi", [P, FCE, P]), zsplit("ea_lo", [P, FCE, P])
        xs = zcut(D_MODEL)
        eact = zcut(D_FFE)
        esil = zcut(2 * HCH, "p (s n) -> p s n", s=2)
        ybuf = zcut(D_MODEL)
        assert at[0] <= HT + AR
        picked = arena[:, 0:2 * TT * D_MODEL].rearrange("p (s c n) -> p s c n", s=TT, c=2)

        ps = ctx.enter_context(nc.psum_tensor("ps", [P, 8 * 512], f32))

        def pair(n):
            return ps[:, 1024 * n:1024 * n + T]

        def main_pair(label):
            return pair(MAIN[label] % 3)

        AUXP = pair(3)

        def halves(ap):
            return ap.rearrange("p (c n) -> p c n", c=2)[:, :, 0:TH]

        def main_halves(label):
            n = MAIN[label] % 3
            return halves(ps[:, 1024 * n:1024 * n + 1024])

        const_in, vec_in, x_in, cond_in = sem("const_in"), sem("vec_in"), sem("x_in"), sem("cond_in")
        w_in_ring = [sem(f"w_arrived{i}") for i in range(RING)]
        w_used, w_summed_v, w_summed_g = sem("w_used"), sem("w_summed_v"), sem("w_summed_g")
        zeroed, zero_rows = sem("zeroed"), sem("zero_rows")
        layer_w_in = sem("layer_w_in")
        cache_k_in, cache_v_in, cache_c_in = sem("cache_k_in"), sem("cache_v_in"), sem("cache_c_in")
        kr_zero = sem("kr_zero")
        main_done, aux_done = sem("main_done"), sem("aux_done")
        cond_ready, lam_exp, lam_prod_ready, mod_ready = sem("cond_ready"), sem("lam_exp"), sem("lam_prod_ready"), sem("mod_ready")
        mod_late = sem("mod_late")
        ada_rows, late_rows, late_rows_done = sem("ada_rows"), sem("late_rows"), sem("late_rows_done")
        ada_done = sem("ada_done")
        sq_ready, sq_used, acc_ready = sem("sq_ready"), sem("sq_used"), sem("acc_ready")
        var_ready, std_ready, xn_ready, h_ready = sem("var_ready"), sem("std_ready"), sem("xn_ready"), sem("h_ready")
        hvar_ready, hstd_ready, heads_normed = sem("hvar_ready"), sem("hstd_ready"), sem("heads_normed")
        lora_ready, raw_ready, rot_used, rope_part, rope_done = (sem(n) for n in ("lora_ready", "raw_ready", "rot_used", "rope_part", "rope_done"))
        lat_normed = sem("lat_normed")
        vd_ready, km_ready, vm_ready, kr_spread = sem("vd_ready"), sem("km_ready"), sem("vm_ready"), sem("kr_spread")
        scores_done, max_ready, exp_done, p_ready = (sem(n) for n in ("scores_done", "max_ready", "exp_done", "p_ready"))
        tr_a_done, tr_b_done, pt_a_ready, pt_b_ready, pv_done, pv_evac = (sem(n) for n in ("tr_a_done", "tr_b_done", "pt_a_ready", "pt_b_ready", "pv_done", "pv_evac"))
        mid_bank = sem("mid_bank")
        x_upd = sem("x_upd")
        silu_ready, hid_product, hid_hi_ready, hid_ready = (sem(n) for n in ("silu_ready", "hid_product", "hid_hi_ready", "hid_ready"))
        t_hi, t_split, down_first = sem("t_hi"), sem("t_split"), sem("down_first")
        h_hi_ready, h_split = sem("h_hi_ready"), sem("h_split")
        mixed_hi, mixed_split = sem("mixed_hi"), sem("mixed_split")
        lg_ready, lmax_ready, lexp_ready, sel_ready, rank_ready, rows_ready = (sem(n) for n in ("lg_ready", "lmax_ready", "lexp_ready", "sel_ready", "rank_ready", "rows_ready"))
        htok_ready, scattered = sem("htok_ready"), sem("scattered")
        m_arrived = [sem(f"m_arrived{i}") for i in range(MRING)]
        w_hi_ready, w_split, pc_done = sem("w_hi_ready"), sem("w_split"), sem("pc_done")
        xs_in, esilu_ready, eact_ready = sem("xs_in"), sem("esilu_ready"), sem("eact_ready")
        etr_done, ehi_ready, etr_evac, y_evac, y_stored = (sem(n) for n in ("etr_done", "ehi_ready", "etr_evac", "y_evac", "y_stored"))
        y_left = sem("y_left")
        gathered = [sem(f"gathered{i}") for i in range(TT)]
        comb_ready = sem("comb_ready")
        y_out, kv_out = sem("y_out"), sem("kv_out")
        dve_step, pool_step = sem("dve_step"), sem("pool_step")

        KEEP = 10
        G_EACT, G_ETR = 2, 6
        TR_OF = {0: 0, 1: 1, 2: 2, 3: 3, "xa": 4, "xb": 5}

        def pieces_done(s, n):
            return SPLITS + NPC * s + n + 1

        N_LAYER_W = 4

        def wait_named(eng, freed):
            eng.wait_ge(sems[freed[0]], freed[1])

        def ada_piece(p):
            n = PIECE_AT[("ada", *p)]
            return ring[:, n % RING, 0:KC * 256].rearrange("p (k n) -> p k n", k=KC), (w_in_ring[n % RING], 16 * (n // RING + 1))

        def sub_raw(q):
            piece, (k0, k1), (c0, c1), _ = SUBS[q]
            if piece is None:
                l = 0 if q < SUB_AT[("rope", 1, 0)] else 1
                return wkr, (layer_w_in, 16 * N_LAYER_W * (l + 1))
            n = PIECE_AT[piece]
            w = P if piece[0] == "down" else (piece[3] if piece[0] == "in" else 256)
            kk = len(FF_HALF[piece[1]]) if piece[0] == "down" else KC
            src = ring[:, n % RING, 0:kk * w].rearrange("p (k n) -> p k n", k=kk)
            return src[:, k0:k1, c0:c1], (w_in_ring[n % RING], 16 * (n // RING + 1))

        def sub_of(t, q):
            _, (k0, k1), (c0, c1), _ = SUBS[q]
            n = (k1 - k0) * (c1 - c0)
            return t[:, q % SUBS_KEPT, 0:n].rearrange("p (k n) -> p k n", k=k1 - k0)
        N_CACHE_C = 2
        block = ctx.enter_context(nc.Block())

        @block.sync
        def _(sp):
            sp.dma_start(cond[:], d["cond"]).then_inc(cond_in, 16)
            sp.dma_start(vecs[:], d["vecs"]).then_inc(vec_in, 16)
            sp.dma_start(lam_in[:], d["lam"]).then_inc(vec_in, 16)

            def piece(n):
                kind = PIECES[n]
                slot = ring[:, n % RING, :]
                if n >= RING:
                    wait_named(sp, piece_freed(n - RING))
                if kind[0] == "ada":
                    src, c, w, kk = w_ada[kind[1]], kind[2] * 256, 256, KC
                elif kind[0] == "in":
                    src, c, w, kk = w_in[kind[1]], kind[2], kind[3], KC
                elif kind[0] == "o":
                    src, c, w, kk = w_o[kind[1]], kind[2] * 256, 256, KC
                elif kind[0] in ("gate", "up"):
                    src, c, w, kk = (w_gate if kind[0] == "gate" else w_up)[0], kind[1] * 256, 256, KC
                else:
                    js = FF_HALF[kind[1]]
                    src, c, w, kk = w_down[0, :, js[0]:js[-1] + 1, :], kind[2] * P, P, len(js)
                dst = slot[:, 0:kk * w].rearrange("p (k n) -> p k n", k=kk)
                sp.dma_start(dst, src[:, :, c:c + w]).then_inc(w_in_ring[n % RING], 16)

            def constants_in():
                for dst, name in ((cos_d, "cos_d"), (sin_d, "sin_d"), (cos_m, "cos_m"), (sin_m, "sin_m"),
                                  (swap_d, "swap_d"), (swap_m, "swap_m"), (ident, "ident"), (before, "before"),
                                  (small, "small")):
                    sp.dma_start(dst[:], d[name]).then_inc(const_in, 16)
                sp.dma_start(router_w[:], d["router"].rearrange("m (k p) n -> (m p) k n", p=P)).then_inc(const_in, 16)

            for n in range(3):
                piece(n)
            sp.dma_start(x_t[:], d["x_t"]).then_inc(x_in, 16)
            for n in range(3, len(PIECES)):
                if n == 6:
                    constants_in()
                if n == PIECE_AT[("o", 0, 0)]:
                    sp.wait_ge(zeroed, 2)
                    for t in range(XTILES):
                        for h in range(2):
                            sp.dma_start(xperm[t * P:(t + 1) * P, 512 * h:512 * h + 512], zeros[:]).then_inc(zero_rows, 16)
                piece(n)

            sp.wait_ge(rows_ready, 2)
            with sp.Fori(0, SLOTS) as s:
                e = sp.value_load(slot_i[0:1, bass.ds(s, 1)], min_val=0, max_val=NE - 1)
                for n in range(NPC):
                    sp.wait_ge(w_split, NPC * s + n + 1)
                    if n < NGU:
                        c = HCH * (n // 2)
                        src = (m_up if n % 2 else m_gate)[:, bass.ds(e * KC, KC), c:c + HCH]
                    else:
                        c = DCH * (n - NGU)
                        src = m_down[:, bass.ds(e * FCE, FCE), c:c + DCH]
                    dst = mraw[:, n % MRING, :].rearrange("p (k n) -> p k n", k=KC if n < NGU else FCE)
                    sp.dma_start(dst, src).then_inc(m_arrived[n % MRING], 16)

            sp.wait_ge(h_ready, 8 * 5)
            yt = d["y_t"]
            sp.dma_start(yt, h_t[:]).then_inc(y_out, 16)
            sp.wait_ge(y_out, 16)
            sp.wait_ge(kv_out, 16 * 4 * DEPTH)

        @block.gpsimd
        def _(pool):
            steps_done = [0]

            def link(ins):
                steps_done[0] += 1
                ins.then_inc(pool_step, 1)
                pool.wait_ge(pool_step, steps_done[0])

            nc.gpsimd.memset(ones[:], 1.0).then_inc(zeroed, 1)
            nc.gpsimd.memset(zeros[:], 0.0).then_inc(zeroed, 1)
            nc.gpsimd.memset(wkr, 0.0).then_inc(kr_zero, 1)
            pool.wait_ge(const_in, 16 * 10)

            def rope_item(l, r):
                n = 13 * l + r
                rows = MQK if r in (0, 9, 10, 11, 12) else P
                cs = cos_m if rows == MQK else cos_d
                src = raw[0:rows, n % 2, :]
                if r == 0:
                    out = kr_t[0:rows, PAST:NKEY]
                elif r <= 4:
                    out = k_t[0:rows, r - 1, PAST:NKEY]
                elif r <= 8:
                    out = q_t[0:rows, r - 5, :]
                else:
                    out = q_t[0:rows, r - 9, :]
                pool.wait_ge(raw_ready, n + 1)
                if r == 9:
                    pool.wait_ge(scores_done, (2 * l + 1) * ITEMS)
                nc.gpsimd.tensor_copy(out[:, N_LAT:T], src[:, N_LAT:T])
                link(nc.gpsimd.tensor_tensor(out[:, 0:N_LAT], src[:, 0:N_LAT], cs[0:rows, :], ALU.mult))
                pool.wait_ge(rot_used, n + 1)
                nc.gpsimd.tensor_tensor(out[:, 0:N_LAT], out[:, 0:N_LAT], rtmp[0:rows, n % 2, :],
                                        ALU.add).then_inc(rope_done, 1)

            def chunk_sums(l, u):
                p = [p for p in ada_after_head(l, u) if ADA_OWNER[p] == "pool"][0]
                w, arrival = ada_piece(p)
                pool.wait_ge(*arrival)
                if u == 0:
                    pool.wait_ge(cond_ready, 1)
                    pool.wait_ge(aux_done, AUX[("vd tail", l)] + 1)
                for g in range(2):
                    link(nc.gpsimd.tensor_tensor(part_prod, w, cond[:, :, g].unsqueeze(2).to_broadcast([P, KC, 256]), ALU.mult))
                    for h in (4, 2):
                        link(nc.gpsimd.tensor_tensor(part_prod[:, 0:h], part_prod[:, 0:h], part_prod[:, h:2 * h], ALU.add))
                    if g == 0 and 8 * l + u:
                        pool.wait_ge(ada_done, 8 * l + u)
                    link(nc.gpsimd.tensor_tensor(part_g[:, g], part_prod[:, 0], part_prod[:, 1], ALU.add))
                pool.sem_inc(w_summed_g, 1)

            for l in range(DEPTH):
                for r in range(9):
                    rope_item(l, r)
                for u in range(HEADS):
                    chunk_sums(l, u)
                for r in range(9, 13):
                    rope_item(l, r)
                for u in range(HEADS, 2 * HEADS):
                    chunk_sums(l, u)

            pool.wait_ge(rows_ready, 1)
            pool.wait_ge(zero_rows, 16 * 2 * XTILES)
            for t in range(TT):
                pool.wait_ge(htok_ready, t + 1)
                for c in range(2):
                    pool.indirect_dma_start(
                        out=xperm, out_offset=bass.IndirectOffsetOnAxis(ap=rowi[:, c, t:t + 1], axis=0),
                        in_=htok[:, t, :], in_offset=None).then_inc(scattered, 16)
            pool.wait_ge(scattered, 16 * 2 * TT)
            pool.dma_start(xs, xperm[0:P, :]).then_inc(xs_in, 16)
            pool.wait_ge(etr_done, 2)
            pool.dma_start(xs, xperm[P:2 * P, :]).then_inc(xs_in, 16)
            pool.drain().then_inc(y_left, 1)
            with pool.Fori(0, SLOTS) as s:
                pool.wait_ge(etr_done, 2 + G_ETR + 6 * s + TR_OF["xb"] + 1)
                pool.dma_start(xs, xperm[bass.ds((s + 2) * P, P), :]).then_inc(xs_in, 16)
                pool.wait_ge(y_evac, s + 2)
                pool.dma_start(yslots[bass.ds(s * P, P), :], ybuf).then_inc(y_stored, 16)
                pool.wait_ge(y_stored, 16 * (s + 1))
                pool.sem_inc(y_left, 1)
            pool.wait_ge(y_stored, 16 * SLOTS)
            pool.wait_ge(xs_in, 16 * (SLOTS + 2))
            for t in range(TT):
                for c in range(2):
                    pool.indirect_dma_start(
                        out=picked[:, t, c, :], out_offset=None, in_=yslots,
                        in_offset=bass.IndirectOffsetOnAxis(ap=rowi[:, c, t:t + 1], axis=0)).then_inc(gathered[t], 16)

        @block.scalar
        def _(act):
            act.wait_ge(cond_in, 16)
            nc.scalar.activation(cond[:], cond[:], ACT.Silu).then_inc(cond_ready, 1)
            act.wait_ge(main_done, MAIN[("lam",)] + 1)
            nc.scalar.activation(lam_e[:].rearrange("p l m -> p (l m)"), main_pair(("lam",))[:, 0:4],
                                 ACT.Exp).then_inc(lam_exp, 1)

            def square(l, kind, k, src, view=lambda a: a):
                n = sq_at(l, kind, k)
                if n >= 2:
                    act.wait_ge(sq_used, n - 1)
                nc.scalar.activation(view(sq[:, n % 2, :]), src, ACT.Square).then_inc(sq_ready, 1)

            def root(v):
                act.wait_ge(var_ready, v)
                nc.scalar.activation(rb[:], rb[:], ACT.Sqrt).then_inc(std_ready, 1)

            def sub_hi_part(q):
                raw_w, arrival = sub_raw(q)
                act.wait_ge(*arrival)
                if q >= SUBS_KEPT:
                    wait_named(act, SUBS[q - SUBS_KEPT][3])
                nc.scalar.activation(sub_of(sub_hi, q), raw_w, ACT.Copy).then_inc(t_hi, 1)

            def modulate(n, l, which, split=True):
                for k in range(KC):
                    act.wait_ge(xn_ready, 8 * n + k + 1)
                    s0 = 0 if which == 0 else 24
                    for c, (a, b) in enumerate(((0, N_LAT), (N_LAT, T))):
                        ins = nc.scalar.activation(h_t[:, k, a:b], h_t[:, k, a:b], ACT.Identity,
                                                   bias=mod[:, l, s0 + k, c:c + 1],
                                                   scale=gain[:, l, which, k, c:c + 1])
                    ins.then_inc(h_ready, 1)
                    if split:
                        act.wait_ge(h_ready, 8 * n + k + 1)
                        nc.scalar.activation(h_hi[:, k, :], h_t[:, k, :], ACT.Copy).then_inc(h_hi_ready, 1)

            def raw_item(l, r):
                n = 13 * l + r
                rows = MQK if r in (0, 9, 10, 11, 12) else P
                act.wait_ge(main_done, MAIN[("rope", l, r)] + 1)
                if n >= 2:
                    act.wait_ge(rope_done, n - 1)
                    act.wait_ge(rot_used, n - 1)
                if r < 9:
                    nc.scalar.activation(halves(raw[0:rows, n % 2, :]), main_halves(("rope", l, r))[0:rows],
                                         ACT.Copy).then_inc(raw_ready, 1)
                else:
                    nc.scalar.activation(raw[0:rows, n % 2, :], main_pair(("rope", l, r))[0:rows, :],
                                         ACT.Copy).then_inc(raw_ready, 1)

            for l in range(DEPTH):
                if l:
                    act.wait_ge(pv_done, 2 * ITEMS * l)
                    act.wait_ge(aux_done, AUX[("uv tail", l - 1)] + 1)
                act.dma_start(wuq, d["w_uq"][l].rearrange("(k p) n -> p k n", p=P)).then_inc(layer_w_in, 16)
                act.dma_start(wuk, d["w_uk"][l]).then_inc(layer_w_in, 16)
                act.dma_start(wuv, d["w_uv"][l]).then_inc(layer_w_in, 16)
                if l == 0:
                    act.wait_ge(kr_zero, 1)
                else:
                    act.wait_ge(t_split, SUB_AT[("rope", 0, 0)] + 1)
                act.dma_start(wkr[:, :, NOPE:MQK], w_in[l, :, :, 1920:1952]).then_inc(layer_w_in, 16)
                if l == 0:
                    act.wait_ge(x_in, 16)
                    for k in range(KC):
                        square(l, "mix", k, x_t[:, k, :])
                if l:
                    act.wait_ge(x_upd, 24)
                act.dma_start(ckv_t[:, 0:PAST], d["cache_ckv"][l]).then_inc(cache_c_in, 16)
                act.dma_start(kr_t[NOPE:MQK, 0:PAST], d["cache_kr"][l]).then_inc(cache_c_in, 16)
                act.dma_start(k_t[:, :, 0:PAST], d["cache_k"][l]).then_inc(cache_k_in, 16)
                act.dma_start(v_n[:, 0:2, :], d["cache_v"][l]).then_inc(cache_v_in, 16)
                q = SUB_AT[("lora", l, 0)]
                sub_hi_part(q)
                sub_hi_part(q + 1)
                root(4 * l + 1)
                modulate(2 * l, l, 0)
                for g in range(3):
                    src = main_halves(("lora", l, g))
                    act.wait_ge(main_done, MAIN[("lora", l, g)] + 1)
                    square(l, "lora", g, src, halves)
                    if l and g == 0:
                        act.wait_ge(x_upd, 24)
                    nc.scalar.activation(halves(lora_raw[:, g, :]), src, ACT.Copy).then_inc(lora_ready, 1)
                    sub_hi_part(q + 2 + g)
                raw_item(l, 0)
                sub_hi_part(q + 5)
                root(4 * l + 2)
                raw_item(l, 1)
                sub_hi_part(q + 6)
                root(4 * l + 3)
                sub_hi_part(q + 7)
                for r in range(2, 9):
                    raw_item(l, r)
                    if r < 8:
                        sub_hi_part(q + 6 + r)
                for n in range(14, 16):
                    sub_hi_part(q + n)
                act.wait_ge(rope_done, 13 * l + 9)
                act.dma_start(d["new_k"][l], k_t[:, :, NKEY - N_PROMPT:NKEY]).then_inc(kv_out, 16)
                act.dma_start(d["new_kr"][l], kr_t[NOPE:MQK, NKEY - N_PROMPT:NKEY]).then_inc(kv_out, 16)
                act.wait_ge(lat_normed, 2 * l + 1)
                act.dma_start(d["new_ckv"][l], ckv_t[:, NKEY - N_PROMPT:NKEY]).then_inc(kv_out, 16)

                def new_values_out(i):
                    if i == 0:
                        act.wait_ge(vd_ready, 10 * l + 10)
                        act.dma_start(d["new_v"][l], v_n[:, KT - 1, :]).then_inc(kv_out, 16)

                def attention(f, between=lambda i: None, start=lambda: None):
                    base = (2 * l + f) * ITEMS
                    maps, scale = (2, D_SCALE) if f == 0 else (1, M_SCALE)

                    def exps(i):
                        it = base + i
                        nk = LAT_KEYS if i % TT < TT - 1 else N_PROMPT
                        sc = ps[:, 1536 * (it % 2):1536 * (it % 2) + 1536].rearrange("p (m n) -> p m n", m=2)
                        if it >= 2:
                            act.wait_ge(tr_a_done, it - 1)
                            act.wait_ge(tr_b_done, n_tr_b(it - 2))
                        if f == 0 and i < 2:
                            act.wait_ge(lat_normed, 2 * l + 2)
                            act.wait_ge(rope_done, 13 * l + 9)
                        act.wait_ge(max_ready, it + 1)
                        for m in range(maps):
                            ins = nc.scalar.activation(e_buf[:, it % 2, m, 0:nk], sc[:, m, 0:nk], ACT.Exp,
                                                       bias=stat[:, it % 2, 2 + m:3 + m], scale=scale,
                                                       accum_out=stat[:, it % 2, 4 + m:5 + m])
                        ins.then_inc(exp_done, 1)

                    exps(0)
                    start()
                    for i in range(ITEMS):
                        it = base + i
                        if i + 1 < ITEMS:
                            exps(i + 1)
                        nt = 4 if i % TT < TT - 1 else 1
                        act.wait_ge(tr_a_done, it + 1)
                        if it >= 2:
                            act.wait_ge(pv_done, it - 1)
                        nc.scalar.activation(pt_buf[:, it % 2, 0:nt, :], ps[:, 3072:3072 + nt * P].rearrange("p (k n) -> p k n", k=nt),
                                             ACT.Copy).then_inc(pt_a_ready, 1)
                        between(i)

                attention(0, new_values_out)
                for h in range(HEADS):
                    if h == 0:
                        act.wait_ge(pv_evac, (2 * l + 1) * ITEMS)
                        act.wait_ge(mod_late, 8 * l + 4)
                    square(l, "head", h, mixed[:, h, :])
                    if h:
                        raw_item(l, 8 + h)
                raw_item(l, 12)
                act.wait_ge(hvar_ready, 4 * l + 4)
                nc.scalar.activation(hrb, hrb, ACT.Sqrt).then_inc(hstd_ready, 1)
                for v in range(KT - 2):
                    act.wait_ge(main_done, MAIN[("uv", l, v)] + 1)
                    nc.scalar.activation(v_n[:, v, :], main_pair(("uv", l, v))[:, 0:512], ACT.Copy).then_inc(vm_ready, 1)

                def last_values():
                    act.wait_ge(aux_done, AUX[("uv tail", l)] + 1)
                    for n in range(2):
                        nc.scalar.activation(v_n[:, KT - 2 + n, :], ps[:, 3072 + 512 * n:3584 + 512 * n],
                                             ACT.Copy).then_inc(vm_ready, 1)

                def head_hi(h):
                    nc.scalar.activation(h_hi[:, h, :], mixed[:, h, :], ACT.Copy).then_inc(mixed_hi, 1)

                def head_share(i):
                    h, step = divmod(i, 4)
                    if h < HEADS and step == 3:
                        act.wait_ge(heads_normed, 4 * l + h + 1)
                        head_hi(h)
                    elif 0 <= i - 4 * HEADS < HEADS - 1:
                        h = i - 3 * HEADS
                        act.wait_ge(pv_evac, (2 * l + 1) * ITEMS + TT * (h - HEADS + 1))
                        head_hi(h)

                attention(1, head_share, last_values)
                act.wait_ge(w_summed_g, 8 * (l + 1))
                q = SUB_AT[("o", l, 0)]
                sub_hi_part(q)
                sub_hi_part(q + 1)
                act.wait_ge(pv_evac, (2 * l + 2) * ITEMS)
                head_hi(2 * HEADS - 1)
                for k in range(KC):
                    act.wait_ge(x_upd, (24 if l else 0) + k + 1)
                    if k == 0:
                        act.wait_ge(mod_late, 8 * l + 8)
                    square(l, "ffn", k, x_t[:, k, :])
                    if k + 2 < KC:
                        sub_hi_part(q + k + 2)
                if l == 0:
                    q = SUB_AT[("gate", 0)]
                    sub_hi_part(q)
                    sub_hi_part(q + 1)
                root(4 * l + 4)
                modulate(2 * l + 1, l, 1, l == 0)
                if l == 0:
                    for half, js in enumerate(FF_HALF):
                        for j in js:
                            act.wait_ge(main_done, MAIN[("gate", j)] + 1)
                            if j >= 2:
                                act.wait_ge(hid_ready, j - 1)
                            nc.scalar.activation(halves(sil[:, j % 2, :]), main_halves(("gate", j)),
                                                 ACT.Silu).then_inc(silu_ready, 1)
                            q += 1
                            sub_hi_part(q + 1)
                            act.wait_ge(hid_product, j + 1)
                            if j == FF_HALF[1][0]:
                                act.wait_ge(main_done, MAIN[("down", 0, KC - 1)] + 1)
                            nc.scalar.activation(hid_hi[:, j - js[0], :], sil[:, j % 2, :], ACT.Copy).then_inc(hid_hi_ready, 1)
                            q += 1
                            sub_hi_part(q + 1)
                        for d_ in range(KC):
                            for _ in range(2):
                                q += 1
                                if not (half and d_ == KC - 1):
                                    sub_hi_part(q + 1)
                            if half:
                                act.wait_ge(x_upd, 16 + d_ + 1)
                                square(1, "mix", d_, x_t[:, d_, :])

            act.wait_ge(lmax_ready, 1)
            nc.scalar.activation(rt[:, 0], rt[:, 0], ACT.Exp).then_inc(lexp_ready, 1)
            for t in range(TT):
                act.wait_ge(main_done, MAIN[("htok", t)] + 1)
                src = ps[:, 1024 * (MAIN[("htok", t)] % 3):1024 * (MAIN[("htok", t)] % 3) + 1024]
                nc.scalar.activation(htok[:, t, :], src, ACT.Copy).then_inc(htok_ready, 1)

            def tr_hi(dst, bank, n, kn):
                act.wait_ge(etr_done, n)
                nc.scalar.activation(dst, ps[:, 512 * bank:512 * bank + kn * P].rearrange("p (k n) -> p k n", k=kn),
                                     ACT.Copy).then_inc(ehi_ready, 1)

            for half in range(2):
                act.wait_ge(scattered, 16 * 2 * TT)
                tr_hi(xs_hi[:, 4 * half:4 * half + 4, :], 4 + TR_OF[("xa", "xb")[half]] % 2, half + 1, 4)

            def piece_hi(s, n):
                act.wait_ge(m_arrived[n % MRING], 16 * (NPC // MRING * s + n // MRING + 1))
                act.wait_ge(pc_done, NPC * s + n + 1)
                nc.scalar.activation(w_hi[:, n % SPLITS, :], mraw[:, n % MRING, :], ACT.Copy).then_inc(w_hi_ready, 1)

            def expert_hi(s, last):
                def ahead(n):
                    if not (last and n >= NPC):
                        piece_hi(s, n)

                def silu(c):
                    act.wait_ge(pc_done, pieces_done(s, 2 * c))
                    act.wait_ge(eact_ready, 4 * s + c + 1)
                    nc.scalar.activation(esil[:, c % 2, :], ps[:, 512 * (2 * c % 4):512 * (2 * c % 4) + HCH],
                                         ACT.Silu).then_inc(esilu_ready, 1)

                def turned(c):
                    j = TR_OF[c]
                    if c in ("xa", "xb"):
                        dst, kn = xs_hi[:, 4 * (j - 4):4 * (j - 4) + 4, :], 4
                    else:
                        dst, kn = ea_hi[:, BLK[c][0]:BLK[c][1], :], BLK[c][1] - BLK[c][0]
                        act.wait_ge(pc_done, pieces_done(s, -1))
                    tr_hi(dst, 4 + j % 2, 2 + G_ETR + 6 * s + j + 1, kn)

                ahead(2)
                for c in range(3):
                    silu(c)
                    if c:
                        turned(c - 1)
                    ahead(2 * c + 3)
                    ahead(2 * c + 4)
                silu(3)
                turned(2)
                ahead(9)
                ahead(10)
                turned(3)
                ahead(11)
                turned("xa")
                ahead(12)
                turned("xb")
                ahead(13)

            piece_hi(0, 0)
            piece_hi(0, 1)
            with act.Fori(0, SLOTS - 1) as s:
                expert_hi(s, False)
            expert_hi(SLOTS - 1, True)

            for k in range(KC):
                act.wait_ge(x_upd, 32 + TT)
                square(DEPTH, "fin", k, x_t[:, k, :])
            root(4 * DEPTH + 1)
            for k in range(KC):
                act.wait_ge(xn_ready, 8 * 4 + k + 1)
                nc.scalar.activation(h_t[:, k, :], h_t[:, k, :], ACT.Copy, scale=vecs[:, V_FIN + k:V_FIN + k + 1]).then_inc(h_ready, 1)

        @block.vector
        def _(dve):
            steps_done = [0]

            def link(ins):
                steps_done[0] += 1
                ins.then_inc(dve_step, 1)
                dve.wait_ge(dve_step, steps_done[0])

            dve.wait_ge(vec_in, 32)
            nc.vector.tensor_tensor(lam_prod[:], lam_in[:, :, :, 0], lam_in[:, :, :, 1], ALU.mult).then_inc(lam_prod_ready, 1)
            for l in range(DEPTH):
                link(nc.vector.tensor_scalar(subg[:, l:l + 1], vecs[:, V_SUB + l:V_SUB + l + 1], 1.0 - lam_init(l), None, ALU.mult))
            dve.wait_ge(lam_exp, 1)
            for l in range(DEPTH):
                link(nc.vector.tensor_tensor(neg_lam[:, l:l + 1], lam_e[:, l, 1:2], lam_e[:, l, 0:1], ALU.subtract))
                link(nc.vector.tensor_scalar(neg_lam[:, l:l + 1], neg_lam[:, l:l + 1], -lam_init(l), None, ALU.add))

            def add_bias(l, c0, n, src):
                b = vecs[:, V_BADA + 48 * l + c0:V_BADA + 48 * l + c0 + n]
                return nc.vector.tensor_tensor(mod[:, l, c0:c0 + n, :], src.rearrange("p (c g) -> p c g", g=2),
                                               b.unsqueeze(2).to_broadcast([P, n, 2]), ALU.add)

            def make_gain(l, which):
                g = vecs[:, (V_MIX, V_FFN)[which] + 8 * l:(V_MIX, V_FFN)[which] + 8 * l + 8]
                s0 = (8, 32)[which]
                link(nc.vector.scalar_tensor_tensor(gain[:, l, which], mod[:, l, s0:s0 + 8, :], 1.0,
                                                    g.unsqueeze(2).to_broadcast([P, KC, 2]), ALU.add, ALU.mult))

            def sub_rest(q):
                raw_w, arrival = sub_raw(q)
                dve.wait_ge(*arrival)
                dve.wait_ge(t_hi, q + 1)
                nc.vector.tensor_tensor(sub_of(sub_lo, q), raw_w, sub_of(sub_hi, q).bitcast(f32),
                                        ALU.subtract).then_inc(t_split, 1)

            def add_square(l, kind, k):
                n = sq_at(l, kind, k)
                dve.wait_ge(sq_ready, n + 1)
                if k == 0:
                    return
                if k > 1:
                    dve.wait_ge(sq_used, n)
                other = sq[:, (n - 1) % 2, :] if k == 1 else rb[:]
                ins = nc.vector.tensor_tensor(rb[:], other, sq[:, n % 2, :], ALU.add).then_inc(sq_used, 2 if k == 1 else 1)
                if k == KC - 1:
                    dve.wait_ge(sq_used, n + 1)
                    dve.sem_inc(acc_ready, 1)

            def norm(n, l, v, aux_label, split=None):
                dve.wait_ge(aux_done, AUX[aux_label] + 1)
                nc.vector.tensor_scalar(rb[:], AUXP, 1.0 / D_MODEL, EPS, ALU.mult, ALU.add).then_inc(var_ready, 1)
                dve.wait_ge(std_ready, v)
                link(nc.vector.reciprocal(rb[:], rb[:]))
                for k in range(KC + 2):
                    if k < KC:
                        nc.vector.tensor_tensor(h_t[:, k, :], x_t[:, k, :], rb[:], ALU.mult).then_inc(xn_ready, 1)
                    if k >= 2 and split is not None:
                        dve.wait_ge(h_hi_ready, split + k - 1)
                        nc.vector.tensor_tensor(h_lo[:, k - 2, :], h_t[:, k - 2, :], h_hi[:, k - 2, :].bitcast(f32),
                                                ALU.subtract).then_inc(h_split, 1)

            def rot(l, r):
                n = 13 * l + r
                rows = MQK if r in (0, 9, 10, 11, 12) else P
                sn = sin_m if rows == MQK else sin_d
                dve.wait_ge(aux_done, AUX[("rot", l, r)] + 1)
                if n >= 2:
                    dve.wait_ge(rope_done, n - 1)
                nc.vector.tensor_tensor(rtmp[0:rows, n % 2, :], AUXP[0:rows, 0:N_LAT], sn[0:rows, :],
                                        ALU.mult).then_inc(rot_used, 1)

            def residual(l, label, d_, g0):
                dve.wait_ge(main_done, MAIN[label] + 1)
                o = 1024 * (MAIN[label] % 3)
                for a, b, bank, c in ((0, TH, 0, 0), (TH, N_LAT, 1, 0), (N_LAT, T, 1, 1)):
                    src = ps[:, o + 512 * bank + a - TH * bank:o + 512 * bank + b - TH * bank]
                    ins = nc.vector.scalar_tensor_tensor(x_t[:, d_, a:b], src, mod[:, l, g0 + d_, c:c + 1],
                                                         x_t[:, d_, a:b], ALU.mult, ALU.add)
                ins.then_inc(x_upd, 1)

            for l in range(DEPTH):
                if l == 0:
                    dve.wait_ge(x_in, 16)
                    dve.wait_ge(const_in, 160)
                if l == 0:
                    for k in range(KC):
                        add_square(0, "mix", k)
                    for n in range(2):
                        dve.wait_ge(main_done, MAIN[("ada0", n)] + 1)
                        o = 1024 * (MAIN[("ada0", n)] % 3)
                        nc.vector.tensor_copy(ada_row0[:, 1024 * n:1024 * n + 1024], ps[0:2, o:o + 1024]).then_inc(ada_rows, 1)
                    dve.wait_ge(main_done, MAIN[("ada0t",)] + 1)
                    add_bias(0, 0, 16, main_pair(("ada0t",))[:, 0:32]).then_inc(mod_ready, 1)
                    dve.wait_ge(mod_ready, 1)
                    make_gain(0, 0)
                q = SUB_AT[("lora", l, 0)]
                sub_rest(q)
                sub_rest(q + 1)
                norm(2 * l, l, 4 * l + 1, ("norm", l, "mix"), 16 * l)
                sub_rest(q + 2)
                sub_rest(q + 3)
                dve.wait_ge(lora_ready, 3 * l + 3)
                sub_rest(q + 4)
                sub_rest(q + 5)
                dve.wait_ge(aux_done, AUX[("norm", l, "ckv")] + 1)
                nc.vector.tensor_scalar(rb[:], AUXP, 1.0 / KVL, EPS, ALU.mult, ALU.add).then_inc(var_ready, 1)
                dve.wait_ge(std_ready, 4 * l + 2)
                link(nc.vector.reciprocal(rb[:], rb[:]))
                nc.vector.scalar_tensor_tensor(ckv_t[:, PAST:NKEY], lora_raw[:, 0, :], vecs[:, V_KVN + l:V_KVN + l + 1],
                                               rb[:], ALU.mult, ALU.mult).then_inc(lat_normed, 1)
                dve.wait_ge(lat_normed, 2 * l + 1)
                sub_rest(q + 6)
                dve.wait_ge(aux_done, AUX[("norm", l, "cq")] + 1)
                nc.vector.tensor_scalar(rb[:], AUXP, 1.0 / QL, EPS, ALU.mult, ALU.add).then_inc(var_ready, 1)
                dve.wait_ge(std_ready, 4 * l + 3)
                link(nc.vector.reciprocal(rb[:], rb[:]))
                for c in range(2):
                    ins = nc.vector.scalar_tensor_tensor(cq_t[:, c, :], lora_raw[:, 1 + c, :],
                                                         vecs[:, V_QN + 2 * l + c:V_QN + 2 * l + c + 1],
                                                         rb[:], ALU.mult, ALU.mult)
                ins.then_inc(lat_normed, 1)
                sub_rest(q + 7)
                for r in range(7):
                    rot(l, r)
                    if r < 6:
                        sub_rest(q + 8 + r)

                def vd(v):
                    half, t = v // TT, v % TT
                    if v < 8:
                        dve.wait_ge(main_done, MAIN[("vd", l, v)] + 1)
                        src = main_pair(("vd", l, v))[:, 0:256]
                    else:
                        dve.wait_ge(aux_done, AUX[("vd tail", l)] + 1)
                        src = ps[:, 3072 + 512 * (v - 8):3328 + 512 * (v - 8)]
                    nc.vector.tensor_copy(v_n[:, 2 + t, 256 * half:256 * half + 256], src).then_inc(vd_ready, 1)

                vd(0)
                rot(l, 7)
                vd(1)
                rot(l, 8)
                for v in range(2, 8):
                    vd(v)
                    if v == 4:
                        sub_rest(q + 14)
                        sub_rest(q + 15)

                def attention(f, between=lambda i: None, start=lambda: None):
                    base = (2 * l + f) * ITEMS
                    maps, scale = (2, D_SCALE) if f == 0 else (1, M_SCALE)

                    def item(i):
                        return base + i, (base + i) % 2, LAT_KEYS if i % TT < TT - 1 else N_PROMPT

                    def maxes(i):
                        it, b, nk = item(i)
                        sc = ps[:, 1536 * b:1536 * b + 1536].rearrange("p (m n) -> p m n", m=2)
                        dve.wait_ge(scores_done, it + 1)
                        if it >= 2:
                            dve.wait_ge(exp_done, it - 1)
                        link(nc.vector.reduce_max(stat[:, b, 0:maps], sc[:, 0:maps, 0:nk], AXX))
                        nc.vector.tensor_scalar(stat[:, b, 2:2 + maps], stat[:, b, 0:maps], -scale, None,
                                                ALU.mult).then_inc(max_ready, 1)

                    def combine(i):
                        it, b, nk = item(i)
                        dve.wait_ge(exp_done, it + 1)
                        if it >= 2:
                            dve.wait_ge(tr_a_done, it - 1)
                            dve.wait_ge(tr_b_done, n_tr_b(it - 2))
                        link(nc.vector.reciprocal(stat[:, b, 6:6 + maps], stat[:, b, 4:4 + maps]))
                        ins = nc.vector.tensor_scalar(diag[:, b, :], ident[:], stat[:, b, 6:7], None, ALU.mult)
                        if f == 0:
                            link(nc.vector.scalar_tensor_tensor(stat[:, b, 8:9], stat[:, b, 4:5], neg_lam[:, l:l + 1],
                                                                stat[:, b, 7:8], ALU.mult, ALU.mult))
                            e1 = e_buf[:, b, 0, 0:nk]
                            ins = nc.vector.scalar_tensor_tensor(e1, e_buf[:, b, 1, 0:nk], stat[:, b, 8:9], e1,
                                                                 ALU.mult, ALU.add)
                        ins.then_inc(p_ready, 1)

                    def pv_out(i):
                        it, b, nk = item(i)
                        h, qt = i // TT, i % TT
                        dve.wait_ge(pv_done, it + 1)
                        nc.vector.tensor_copy(mixed[:, 4 * f + h, qt * P:(qt + 1) * P], ps[:, 3840:3968]).then_inc(pv_evac, 1)

                    def pt_b(i):
                        it, b, nk = item(i)
                        dve.wait_ge(tr_b_done, n_tr_b(it))
                        if it >= 2:
                            dve.wait_ge(pv_done, it - 1)
                        nc.vector.tensor_copy(pt_buf[:, b, 4:6, :], ps[:, 3584:3840].rearrange("p (k n) -> p k n", k=2)).then_inc(pt_b_ready, 1)

                    def late_row_copy(u, b):
                        dve.wait_ge(late_rows_done, u + 1)
                        if u:
                            dve.wait_ge(ada_done, u)
                        nc.vector.tensor_copy(ada_row[:, 0:256], ps[0:2, 1536 * b:1536 * b + 256]).then_inc(late_rows, 1)

                    def chunk_sums(i):
                        u, step = 4 * f + i // TT, i % TT - 1
                        if step < 0:
                            return
                        p = [p for p in ada_after_head(l, u) if ADA_OWNER[p] == "dve"][0]
                        w, arrival = ada_piece(p)
                        if step == 0:
                            dve.wait_ge(*arrival)
                            dve.wait_ge(cond_ready, 1)
                            if 8 * l + u:
                                dve.wait_ge(ada_done, 8 * l + u)
                        for k in (2 * step, 2 * step + 1):
                            for g in range(2):
                                if k == 0:
                                    ins = nc.vector.tensor_scalar(part_v[:, g], w[:, k], cond[:, k, g:g + 1], None, ALU.mult)
                                else:
                                    ins = nc.vector.scalar_tensor_tensor(part_v[:, g], w[:, k], cond[:, k, g:g + 1], part_v[:, g],
                                                                         ALU.mult, ALU.add)
                            if k == KC - 1:
                                ins.then_inc(w_summed_v, 1)
                            else:
                                link(ins)

                    def late_mods(u):
                        todo = ada_after_head(l, u)
                        dve.wait_ge(ada_done, 8 * l + u + 1)
                        src = ps[:, 3968:3968 + 4 * len(todo)]
                        for n, (ll, c) in enumerate(todo):
                            ins = add_bias(ll, 2 * c, 2, src[:, 4 * n:4 * n + 4])
                        ins.then_inc(mod_late, 1)

                    maxes(0)
                    combine(0)
                    start()
                    for i in range(ITEMS):
                        if i + 1 < ITEMS:
                            maxes(i + 1)
                        if i:
                            pv_out(i - 1)
                        if i % TT == TT - 1 and l == 0:
                            late_row_copy(4 * f + i // TT, (base + i) % 2)
                        if i % TT == 0 and i:
                            late_mods(4 * f + i // TT - 1)
                        chunk_sums(i)
                        if i % TT < TT - 1:
                            pt_b(i)
                        if i + 1 < ITEMS:
                            combine(i + 1)
                        between(i)
                    pv_out(ITEMS - 1)
                    late_mods(4 * f + HEADS - 1)

                def last_values():
                    vd(8)
                    vd(9)

                attention(0, start=last_values)
                for h in range(HEADS):
                    dve.wait_ge(aux_done, AUX[("norm", l, "head", h)] + 1)
                    nc.vector.tensor_scalar(hrb[:, h, :], AUXP, 1.0 / P, EPS, ALU.mult, ALU.add).then_inc(hvar_ready, 1)
                    if h:
                        rot(l, 8 + h)
                rot(l, 12)
                for h in range(HEADS):
                    if h == 0:
                        dve.wait_ge(kv_out, 16 * 4 * (l + 1))
                    dve.wait_ge(main_done, MAIN[("uk", l, h)] + 1)
                    src = ps[0:NOPE, 1024 * (MAIN[("uk", l, h)] % 3):1024 * (MAIN[("uk", l, h)] % 3) + 1024]
                    nc.vector.tensor_copy(k_t[0:NOPE, h, :].rearrange("p (c n) -> p c n", c=2),
                                          src.rearrange("p (c n) -> p c n", c=2)[:, :, 0:448]).then_inc(km_ready, 1)
                    if h == 0:
                        dve.wait_ge(rope_done, 13 * l + 9)
                        dve.wait_ge(cache_c_in, 16 * N_CACHE_C * (l + 1))
                    nc.vector.tensor_copy(k_t[NOPE:MQK, h, :], kr_t[NOPE:MQK, :]).then_inc(kr_spread, 1)

                def head_rest(h):
                    dve.wait_ge(mixed_hi, 8 * l + h + 1)
                    nc.vector.tensor_tensor(h_lo[:, h, :], mixed[:, h, :], h_hi[:, h, :].bitcast(f32),
                                            ALU.subtract).then_inc(mixed_split, 1)

                def head_norm(i):
                    h, step = divmod(i, 4)
                    if h < HEADS and step < 2:
                        if i == 0:
                            dve.wait_ge(hstd_ready, l + 1)
                        r = hrb[:, h, TH * step:TH * step + TH]
                        link(nc.vector.reciprocal(r, r))
                    elif h < HEADS and step == 2:
                        nc.vector.scalar_tensor_tensor(mixed[:, h, :], mixed[:, h, :], subg[:, l:l + 1], hrb[:, h, :],
                                                       ALU.mult, ALU.mult).then_inc(heads_normed, 1)
                    elif h < HEADS:
                        head_rest(h)
                    elif i - 4 * HEADS < HEADS - 1:
                        head_rest(i - 3 * HEADS)

                attention(1, head_norm)
                q = SUB_AT[("o", l, 0)]
                dve.wait_ge(w_summed_g, 8 * (l + 1))
                sub_rest(q)
                sub_rest(q + 1)
                head_rest(2 * HEADS - 1)
                dve.wait_ge(mod_late, 8 * l + 8)
                make_gain(l, 1)
                if l + 1 < DEPTH:
                    make_gain(l + 1, 0)
                for d_ in range(KC):
                    residual(l, ("o", l, d_), d_, 16)
                    if d_:
                        add_square(l, "ffn", d_ - 1)
                    if d_ + 2 < KC:
                        sub_rest(q + d_ + 2)
                add_square(l, "ffn", KC - 1)
                if l == 0:
                    q = SUB_AT[("gate", 0)]
                    sub_rest(q)
                    sub_rest(q + 1)
                norm(2 * l + 1, l, 4 * l + 4, ("norm", l, "ffn"), 8 if l == 0 else None)
                if l == 0:
                    for half, js in enumerate(FF_HALF):
                        for j in js:
                            q += 1
                            sub_rest(q + 1)
                            dve.wait_ge(main_done, MAIN[("up", j)] + 1)
                            dve.wait_ge(silu_ready, j + 1)
                            nc.vector.tensor_tensor(halves(sil[:, j % 2, :]), halves(sil[:, j % 2, :]), main_halves(("up", j)),
                                                    ALU.mult).then_inc(hid_product, 1)
                            dve.wait_ge(hid_hi_ready, j + 1)
                            nc.vector.tensor_tensor(hid_lo[:, j - js[0], :], sil[:, j % 2, :],
                                                    hid_hi[:, j - js[0], :].bitcast(f32), ALU.subtract).then_inc(hid_ready, 1)
                            q += 1
                            sub_rest(q + 1)
                        for d_ in range(KC):
                            for _ in range(2):
                                q += 1
                                if not (half and d_ == KC - 1):
                                    sub_rest(q + 1)
                            residual(l, ("down", half, d_), d_, 40)
                            if half and d_:
                                add_square(1, "mix", d_ - 1)
                    add_square(1, "mix", KC - 1)

            dve.wait_ge(aux_done, AUX[("router",)] + 1)
            nc.vector.tensor_copy(lg[:].rearrange("p t e -> p (t e)"), AUXP[:, 0:TT * NE]).then_inc(lg_ready, 1)
            dve.wait_ge(lg_ready, 1)
            by_e = lg[:].unsqueeze(3).to_broadcast([P, TT, NE, NE])
            by_o = lg[:].unsqueeze(2).to_broadcast([P, TT, NE, NE])

            def flat(a):
                return a.rearrange("p t e o -> p t (e o)")

            link(nc.vector.reduce_max(rv[:, 0], lg[:], AXX))
            link(nc.vector.tensor_tensor(rt[:, 0], lg[:], rv[:, 0].unsqueeze(2).to_broadcast([P, TT, NE]), ALU.subtract))
            nc.vector.drain().then_inc(lmax_ready, 1)
            link(nc.vector.tensor_tensor(cmp_a[:], by_o, by_e, ALU.is_gt))
            link(nc.vector.tensor_tensor(cmp_b[:], by_o, by_e, ALU.is_equal))
            for t in range(TT):
                link(nc.vector.tensor_tensor(cmp_b[:, t], cmp_b[:, t], tri8, ALU.mult))
            link(nc.vector.tensor_tensor(flat(cmp_a[:]), flat(cmp_a[:]), flat(cmp_b[:]), ALU.add))
            link(nc.vector.reduce_sum(rt[:, 1], cmp_a[:], AXX))
            nc.vector.tensor_scalar(rt[:, 4], rt[:, 1], 2.0, None, ALU.is_lt).then_inc(sel_ready, 1)
            link(nc.vector.tensor_scalar(rt[:, 2], rt[:, 1], 0.0, None, ALU.is_equal))
            link(nc.vector.tensor_scalar(rt[:, 3], rt[:, 1], 1.0, None, ALU.is_equal))
            dve.wait_ge(aux_done, AUX[("rank",)] + 1)
            link(nc.vector.tensor_copy(rt[:, 7].rearrange("p t e -> p (t e)"), AUXP[:, TT * NE:2 * TT * NE]))
            for t in range(1, TT):
                link(nc.vector.tensor_tensor(rt[:, 7, t], rt[:, 7, t - 1], rt[:, 7, t], ALU.add))
            nc.vector.tensor_copy(cnt[:, 0], rt[:, 7, TT - 1])
            nc.vector.tensor_copy(rt[:, 5, 0], AUXP[:, 0:NE])
            nc.vector.tensor_tensor(rt[:, 5, 1:TT], rt[:, 7, 0:TT - 1],
                                    AUXP[:, NE:TT * NE].rearrange("p (t e) -> p t e", e=NE), ALU.add).then_inc(rank_ready, 1)
            dve.wait_ge(rank_ready, 1)
            c58 = cmp_a[:, 0].rearrange("p a b -> p (a b)")[:, 0:NE * TT].rearrange("p (a b) -> p a b", a=NE)
            link(nc.vector.tensor_tensor(c58, cnt[:, 0].unsqueeze(2).to_broadcast([P, NE, TT]),
                                         steps.unsqueeze(1).to_broadcast([P, NE, TT]), ALU.is_gt))
            link(nc.vector.reduce_sum(cnt[:, 1], c58, AXX))
            link(nc.vector.tensor_tensor(cmp_a[:, 0], cnt[:, 1].unsqueeze(1).to_broadcast([P, NE, NE]), tri8, ALU.mult))
            link(nc.vector.reduce_sum(cnt[:, 2], cmp_a[:, 0], AXX))
            link(nc.vector.tensor_scalar(cnt[:, 3], cnt[:, 2], float(P), None, ALU.mult))
            link(nc.vector.tensor_tensor(rt[:, 5], rt[:, 5], cnt[:, 3].unsqueeze(1).to_broadcast([P, TT, NE]), ALU.add))
            for c in range(2):
                link(nc.vector.tensor_tensor(rt[:, 6], rt[:, 2 + c], rt[:, 5], ALU.mult))
                link(nc.vector.reduce_sum(rv[:, 1 + c], rt[:, 6], AXX))
            nc.vector.tensor_copy(rowi[:], rv[:, 1:3]).then_inc(rows_ready, 1)
            c17 = cmp_b[:, 0:2].rearrange("p t a b -> p (t a b)")[:, 0:SLOTS * 7].rearrange("p (a b) -> p a b", a=SLOTS)
            link(nc.vector.tensor_tensor(c17, slot_rows.unsqueeze(2).to_broadcast([P, SLOTS, 7]),
                                         cnt[:, 3, 1:8].unsqueeze(1).to_broadcast([P, SLOTS, 7]), ALU.is_ge))
            link(nc.vector.reduce_sum(slot_e[:], c17, AXX))
            nc.vector.tensor_copy(slot_i[:], slot_e[:]).then_inc(rows_ready, 1)
            dve.wait_ge(lexp_ready, 1)
            link(nc.vector.reduce_sum(rv[:, 3], rt[:, 0], AXX))
            link(nc.vector.reciprocal(rv[:, 4], rv[:, 3]))
            link(nc.vector.tensor_tensor(rt[:, 0], rt[:, 0], rv[:, 4].unsqueeze(2).to_broadcast([P, TT, NE]), ALU.mult))
            for c in range(2):
                link(nc.vector.tensor_tensor(rt[:, 6], rt[:, 2 + c], rt[:, 0], ALU.mult))
                link(nc.vector.reduce_sum(rv[:, 5 + c], rt[:, 6], AXX))
            link(nc.vector.tensor_tensor(rv[:, 7], rv[:, 5], rv[:, 6], ALU.add))
            link(nc.vector.reciprocal(rv[:, 8], rv[:, 7]))
            for c in range(2):
                link(nc.vector.tensor_tensor(rv[:, 9 + c], rv[:, 5 + c], rv[:, 8], ALU.mult))

            def piece_lo(s, n, h):
                if h == 0:
                    dve.wait_ge(m_arrived[n % MRING], 16 * (NPC // MRING * s + n // MRING + 1))
                    dve.wait_ge(w_hi_ready, NPC * s + n + 1)
                a = slice(PIECE_F // 2 * h, PIECE_F // 2 * (h + 1))
                ins = nc.vector.tensor_tensor(w_lo[:, n % SPLITS, a], mraw[:, n % MRING, a],
                                              w_hi[:, n % SPLITS, a].bitcast(f32), ALU.subtract)
                if h:
                    ins.then_inc(w_split, 1)

            def tr_lo(dst, hi, bank, n, kn):
                dve.wait_ge(ehi_ready, n)
                nc.vector.tensor_tensor(dst, ps[:, 512 * bank:512 * bank + kn * P].rearrange("p (k n) -> p k n", k=kn),
                                        hi.bitcast(f32), ALU.subtract).then_inc(etr_evac, 1)

            def expert_lo(s, last):
                def ahead(n, halves=(0, 1)):
                    for h in halves:
                        if not (last and n >= NPC):
                            piece_lo(s, n, h)

                def turned(c):
                    j = TR_OF[c]
                    if c in ("xa", "xb"):
                        a = slice(4 * (j - 4), 4 * (j - 4) + 4)
                        dst, hi, kn = xs_lo[:, a, :], xs_hi[:, a, :], 4
                    else:
                        a = slice(*BLK[c])
                        dst, hi, kn = ea_lo[:, a, :], ea_hi[:, a, :], BLK[c][1] - BLK[c][0]
                    tr_lo(dst, hi, 4 + j % 2, 2 + 6 * s + j + 1, kn)

                def product(c):
                    bank = (2 * c + 1) % 4
                    dve.wait_ge(pc_done, pieces_done(s, 2 * c + 1))
                    dve.wait_ge(esilu_ready, 4 * s + c + 1)
                    dve.wait_ge(etr_done, 2 + 6 * s + TR_OF[min(c + 1, 3)] + 1)
                    nc.vector.tensor_tensor(eact[:, HCH * c:HCH * (c + 1)], esil[:, c % 2, :],
                                            ps[:, 512 * bank:512 * bank + HCH], ALU.mult).then_inc(eact_ready, 1)

                ahead(2)
                for c in range(3):
                    if c:
                        turned(c - 1)
                    ahead(2 * c + 3)
                    product(c)
                    ahead(2 * c + 4)
                turned(2)
                ahead(9, (0,))
                product(3)
                ahead(9, (1,))
                turned(3)
                ahead(10)
                ahead(11)
                turned("xa")
                ahead(12)
                turned("xb")
                ahead(13)
                dve.wait_ge(pc_done, pieces_done(s, NPC - 1))
                dve.wait_ge(y_left, s + 1)
                nc.vector.tensor_copy(ybuf, ps[:, 3072:4096]).then_inc(y_evac, 1)

            dve.wait_ge(htok_ready, TT)
            nc.vector.drain().then_inc(w_split, 1)
            dve.wait_ge(scattered, 16 * 2 * TT)
            nc.vector.drain().then_inc(w_split, MRING - 1)
            nc.vector.drain().then_inc(eact_ready, G_EACT)
            nc.vector.drain().then_inc(y_evac, 1)
            for half in range(2):
                a = slice(4 * half, 4 * half + 4)
                tr_lo(xs_lo[:, a, :], xs_hi[:, a, :], 4 + TR_OF[("xa", "xb")[half]] % 2, half + 1, 4)
            for n in range(2):
                for h in range(2):
                    piece_lo(0, n, h)
            with dve.Fori(0, SLOTS - 1) as s:
                expert_lo(s, False)
            expert_lo(SLOTS - 1, True)

            def weigh(t):
                dve.wait_ge(gathered[t], 32)
                y1, y2 = picked[:, t, 0, :], picked[:, t, 1, :]
                link(nc.vector.tensor_scalar(y2, y2, rv[:, 10, t:t + 1], None, ALU.mult))
                nc.vector.scalar_tensor_tensor(y1, y1, rv[:, 9, t:t + 1], y2, ALU.mult, ALU.add).then_inc(comb_ready, 1)

            weigh(0)
            for t in range(TT):
                if t + 1 < TT:
                    weigh(t + 1)
                m = MAIN[("comb", t)]
                dve.wait_ge(main_done, m + 1)
                g = 0 if t < TT - 1 else 1
                for k in range(KC):
                    ins = nc.vector.scalar_tensor_tensor(
                        x_t[:, k, t * P:(t + 1) * P], ps[:, 1024 * (m % 3) + k * P:1024 * (m % 3) + (k + 1) * P],
                        mod[:, 1, 40 + k, g:g + 1], x_t[:, k, t * P:(t + 1) * P], ALU.mult, ALU.add)
                ins.then_inc(x_upd, 1)
            dve.wait_ge(x_upd, 32 + TT)
            for k in range(KC):
                add_square(DEPTH, "fin", k)
            norm(4, DEPTH, 4 * DEPTH + 1, ("norm", DEPTH, "fin"))

        @block.tensor
        def _(pe):
            LAT, PRM = slice(0, N_LAT), slice(N_LAT, T)

            def claim_main(label):
                m = MAIN[label]
                if m >= 3:
                    name, val = MAIN_FREED[m - 3]
                    pe.wait_ge(sems[name], val)
                return main_pair(label)

            def claim_aux(label):
                n = AUX[label]
                if n >= 1:
                    name, val = AUX_FREED[n - 1]
                    pe.wait_ge(sems[name], val)
                return AUXP

            def arrived(p):
                n = PIECE_AT[p]
                pe.wait_ge(w_in_ring[n % RING], 16 * (n // RING + 1))
                return ring[:, n % RING, :]

            def both(out, lhs, rhs, start, stop):
                nc.tensor.matmul(out[:, LAT], lhs, rhs[:, LAT], start=start, stop=stop)
                return nc.tensor.matmul(out[:, PRM], lhs, rhs[:, PRM], start=start, stop=stop)

            def sum_square(l, kind, k, first, last):
                n = sq_at(l, kind, k)
                pe.wait_ge(sq_ready, n + 1)
                return both(AUXP, ones[:], sq[:, n % 2, :], first, last)

            def sum_chunks(n, label):
                claim_aux(label)
                pe.wait_ge(acc_ready, n)
                both(AUXP, ones[:], rb[:], True, True).then_inc(aux_done, 1)

            def keep_busy(label, n):
                out = claim_main(label)
                for _ in range(n):
                    nc.tensor.matmul(out[:, 0:N_LAT], ones[:], cos_d[:], start=True, stop=True)

            pe.wait_ge(lam_prod_ready, 1)
            pe.wait_ge(zeroed, 2)
            lam_ps = claim_main(("lam",))
            nc.tensor.matmul(lam_ps[:, 0:4], ones[0:HD, :], lam_prod[:].rearrange("p l m -> p (l m)"),
                             start=True, stop=True).then_inc(main_done, 1)
            pe.wait_ge(cond_ready, 1)

            def ada(l, c, out):
                w = arrived(("ada", l, c))[:, 0:KC * 256].rearrange("p (k n) -> p k n", k=KC)
                for k in range(KC):
                    ins = nc.tensor.matmul(out, cond[:, k, :], w[:, k, :], start=k == 0, stop=k == KC - 1)
                return ins.then_inc(w_used, 1)

            def ada_turn(row, out, n):
                for j in range(n):
                    ins = nc.tensor.matmul(out[:, 2 * j:2 * j + 2], row[:, j * P:(j + 1) * P], ident[0:2, 0:2],
                                           start=True, stop=True)
                return ins

            for n in range(2):
                claim_main(("ada0", n))
                o = 1024 * (MAIN[("ada0", n)] % 3)
                for c in range(4):
                    ada(0, 4 * n + c, ps[0:2, o + 256 * c:o + 256 * c + 256])
                pe.drain().then_inc(main_done, 1)
            claim_main(("ada0t",))
            pe.wait_ge(ada_rows, 2)
            pe.wait_ge(const_in, 160)
            ada_turn(ada_row0, main_pair(("ada0t",)), 16).then_inc(main_done, 1)

            for l in range(DEPTH):
                if l == 0:
                    sum_chunks(1, ("norm", 0, "mix"))
                    keep_busy(("lora", 0, 0), KEEP)

                def split_sub(label):
                    q = SUB_AT[label]
                    pe.wait_ge(t_split, q + 1)
                    return sub_of(sub_hi, q), sub_of(sub_lo, q)

                def project_pair(a, b, ready):
                    ws = []
                    for label in (a, b):
                        claim_main(label)
                        ws.append(split_sub(label))
                    for k in range(KC):
                        pe.wait_ge(ready[0], ready[1] + k + 1)
                        for label, w in zip((a, b), ws):
                            ins = split_both(label, [p[:, k:k + 1, :] for p in w], h_hi, h_lo, k, k + 1, KC)
                            if k == KC - 1:
                                ins.then_inc(main_done, 1)

                def split_both(label, w, x_hi, x_lo, k0, k1, kn, ready=None):
                    w_hi_, w_lo_ = w
                    o = 1024 * (MAIN[label] % 3)
                    for k in range(k0, k1):
                        if ready:
                            pe.wait_ge(ready[0], ready[1] + k + 1)
                        for n, (a, b) in enumerate(((w_lo_, x_hi), (w_hi_, x_lo), (w_hi_, x_hi))):
                            for half in range(2):
                                ins = nc.tensor.matmul(ps[:, o + 512 * half:o + 512 * half + TH], a[:, k - k0, :],
                                                       b[:, k, TH * half:TH * half + TH],
                                                       start=k == 0 and n == 0, stop=k == kn - 1 and n == 2)
                    return ins

                def project(label):
                    claim_main(label)
                    split_both(label, split_sub(label), h_hi, h_lo, 0, KC, KC).then_inc(main_done, 1)

                def rot(r):
                    rows = MQK if r in (0, 9, 10, 11, 12) else P
                    sw = swap_m if rows == MQK else swap_d
                    n = 13 * l + r
                    claim_aux(("rot", l, r))
                    pe.wait_ge(raw_ready, n + 1)
                    nc.tensor.matmul(AUXP[0:rows, LAT], sw[:], raw[0:rows, n % 2, LAT], start=True, stop=True).then_inc(aux_done, 1)

                project_pair(("lora", l, 0), ("lora", l, 1), (h_split, 16 * l))
                project(("lora", l, 2))
                project(("rope", l, 0))
                claim_aux(("norm", l, "ckv"))
                sum_square(l, "lora", 0, True, True).then_inc(sq_used, 1)
                pe.drain().then_inc(aux_done, 1)
                project(("rope", l, 1))
                claim_aux(("norm", l, "cq"))
                for g in (1, 2):
                    sum_square(l, "lora", g, g == 1, g == 2).then_inc(sq_used, 1)
                pe.drain().then_inc(aux_done, 1)
                if l == 0:
                    pe.wait_ge(const_in, 160)
                project(("rope", l, 2))
                rot(0)
                for r in range(3, 9):
                    project(("rope", l, r))
                    rot(r - 2)
                def value_tile(v):
                    half, t = v // TT, v % TT
                    if v < 8:
                        claim_main(("vd", l, v))
                        out = main_pair(("vd", l, v))[:, 0:256]
                    else:
                        out = ps[:, 3072 + 512 * (v - 8):3328 + 512 * (v - 8)]
                    for kh in range(2):
                        whi, wlo = split_sub(("vd", l, half, kh))
                        for k in range(4 * kh, 4 * kh + 4):
                            tile = slice(t * P, (t + 1) * P)
                            nc.tensor.matmul(out, h_lo[:, k, tile], whi[:, k % 4, :], start=k == 0, stop=False)
                            nc.tensor.matmul(out, h_hi[:, k, tile], wlo[:, k % 4, :], start=False, stop=False)
                            ins = nc.tensor.matmul(out, h_hi[:, k, tile], whi[:, k % 4, :], start=False, stop=k == KC - 1)
                    return ins

                for v in range(8):
                    value_tile(v).then_inc(main_done, 1)
                    if v == 0:
                        rot(7)
                    if v == 1:
                        rot(8)

                def attention(f, last_values):
                    base = (2 * l + f) * ITEMS

                    def item(i):
                        h, qt = i // TT, i % TT
                        lat = qt < TT - 1
                        return base + i, (base + i) % 2, h, qt, lat

                    def scores(i):
                        it, b, h, qt, lat = item(i)
                        if it >= 2:
                            pe.wait_ge(exp_done, it - 1)
                        if l == 0 and i >= 2 and (i - 2) % TT == TT - 1:
                            pe.wait_ge(late_rows, 4 * f + (i - 2) // TT + 1)
                        o = 1536 * b
                        rows = [(0, HD), (HD, P)] if f == 0 else [(0, MQK)]
                        for m, (r0, r1) in enumerate(rows):
                            q = q_t[r0:r1, h, qt * P:(qt + 1) * P]
                            if lat:
                                parts = ((512, 768), (0, 512)) if m == 0 else ((256, 768), (0, 256))
                                for n, (a, z) in enumerate(parts):
                                    if m == 1 and n == 1:
                                        pe.wait_ge(mid_bank, (4 * l + h) * (TT - 1) + qt + 1)
                                    ins = nc.tensor.matmul(ps[:, o + 768 * m + a:o + 768 * m + z], q, k_t[r0:r1, h, a:z],
                                                           start=True, stop=True)
                                    if f == 0 and m == 0 and n == 0:
                                        ins.then_inc(mid_bank, 1)
                            else:
                                ins = nc.tensor.matmul(ps[:, o + 768 * m:o + 768 * m + P], q, k_t[r0:r1, h, LAT_KEYS:NKEY],
                                                       start=True, stop=True)
                        ins.then_inc(scores_done, 1)

                    def turn(h):
                        u = 4 * f + h
                        for n, p in enumerate(ada_after_head(l, u)):
                            out = ps[:, 3968 + 4 * n:3972 + 4 * n]
                            if ADA_OWNER[p] == "pe":
                                pe.wait_ge(late_rows, u + 1)
                                ada_turn(ada_row, out, 2)
                                continue
                            part = part_v if ADA_OWNER[p] == "dve" else part_g
                            name, val = piece_freed(PIECE_AT[("ada", *p)])
                            pe.wait_ge(sems[name], val)
                            for j in range(2):
                                for g in range(2):
                                    ins = nc.tensor.matmul(out[:, 2 * j + g:2 * j + g + 1], part[:, g, j * P:(j + 1) * P],
                                                           ones[:, 0:1], start=True, stop=True)
                        ins.then_inc(ada_done, 1)

                    def transposes(i):
                        it, b, h, qt, lat = item(i)
                        pe.wait_ge(p_ready, it + 1)
                        if it:
                            pe.wait_ge(pt_a_ready, it)
                        for k in range(4 if lat else 1):
                            ins = nc.tensor.matmul(ps[:, 3072 + k * P:3072 + (k + 1) * P], e_buf[:, b, 0, k * P:(k + 1) * P], diag[:, b, :],
                                                   start=True, stop=True)
                        ins.then_inc(tr_a_done, 1)
                        if it:
                            pe.wait_ge(pv_evac, it)
                        if qt == TT - 1 and l == 0:
                            ada(*ada_after_head(l, 4 * f + h)[0], ps[0:2, 1536 * b:1536 * b + 256])
                            pe.drain().then_inc(late_rows_done, 1)
                        if qt == 0 and h:
                            turn(h - 1)
                        if lat:
                            if qt == 0 and h:
                                pe.wait_ge(mod_late, 8 * l + 4 * f + h)
                            for k in range(4, 6):
                                ins = nc.tensor.matmul(ps[:, 3584 + (k - 4) * P:3584 + (k - 3) * P], e_buf[:, b, 0, k * P:(k + 1) * P],
                                                       diag[:, b, :], start=True, stop=True)
                            ins.then_inc(tr_b_done, 1)

                    def values(i):
                        it, b, h, qt, lat = item(i)
                        pe.wait_ge(pt_a_ready, it + 1)
                        if lat:
                            pe.wait_ge(pt_b_ready, n_tr_b(it))
                        if it:
                            pe.wait_ge(pv_evac, it)
                        kts = range(6) if lat else (KT - 1,)
                        for n, kt in enumerate(kts):
                            ins = nc.tensor.matmul(ps[:, 3840:3968], v_n[:, kt, h * P:(h + 1) * P], pt_buf[:, b, n, :],
                                                   start=n == 0, stop=n == len(kts) - 1)
                        ins.then_inc(pv_done, 1)

                    scores(0)
                    scores(1)
                    last_values()
                    for i in range(ITEMS):
                        if i and i + 1 < ITEMS:
                            scores(i + 1)
                        if i:
                            values(i - 1)
                        transposes(i)
                    values(ITEMS - 1)
                    pe.wait_ge(pv_evac, base + ITEMS)
                    turn(HEADS - 1)
                    pe.wait_ge(mod_late, 8 * l + 4 * f + HEADS)

                pe.wait_ge(rope_done, 13 * l + 9)
                pe.wait_ge(vd_ready, 10 * l + 8)
                pe.wait_ge(cache_k_in, 16 * (l + 1))
                pe.wait_ge(cache_v_in, 16 * (l + 1))
                pe.wait_ge(rot_used, 13 * l + 9)

                def last_value_tiles():
                    claim_aux(("vd tail", l))
                    value_tile(8)
                    value_tile(9).then_inc(aux_done, 1)
                    pe.wait_ge(vd_ready, 10 * l + 10)

                attention(0, last_value_tiles)

                pe.wait_ge(pv_evac, (2 * l + 1) * ITEMS)
                pe.wait_ge(exp_done, (2 * l + 1) * ITEMS)
                for h in range(HEADS):
                    claim_aux(("norm", l, "head", h))
                    sum_square(l, "head", h, True, True).then_inc(sq_used, 1)
                    pe.drain().then_inc(aux_done, 1)
                    out = claim_main(("rope", l, 9 + h))
                    pe.wait_ge(lat_normed, 2 * l + 2)
                    for k in range(2):
                        ins = both(out[0:MQK], wuq[:, k, h * MQK:(h + 1) * MQK], cq_t[:, k, :], k == 0, k == 1)
                    ins.then_inc(main_done, 1)
                    if h:
                        rot(8 + h)
                rot(12)
                pe.wait_ge(cache_c_in, 16 * N_CACHE_C * (l + 1))
                for h in range(HEADS):
                    claim_main(("uk", l, h))
                    o = 1024 * (MAIN[("uk", l, h)] % 3)
                    for c in range(2):
                        ins = nc.tensor.matmul(ps[0:NOPE, o + 512 * c:o + 512 * c + 448], wuk[:, h * NOPE:(h + 1) * NOPE],
                                               ckv_t[:, 448 * c:448 * c + 448], start=True, stop=True)
                    ins.then_inc(main_done, 1)
                for v in range(KT - 2):
                    o = 1024 * (MAIN[("uv", l, v)] % 3)
                    claim_main(("uv", l, v))
                    nc.tensor.matmul(ps[:, o:o + 512], ckv_t[:, v * P:(v + 1) * P], wuv, start=True, stop=True).then_inc(main_done, 1)
                pe.wait_ge(rope_done, 13 * l + 13)
                pe.wait_ge(vm_ready, KT * (l + 1) - 2)
                pe.wait_ge(km_ready, 4 * (l + 1))
                pe.wait_ge(kr_spread, 4 * (l + 1))

                def last_value_rows():
                    claim_aux(("uv tail", l))
                    for n in range(2):
                        v = KT - 2 + n
                        ins = nc.tensor.matmul(ps[:, 3072 + 512 * n:3584 + 512 * n], ckv_t[:, v * P:(v + 1) * P], wuv,
                                               start=True, stop=True)
                    ins.then_inc(aux_done, 1)
                    pe.wait_ge(vm_ready, KT * (l + 1))

                attention(1, last_value_rows)

                pe.wait_ge(pv_evac, (2 * l + 2) * ITEMS)
                pe.wait_ge(exp_done, (2 * l + 2) * ITEMS)
                keep_busy(("o", l, 0), 4)
                for d_ in range(KC):
                    claim_main(("o", l, d_))
                    split_both(("o", l, d_), split_sub(("o", l, d_)), h_hi, h_lo, 0, KC, KC,
                               (mixed_split, 8 * l) if d_ == 0 else None).then_inc(main_done, 1)
                sum_chunks(2 * l + 2, ("norm", l, "ffn"))
                keep_busy(("gate", 0) if l == 0 else ("htok", 0), KEEP if l == 0 else KEEP + 4)

                if l == 0:
                    for half, js in enumerate(FF_HALF):
                        for j in js:
                            if j == 0:
                                project_pair(("gate", 0), ("up", 0), (h_split, 8))
                                continue
                            project(("gate", j))
                            project(("up", j))
                        kn = len(js)
                        for d_ in range(KC):
                            claim_main(("down", half, d_))
                            for part in range(2):
                                w = split_sub(("down", half, d_, part))
                                ins = split_both(("down", half, d_), w, hid_hi, hid_lo, part * kn // 2, (part + 1) * kn // 2,
                                                 kn, (hid_ready, js[0]) if d_ == 0 else None)
                                ins.then_inc(main_done if part else down_first, 1)
                    sum_chunks(3, ("norm", 1, "mix"))
                    keep_busy(("lora", 1, 0), KEEP)

            claim_aux(("router",))
            for k in range(KC):
                pe.wait_ge(h_ready, 24 + k + 1)
            for t in range(TT):
                for k in range(KC):
                    ins = nc.tensor.matmul(AUXP[:, t * NE:(t + 1) * NE], h_t[:, k, t * P:(t + 1) * P], router_w[:, k, :],
                                           start=k == 0, stop=k == KC - 1)
            ins.then_inc(aux_done, 1)

            def htok_rows(t):
                claim_main(("htok", t))
                o = 1024 * (MAIN[("htok", t)] % 3)
                for k in range(KC):
                    ins = nc.tensor.transpose(ps[:, o + k * P:o + (k + 1) * P], h_t[:, k, t * P:(t + 1) * P], ident[:])
                ins.then_inc(main_done, 1)

            for t in range(3):
                htok_rows(t)
            claim_aux(("rank",))
            pe.wait_ge(sel_ready, 1)
            sel = rt[:, 4].rearrange("p t e -> p (t e)")
            nc.tensor.matmul(AUXP[:, 0:TT * NE], before[:], sel, start=True, stop=True)
            nc.tensor.matmul(AUXP[:, TT * NE:2 * TT * NE], ones[:], sel, start=True, stop=True).then_inc(aux_done, 1)
            for t in range(3, TT):
                htok_rows(t)

            pe.wait_ge(htok_ready, TT)
            pe.wait_ge(rank_ready, 1)

            def x_transposes(half):
                bank = 4 + TR_OF[("xa", "xb")[half]] % 2
                for k in range(4):
                    ins = nc.tensor.transpose(ps[:, 512 * bank + k * P:512 * bank + (k + 1) * P],
                                              xs[:, (4 * half + k) * P:(4 * half + k + 1) * P], ident[:])
                return ins

            pe.drain().then_inc(pc_done, SPLITS)
            for _ in range(26):
                nc.tensor.matmul(ps[:, 0:N_LAT], ones[:], cos_d[:], start=True, stop=True)
            pe.wait_ge(xs_in, 16)
            for half in range(2):
                x_transposes(half).then_inc(etr_done, 1)
            pe.drain().then_inc(etr_done, G_ETR)

            def split_product(out, a_hi, a_lo, b_hi, b_lo, start, stop):
                nc.tensor.matmul(out, a_lo, b_hi, start=start, stop=False)
                nc.tensor.matmul(out, a_hi, b_lo, start=False, stop=False)
                return nc.tensor.matmul(out, a_hi, b_hi, start=False, stop=stop)

            with pe.Fori(0, SLOTS) as s:
                def tr(c):
                    j = TR_OF[c]
                    bank = 4 + j % 2
                    pe.wait_ge(etr_evac, 6 * s + j + 1)
                    if c == "xa":
                        pe.wait_ge(xs_in, 16 * (s + 2))
                    if c in ("xa", "xb"):
                        x_transposes(j - TR_OF["xa"]).then_inc(etr_done, 1)
                        return
                    pe.wait_ge(eact_ready, G_EACT + 4 * s + c + 1)
                    for n, k in enumerate(range(*BLK[c])):
                        ins = nc.tensor.transpose(ps[:, 512 * bank + n * P:512 * bank + (n + 1) * P],
                                                  eact[:, k * P:(k + 1) * P], ident[:])
                    ins.then_inc(etr_done, 1)

                def split_piece(n):
                    pe.wait_ge(w_split, MRING + NPC * s + n + 1)
                    k = KC if n < NGU else FCE
                    return (w_hi[:, n % SPLITS, :].rearrange("p (k n) -> p k n", k=k),
                            w_lo[:, n % SPLITS, :].rearrange("p (k n) -> p k n", k=k))

                def gate_up(n):
                    if n % 2 == 0:
                        pe.wait_ge(eact_ready, 4 * s + n // 2 + 1)
                    if n == 0:
                        pe.wait_ge(etr_evac, 6 * s + 2)
                    hi, lo = split_piece(n)
                    for k in range(KC):
                        ins = split_product(ps[:, 512 * (n % 4):512 * (n % 4) + HCH], xs_hi[:, k, :], xs_lo[:, k, :],
                                            hi[:, k, :], lo[:, k, :], k == 0, k == KC - 1)
                    ins.then_inc(pc_done, 1)

                def down(n, blocks, hi, lo):
                    c = 3072 + DCH * (n - NGU)
                    for k in range(*blocks):
                        ins = split_product(ps[:, c:c + DCH], ea_hi[:, k, :], ea_lo[:, k, :], hi[:, k, :], lo[:, k, :],
                                            k == 0, k == FCE - 1)
                    return ins

                for n in range(3):
                    gate_up(n)
                tr(0)
                gate_up(3)
                gate_up(4)
                tr(1)
                gate_up(5)
                gate_up(6)
                tr(2)
                gate_up(7)
                pe.wait_ge(y_evac, s + 1)
                hi, lo = split_piece(8)
                pe.wait_ge(etr_evac, 2 + 6 * s + TR_OF[1] + 1)
                down(8, (0, 5), hi, lo)
                tr(3)
                pe.wait_ge(etr_evac, 2 + 6 * s + TR_OF[2] + 1)
                down(8, (5, 8), hi, lo)
                pe.wait_ge(etr_evac, 2 + 6 * s + TR_OF[3] + 1)
                down(8, (8, 11), hi, lo).then_inc(pc_done, 1)
                tr("xa")
                for n in range(9, NPC):
                    hi, lo = split_piece(n)
                    down(n, (0, FCE), hi, lo).then_inc(pc_done, 1)
                    if n == 9:
                        tr("xb")

            pe.wait_ge(y_evac, SLOTS + 1)
            for t in range(TT):
                claim_main(("comb", t))
                o = 1024 * (MAIN[("comb", t)] % 3)
                pe.wait_ge(comb_ready, t + 1)
                for k in range(KC):
                    ins = nc.tensor.transpose(ps[:, o + k * P:o + (k + 1) * P], picked[:, t, 0, k * P:(k + 1) * P], ident[:])
                ins.then_inc(main_done, 1)
            sum_chunks(5, ("norm", DEPTH, "fin"))


def constants():
    t = np.arange(N_LAT)
    rows, cols = (t // GRID_W).astype(np.float32), (t % GRID_W).astype(np.float32)

    def axial(width):
        half = width // 4
        freqs = np.float32(THETA) ** (-np.arange(half, dtype=np.float32) / np.float32(half))
        cos, sin, partner = [], [], []
        for block, pos in enumerate((rows, cols)):
            for side in range(2):
                for j in range(half):
                    ang = pos * freqs[j]
                    cos.append(np.cos(ang))
                    sin.append(np.sin(ang) * (-1.0, 1.0)[side])
                    partner.append(block * 2 * half + (1 - side) * half + j)
        return np.array(cos, np.float32), np.array(sin, np.float32), partner

    def swap(partner):
        m = np.zeros((len(partner),) * 2, np.float32)
        m[partner, np.arange(len(partner))] = 1.0
        return m

    c, s, p = axial(HD)
    out = {"cos_d": np.concatenate([c, c]), "sin_d": np.concatenate([s, s]),
           "swap_d": swap(p + [HD + i for i in p])}
    c, s, p = axial(ROPE)
    out["cos_m"] = np.concatenate([np.ones((NOPE, N_LAT), np.float32), c])
    out["sin_m"] = np.concatenate([np.zeros((NOPE, N_LAT), np.float32), s])
    out["swap_m"] = swap(list(range(NOPE)) + [NOPE + i for i in p])
    out["ident"] = np.eye(P, dtype=np.float32)
    out["before"] = np.triu(np.ones((P, P), np.float32), 1)
    small = np.concatenate([np.tril(np.ones((NE, NE)), -1).ravel(), np.arange(TT) * P, np.arange(SLOTS) * P])
    out["small"] = np.broadcast_to(small.astype(np.float32), (P, small.size)).copy()
    return out


_WEIGHTS = ["w_ada", "w_in", "w_uq", "w_uk", "w_uv", "w_o", "w_gate", "w_up", "w_down", "router",
            "moe_w_gate", "moe_w_up", "moe_w_down"]
_OUTS = {"y_t": (P, KC, T), "new_k": (DEPTH, P, HEADS, N_PROMPT), "new_v": (DEPTH, N_PROMPT, HEADS * P),
         "new_ckv": (DEPTH, P, N_PROMPT), "new_kr": (DEPTH, ROPE, N_PROMPT)}


def layout(x):
    def col(a):
        return np.ascontiguousarray(a.reshape(-1, P).T)

    a = {n: x[n] for n in _WEIGHTS}
    tokens = np.concatenate([x["x_sample"][0], x["x_prompt"][0]], axis=0)
    a["x_t"] = tokens.T.reshape(KC, P, T).transpose(1, 0, 2)
    a["cond"] = np.stack([col(x["c"][0]), col(x["c_ctx"])], axis=2)
    a["vecs"] = np.concatenate([col(x[n].reshape(-1)) for n in
                                ("b_ada", "norm_mix_g", "norm_ffn_g", "final_norm_g", "mla_q_norm_g",
                                 "mla_kv_norm_g", "diff_subln_g")], axis=1)
    lam = np.stack([np.stack([x["diff_lq1"], x["diff_lk1"]], -1), np.stack([x["diff_lq2"], x["diff_lk2"]], -1)], 2)
    a["lam"] = lam.transpose(1, 0, 2, 3)
    a["cache_k"] = x["cache_diff_k"][0].transpose(0, 3, 2, 1)
    v = x["cache_diff_v"][0].reshape(DEPTH, PAST // P, P, HEADS * P)
    a["cache_v"] = v.transpose(0, 2, 1, 3)
    a["cache_ckv"] = x["cache_mla_ckv"][0].transpose(0, 2, 1)
    a["cache_kr"] = x["cache_mla_krope"][0].transpose(0, 2, 1)
    return a


def kernel(**inputs):
    import concourse.bacc as _bacc
    from concourse.bass_utils import run_bass_kernel_spmd as _run

    nc = _bacc.Bacc("TRN2", target_bir_lowering=False, num_devices=1)
    arrays = {}
    aps = {}
    laid = layout({n: np.asarray(v) for n, v in inputs.items()})
    for name, a in {**laid, **constants()}.items():
        a = np.ascontiguousarray(a)
        arrays[f"in_{name}"] = a
        aps[name] = nc.dram_tensor(f"in_{name}", a.shape, mybir.dt.from_np(a.dtype), kind="ExternalInput").ap()
    for name, shape in _OUTS.items():
        aps[name] = nc.dram_tensor(f"out_{name}", shape, mybir.dt.float32, kind="ExternalOutput").ap()
    build(nc, aps)
    r = _run(nc, [arrays], core_ids=[0]).results[0]
    y = np.asarray(r["out_y_t"]).transpose(2, 1, 0).reshape(T, D_MODEL)
    new_k = np.asarray(r["out_new_k"]).transpose(0, 3, 2, 1)[None]
    new_v = np.asarray(r["out_new_v"]).reshape(1, DEPTH, N_PROMPT, HEADS, P)
    new_ckv = np.asarray(r["out_new_ckv"]).transpose(0, 2, 1)[None]
    new_kr = np.asarray(r["out_new_kr"]).transpose(0, 2, 1)[None]
    return (np.ascontiguousarray(y[N_LAT:])[None], np.ascontiguousarray(y[:N_LAT])[None],
            np.ascontiguousarray(new_k), np.ascontiguousarray(new_v), np.ascontiguousarray(new_ckv),
            np.ascontiguousarray(new_kr))
```
